# Optimizing a Trainium2 kernel written in Bass

```python
import math
import jax, jax.numpy as jnp
from jax import lax
import numpy as np

D_MODEL = 1024
BATCH = 1
SEQ = 1024
DEPTH = 2
DEC_BATCH = 8
DEC_SEQ = 4
PAST_LEN = 2048
PAGE_SIZE = 128

N_PAIRS = DEPTH // 2
N_META = 16
H_A = 4
DK_A = 128
DV_A = 128
H_B = 4
DK_B = 128
DV_B = 128
H_C = 4
DC = 64
H_D = 4
DH_D = 128
H_I = 4
D_IDX = 64
TOPK_MAX = 256
D_FF = 2816
CONV_W = 3
ROPE_THETA = 500000.0
ROT_FRAC = 4
CHUNK = 64
QBLK = 128
EPS = 1e-6
REC_COLS = (H_A * DK_A, H_A * DK_A, H_A * DV_A, H_A * DV_A, H_B * DK_B, H_B * DK_B, H_B * DV_B, H_B * DV_B, 2 * H_B)
ATT_COLS = (H_C * 2 * DC, H_C * 2 * DC, H_C * 2 * DC, H_D * DH_D, DH_D, DH_D, H_I * D_IDX, D_IDX, H_I)
REC_OUT = H_A * DV_A + H_B * DV_B
ATT_OUT = H_C * 2 * DC + H_D * DH_D

kernel_name = 'hybrid_hgrn2_mlstm_diffattn_dsa_step'

def split_cols(a, sizes):
    return jnp.split(a, np.cumsum(sizes)[:-1].tolist(), axis=-1)

def rms_norm(x, g):
    xf = x.astype(jnp.float32)
    y = xf * lax.rsqrt(jnp.mean(xf * xf, axis=-1, keepdims=True) + EPS)
    return (y * g.astype(jnp.float32)).astype(x.dtype)

def partial_rotary(x, pos):
    d = x.shape[-1]
    r = d // ROT_FRAC
    half = r // 2
    inv = ROPE_THETA ** (-jnp.arange(half, dtype=jnp.float32) * 2.0 / r)
    ang = pos.astype(jnp.float32)[:, None] * inv[None, :]
    shape = (1, pos.shape[0]) + (1,) * (x.ndim - 3) + (half,)
    cos, sin = jnp.cos(ang).reshape(shape), jnp.sin(ang).reshape(shape)
    xf = x.astype(jnp.float32)
    x1, x2 = xf[..., :half], xf[..., half:r]
    out = jnp.concatenate([x1 * cos - x2 * sin, x1 * sin + x2 * cos, xf[..., r:]], axis=-1)
    return out.astype(x.dtype)

def conv_ffn(h, buf, w_up, cw, cb, w_down):
    T = h.shape[1]
    ug, uv = jnp.split(h @ w_up, 2, axis=-1)
    full = jnp.concatenate([buf.astype(ug.dtype), ug], axis=1)
    conv = cb
    for j in range(CONV_W):
        conv = conv + cw[j] * full[:, j:j + T]
    y = (jax.nn.silu(conv) * uv) @ w_down
    return y, full[:, full.shape[1] - (CONV_W - 1):]

def hgrn2_segment(q, k, v, logf, S, chunk):
    B_, T, H, _ = q.shape
    dv = v.shape[-1]
    nc = T // chunk
    causal = jnp.tril(jnp.ones((chunk, chunk), dtype=bool))

    def blocks(a):
        return a.reshape(B_, nc, chunk, H, a.shape[-1]).transpose(1, 0, 3, 2, 4)

    def step(S, inp):
        qc, kc, vc, gc = inp
        bc = jnp.cumsum(gc, axis=2)
        o = jnp.einsum('bhtd,bhde->bhte', qc * jnp.exp(bc), S)
        rel = jnp.where(causal[:, :, None], bc[:, :, :, None, :] - bc[:, :, None, :, :], -jnp.inf)
        a = jnp.einsum('bhtd,bhsd,bhtsd->bhts', qc, kc, jnp.exp(rel))
        o = o + jnp.einsum('bhts,bhse->bhte', a, vc)
        last = bc[:, :, -1:, :]
        S = jnp.exp(last[:, :, 0, :, None]) * S + jnp.einsum('bhsd,bhse->bhde', kc * jnp.exp(last - bc), vc)
        return S, o

    S, o = lax.scan(step, S, (blocks(q), blocks(k), blocks(v), blocks(logf)))
    return S, o.transpose(1, 0, 3, 2, 4).reshape(B_, T, H, dv)

def mlstm_segment(q, k, v, ig, lf, C, n, m, chunk):
    B_, T, H, _ = q.shape
    dv = v.shape[-1]
    nc = T // chunk
    causal = jnp.tril(jnp.ones((chunk, chunk), dtype=bool))

    def blocks(a):
        return a.reshape(B_, nc, chunk, H, a.shape[-1]).transpose(1, 0, 3, 2, 4)

    def gblocks(a):
        return a.reshape(B_, nc, chunk, H).transpose(1, 0, 3, 2)

    def step(carry, inp):
        C, n, m = carry
        qc, kc, vc, ic, fc = inp
        b = jnp.cumsum(fc, axis=-1)
        dmat = jnp.where(causal, b[..., :, None] - b[..., None, :] + ic[..., None, :], -jnp.inf)
        inter = b + m[..., None]
        mt = jnp.maximum(inter, dmat.max(axis=-1))
        w = jnp.exp(dmat - mt[..., None]) * jnp.einsum('bhtd,bhsd->bhts', qc, kc)
        wi = jnp.exp(inter - mt)
        num = wi[..., None] * jnp.einsum('bhtd,bhde->bhte', qc, C) + jnp.einsum('bhts,bhse->bhte', w, vc)
        den = wi * jnp.einsum('bhtd,bhd->bht', qc, n) + w.sum(axis=-1)
        hc = num / jnp.maximum(jnp.abs(den), jnp.exp(-mt))[..., None]
        m_new = mt[..., -1]
        decay = jnp.exp(b[..., -1] + m - m_new)
        kw = kc * jnp.exp(b[..., -1:] - b + ic - m_new[..., None])[..., None]
        C = decay[..., None, None] * C + jnp.einsum('bhsd,bhse->bhde', kw, vc)
        n = decay[..., None] * n + kw.sum(axis=2)
        return (C, n, m_new), hc

    (C, n, m), h = lax.scan(step, (C, n, m), (blocks(q), blocks(k), blocks(v), gblocks(ig), gblocks(lf)))
    return C, n, m, h.transpose(1, 0, 3, 2, 4).reshape(B_, T, H, dv)

def rec_mixer(h, segments, S_a, C_b, n_b, m_b, w_in, b_gates, lb, g_a, g_b):
    f32 = jnp.float32
    B_, T, _ = h.shape
    qa, fa, ia, ga, qb, kb, vb, ob, gt = split_cols(h @ w_in, REC_COLS)

    def heads(a, H):
        return a.reshape(B_, T, H, -1).astype(f32)

    lbh = lb.reshape(H_A, DK_A)
    f = lbh + (1.0 - lbh) * jax.nn.sigmoid(heads(fa, H_A))
    logf_a, k_a = jnp.log(f), 1.0 - f
    q_a = heads(qa, H_A) * DK_A ** -0.5
    v_a = heads(ia, H_A)
    q_b = heads(qb, H_B)
    k_b = heads(kb, H_B) * DK_B ** -0.5
    v_b = heads(vb, H_B)
    gt = gt.astype(f32).reshape(B_, T, 2, H_B) + b_gates.astype(f32)
    ig, lf = gt[:, :, 0], jax.nn.log_sigmoid(gt[:, :, 1])
    S, C, n, m = S_a.astype(f32), C_b.astype(f32), n_b.astype(f32), m_b.astype(f32)
    outs_a, outs_b = [], []
    t0 = 0
    for length, chunk in segments:
        sl = slice(t0, t0 + length)
        S, oa = hgrn2_segment(q_a[:, sl], k_a[:, sl], v_a[:, sl], logf_a[:, sl], S, chunk)
        C, n, m, obb = mlstm_segment(q_b[:, sl], k_b[:, sl], v_b[:, sl], ig[:, sl], lf[:, sl], C, n, m, chunk)
        outs_a.append(oa)
        outs_b.append(obb)
        t0 += length
    y_a = rms_norm(jnp.concatenate(outs_a, axis=1), g_a) * jax.nn.silu(heads(ga, H_A))
    y_b = rms_norm(jnp.concatenate(outs_b, axis=1), g_b) * jax.nn.sigmoid(heads(ob, H_B))
    y = jnp.concatenate([y_a.reshape(B_, T, -1), y_b.reshape(B_, T, -1)], axis=-1).astype(h.dtype)
    return y, S, C, n, m

def att_project(h, pos, w_in):
    B_, T, _ = h.shape
    qc, kc, vc, qd, kd, vd, qi, ki, wi = split_cols(h @ w_in, ATT_COLS)
    qc = partial_rotary(qc.reshape(B_, T, H_C, 2, DC), pos)
    kc = partial_rotary(kc.reshape(B_, T, H_C, 2, DC), pos).reshape(B_, T, H_C, 2 * DC)
    vc = vc.reshape(B_, T, H_C, 2 * DC)
    qd = partial_rotary(qd.reshape(B_, T, H_D, DH_D), pos)
    kd = partial_rotary(kd, pos)
    qi = partial_rotary(qi.reshape(B_, T, H_I, D_IDX), pos)
    ki = partial_rotary(ki, pos)
    return qc, qd, qi, wi, kc, vc, kd, vd, ki

def att_queries(qc, qd, qi, wi, qpos, kc, vc, kd, vd, ki, kpos, lam, lam_init, g_c, n_sel):
    f32 = jnp.float32
    B_, Tq = qc.shape[:2]
    mask = kpos[None, :] <= qpos[:, None]
    kc2 = kc.reshape(kc.shape[:3] + (2, DC))
    s = jnp.einsum('bqhcd,bshcd->bhcqs', qc, kc2).astype(f32) * DC ** -0.5
    p = jax.nn.softmax(jnp.where(mask, s, -jnp.inf), axis=-1)
    a = p[:, :, 0] - lam * p[:, :, 1]
    oc = jnp.einsum('bhqs,bshe->bqhe', a.astype(vc.dtype), vc)
    oc = (rms_norm(oc, g_c) * (1.0 - lam_init)).reshape(B_, Tq, H_C * 2 * DC)
    sc = jnp.einsum('bqhd,bsd->bqhs', qi, ki).astype(f32) * D_IDX ** -0.5
    score = jnp.einsum('bqh,bqhs->bqs', wi.astype(f32) * H_I ** -0.5, jax.nn.relu(sc))
    _, idx = lax.top_k(jnp.where(mask, score, -jnp.inf), n_sel)
    valid = kpos[idx] <= qpos[None, :, None]
    take = jax.vmap(lambda rows, ix: rows[ix])
    ks, vs = take(kd, idx), take(vd, idx)
    sd = jnp.einsum('bqhd,bqnd->bqhn', qd, ks).astype(f32) * DH_D ** -0.5
    pd = jax.nn.softmax(jnp.where(valid[:, :, None, :], sd, -jnp.inf), axis=-1)
    od = jnp.einsum('bqhn,bqnd->bqhd', pd.astype(vs.dtype), vs).reshape(B_, Tq, H_D * DH_D)
    return jnp.concatenate([oc, od.astype(oc.dtype)], axis=-1)

def diff_lambda_value(lam_p, lam_init):
    lq1, lk1, lq2, lk2 = lam_p.astype(jnp.float32)
    return jnp.exp(jnp.sum(lq1 * lk1)) - jnp.exp(jnp.sum(lq2 * lk2)) + lam_init

def prompt_attention(h, w_in, lam, lam_init, g_c, n_sel):
    B_, T, _ = h.shape
    pos = jnp.arange(T, dtype=jnp.int32)
    qc, qd, qi, wi, kc, vc, kd, vd, ki = att_project(h, pos, w_in)
    Tp = -(-T // QBLK) * QBLK
    nb = Tp // QBLK

    def qblocks(a):
        a = jnp.pad(a, [(0, 0), (0, Tp - T)] + [(0, 0)] * (a.ndim - 2))
        return a.reshape((B_, nb, QBLK) + a.shape[2:]).swapaxes(0, 1)

    qpos = jnp.arange(Tp, dtype=jnp.int32).reshape(nb, QBLK)

    def one(blk):
        qc_b, qd_b, qi_b, wi_b, qp = blk
        return att_queries(qc_b, qd_b, qi_b, wi_b, qp, kc, vc, kd, vd, ki, pos, lam, lam_init, g_c, n_sel)

    out = lax.map(one, (qblocks(qc), qblocks(qd), qblocks(qi), qblocks(wi), qpos))
    out = out.swapaxes(0, 1).reshape(B_, Tp, ATT_OUT)[:, :T]
    return out, (kc, vc, kd, vd, ki)

def gather_pages(cache, page_table):
    g = cache[page_table]
    return g.reshape((page_table.shape[0], -1) + cache.shape[2:])

def sample_attention(h, pos, page_table, ck, cv, dk, dv, ik, w_in, lam, lam_init, g_c, n_sel):
    qc, qd, qi, wi, kc, vc, kd, vd, ki = att_project(h, pos, w_in)

    def with_past(cache, new):
        return jnp.concatenate([gather_pages(cache, page_table).astype(new.dtype), new], axis=1)

    kpos = jnp.arange(PAST_LEN + h.shape[1], dtype=jnp.int32)
    out = att_queries(qc, qd, qi, wi, pos, with_past(ck, kc), with_past(cv, vc), with_past(dk, kd),
                      with_past(dv, vd), with_past(ik, ki), kpos, lam, lam_init, g_c, n_sel)
    return out, (kc, vc, kd, vd, ki)

def setup_inputs(seed: int = 0) -> dict:
    key = jax.random.key(seed)
    it = iter(list(jax.random.split(key, 40)))

    def nrm(shape, scale):
        return jax.random.normal(next(it), shape, jnp.float32) * scale

    n_pages = PAST_LEN // PAGE_SIZE
    n_used = DEC_BATCH * n_pages
    n_pool = n_used + max(1, n_used // 4)
    page_table = jax.random.permutation(next(it), n_pool)[:n_used].reshape(DEC_BATCH, n_pages).astype(jnp.int32)
    b_gates = jnp.stack([nrm((N_PAIRS, H_B), 0.1),
                         jnp.linspace(3.0, 6.0, H_B, dtype=jnp.float32)[None] + nrm((N_PAIRS, H_B), 0.01)], axis=1)
    return {
        'x_prompt': nrm((BATCH, SEQ, D_MODEL), 1.0),
        'x_sample': nrm((DEC_BATCH, DEC_SEQ, D_MODEL), 1.0),
        'state_hgrn': nrm((N_PAIRS, DEC_BATCH, H_A, DK_A, DV_A), 0.5),
        'state_mlstm_C': nrm((N_PAIRS, DEC_BATCH, H_B, DK_B, DV_B), 0.5),
        'state_mlstm_n': nrm((N_PAIRS, DEC_BATCH, H_B, DK_B), 0.5),
        'state_mlstm_m': nrm((N_PAIRS, DEC_BATCH, H_B), 1.0),
        'state_ffn_conv': nrm((DEPTH, DEC_BATCH, CONV_W - 1, D_FF), 1.0),
        'cache_diff_k': nrm((N_PAIRS, n_pool, PAGE_SIZE, H_C, 2 * DC), 1.0),
        'cache_diff_v': nrm((N_PAIRS, n_pool, PAGE_SIZE, H_C, 2 * DC), 1.0),
        'cache_dsa_k': nrm((N_PAIRS, n_pool, PAGE_SIZE, DH_D), 1.0),
        'cache_dsa_v': nrm((N_PAIRS, n_pool, PAGE_SIZE, DH_D), 1.0),
        'cache_idx_k': nrm((N_PAIRS, n_pool, PAGE_SIZE, D_IDX), 1.0),
        'page_table': page_table,
        'meta_tokens': nrm((N_META, D_MODEL), 1.0),
        'norm_gains': 1.0 + nrm((DEPTH, 4, D_MODEL), 0.01),
        'w_in_rec': nrm((N_PAIRS, D_MODEL, sum(REC_COLS)), D_MODEL ** -0.5),
        'b_gates_rec': b_gates,
        'lb_logits': nrm((N_PAIRS + 1, H_A * DK_A), 0.5),
        'g_norm_hgrn': 1.0 + nrm((N_PAIRS, DV_A), 0.01),
        'g_norm_mlstm': 1.0 + nrm((N_PAIRS, DV_B), 0.01),
        'w_out_rec': nrm((N_PAIRS, REC_OUT, D_MODEL), REC_OUT ** -0.5),
        'w_in_att': nrm((N_PAIRS, D_MODEL, sum(ATT_COLS)), D_MODEL ** -0.5),
        'diff_lambda': nrm((N_PAIRS, 4, DC), 0.1),
        'g_norm_diff': 1.0 + nrm((N_PAIRS, 2 * DC), 0.01),
        'w_out_att': nrm((N_PAIRS, ATT_OUT, D_MODEL), ATT_OUT ** -0.5),
        'w_ffn_up': nrm((DEPTH, D_MODEL, 2 * D_FF), D_MODEL ** -0.5),
        'ffn_conv_w': nrm((DEPTH, CONV_W, D_FF), CONV_W ** -0.5),
        'ffn_conv_b': nrm((DEPTH, D_FF), 0.01),
        'w_ffn_down': nrm((DEPTH, D_FF, D_MODEL), D_FF ** -0.5),
    }

def reference(x_prompt, x_sample, state_hgrn, state_mlstm_C, state_mlstm_n, state_mlstm_m, state_ffn_conv,
              cache_diff_k, cache_diff_v, cache_dsa_k, cache_dsa_v, cache_idx_k, page_table, meta_tokens,
              norm_gains, w_in_rec, b_gates_rec, lb_logits, g_norm_hgrn, g_norm_mlstm, w_out_rec, w_in_att,
              diff_lambda, g_norm_diff, w_out_att, w_ffn_up, ffn_conv_w, ffn_conv_b, w_ffn_down):
    f32 = jnp.float32
    B_p, T_in = x_prompt.shape[:2]
    T_s = x_sample.shape[1]
    meta = jnp.broadcast_to(meta_tokens.astype(x_prompt.dtype)[None], (B_p, N_META, D_MODEL))
    xp = jnp.concatenate([meta, x_prompt], axis=1)
    xs = x_sample
    seg_p = [(N_META, N_META), (T_in, min(CHUNK, T_in))]
    seg_s = [(T_s, T_s)]
    pos_s = PAST_LEN + jnp.arange(T_s, dtype=jnp.int32)
    sel_p = min(TOPK_MAX, T_in // 4)
    sel_s = min(TOPK_MAX, (PAST_LEN + T_s) // 4)
    lb_all = jnp.cumsum(jax.nn.softmax(lb_logits.astype(f32), axis=0), axis=0)
    rec_p = [[], [], [], []]
    rec_s = [[], [], [], []]
    conv_p, conv_s = [], []
    att_p = [[], [], [], [], []]
    att_s = [[], [], [], [], []]
    for l in range(DEPTH):
        p = l // 2
        g = norm_gains[l]
        hp, hs = rms_norm(xp, g[0]), rms_norm(xs, g[0])
        if l % 2 == 0:
            prm = (w_in_rec[p], b_gates_rec[p], lb_all[p], g_norm_hgrn[p], g_norm_mlstm[p])
            zp = (jnp.zeros((B_p, H_A, DK_A, DV_A), f32), jnp.zeros((B_p, H_B, DK_B, DV_B), f32),
                  jnp.zeros((B_p, H_B, DK_B), f32), jnp.zeros((B_p, H_B), f32))
            mp, *st_p = rec_mixer(hp, seg_p, *zp, *prm)
            ms, *st_s = rec_mixer(hs, seg_s, state_hgrn[p], state_mlstm_C[p], state_mlstm_n[p], state_mlstm_m[p], *prm)
            for j in range(4):
                rec_p[j].append(st_p[j])
                rec_s[j].append(st_s[j])
            mp, ms = mp @ w_out_rec[p], ms @ w_out_rec[p]
        else:
            lam_init = 0.8 - 0.6 * math.exp(-0.3 * l)
            lam = diff_lambda_value(diff_lambda[p], lam_init)
            mp, rows_p = prompt_attention(hp, w_in_att[p], lam, lam_init, g_norm_diff[p], sel_p)
            ms, rows_s = sample_attention(hs, pos_s, page_table, cache_diff_k[p], cache_diff_v[p], cache_dsa_k[p],
                                          cache_dsa_v[p], cache_idx_k[p], w_in_att[p], lam, lam_init, g_norm_diff[p], sel_s)
            for j in range(5):
                att_p[j].append(rows_p[j])
                att_s[j].append(rows_s[j])
            mp, ms = mp @ w_out_att[p], ms @ w_out_att[p]
        xp = xp + rms_norm(mp, g[1])
        xs = xs + rms_norm(ms, g[1])
        fp, bp = conv_ffn(rms_norm(xp, g[2]), jnp.zeros((B_p, CONV_W - 1, D_FF), xp.dtype),
                          w_ffn_up[l], ffn_conv_w[l], ffn_conv_b[l], w_ffn_down[l])
        fs, bs = conv_ffn(rms_norm(xs, g[2]), state_ffn_conv[l], w_ffn_up[l], ffn_conv_w[l], ffn_conv_b[l], w_ffn_down[l])
        conv_p.append(bp)
        conv_s.append(bs)
        xp = xp + rms_norm(fp, g[3])
        xs = xs + rms_norm(fs, g[3])
    return (xp[:, N_META:], xs,
            jnp.stack(rec_p[0]), jnp.stack(rec_s[0]),
            jnp.stack(rec_p[1]), jnp.stack(rec_s[1]),
            jnp.stack(rec_p[2]), jnp.stack(rec_s[2]),
            jnp.stack(rec_p[3]), jnp.stack(rec_s[3]),
            jnp.stack(conv_p), jnp.stack(conv_s),
            jnp.stack(att_p[0]), jnp.stack(att_s[0]),
            jnp.stack(att_p[1]), jnp.stack(att_s[1]),
            jnp.stack(att_p[2]), jnp.stack(att_s[2]),
            jnp.stack(att_p[3]), jnp.stack(att_s[3]),
            jnp.stack(att_p[4]), jnp.stack(att_s[4]))


_drawn_inputs = setup_inputs


def setup_inputs(seed=0):
    import zlib

    import numpy as np

    out = dict(_drawn_inputs(seed))
    spreads = {}
    factors = {'g_norm_hgrn': 39.469,
     'g_norm_mlstm': 42.204,
     'g_norm_diff': 64.0,
     'ffn_conv_b': 5.13,
     'cache_dsa_k': 6.645,
     'cache_dsa_v': 5.23,
     'cache_idx_k': 5.566}
    for name, (base, spread) in spreads.items():
        noise = np.random.default_rng([zlib.crc32(name.encode()), seed]).standard_normal(out[name].shape)
        drawn = base * np.exp(spread * noise) if base else spread * noise
        out[name] = __import__('jax').numpy.asarray(drawn.astype(out[name].dtype))
    for name, factor in factors.items():
        out[name] = (out[name] * factor).astype(out[name].dtype)
    return out
```

```python
import math
from contextlib import ExitStack

import numpy as np

import concourse.bass as bass
from concourse import mybir

P = 128
F32 = mybir.dt.float32
U32 = mybir.dt.uint32
I32 = mybir.dt.int32
ACT = mybir.ActivationFunctionType
ALU = mybir.AluOpType
AX = mybir.AxisListType

D = 1024
KD = D // P
SEQ, N_META = 1024, 16
TP = SEQ + N_META
DB, DT = 8, 4
TS = DB * DT
T = TP + TS
NT = (T + P - 1) // P
LAST = T - (NT - 1) * P
PTAIL = TP - (NT - 1) * P
CH = [(0, 384), (384, 384), (768, T - 768)]
H = 4
DFF = 2816
NF = DFF // P
PAST, PAGE = 2048, 128
NPG = PAST // PAGE
TOPK = 256
DC = 64
EPS = 1e-6
NEG = -1e30
PICKED = -3e38


def rows_of(m):
    return P if m < NT - 1 else LAST


def clear_semaphores(nc, handles):
    with nc.Block() as block:
        @block.gpsimd
        def _(pool):
            for s in handles:
                pool.sem_clear(s)


TG = 3
WK = 2
NW = 4


def project_add_norm(nc, tag, const, x_in, act_t, kb, w_dram, gain_post, x_out, gain_next, h_t, y_outs=None):
    ident = const["ident"]
    with ExitStack() as ctx:
        def sb(name, shape, dt=F32):
            return ctx.enter_context(nc.sbuf_tensor(f"{tag}_{name}", shape, dt))

        used = []

        def sem(name):
            used.append(ctx.enter_context(nc.semaphore(f"{tag}_{name}")))
            return used[-1]

        NX = 3
        loads = kb // WK
        xt = sb("xt", [P, NX, D])
        sq = sb("sq", [P, D])
        stat = sb("stat", [P, NT, 8])
        if act_t is not None:
            yt = sb("yt", [P, TG, D])
            gp = sb("gp", [P, D])
            w_sb = sb("w", [P, NW, WK, D])
            ps_y = ctx.enter_context(nc.psum_tensor(f"{tag}_psy", [P, TG, D], F32))
        w_in = [sem(f"w_in{i}") for i in range(NW)]
        w_used = sem("w_used")
        if h_t is not None:
            xn = sb("xn", [P, 2, D])
            gn = sb("gn", [P, KD])
            ps_t = ctx.enter_context(nc.psum_tensor(f"{tag}_pst", [P, KD, P], F32))
        x_in_sem = [sem(f"x_in{i}") for i in range(NX)]
        gains_in = sem("gains_in")
        y_done = sem("y_done")
        y_read = sem("y_read")
        ysq_done = sem("ysq_done")
        yvar_done = sem("yvar_done")
        ystd_done = sem("ystd_done")
        x_new = sem("x_new")
        x_out_sem = [sem(f"x_out{i}") for i in range(NX)]
        xsq_done = sem("xsq_done")
        xvar_done = sem("xvar_done")
        xstd_done = sem("xstd_done")
        xrs_done = sem("xrs_done")
        xn_done = sem("xn_done")
        turned = sem("turned")
        h_done = sem("h_done")
        dve_chain = sem("dve_chain")

        ctx.callback(clear_semaphores, nc, used)
        block = ctx.enter_context(nc.Block())

        def stores(m):
            if y_outs is None:
                return [(x_out[m * P:m * P + rows_of(m), :], 0, rows_of(m))] if x_out is not None else []
            return y_outs(m)

        def stored(m):
            return 16 * sum(len(stores(i)) for i in range(m % NX, m + 1, NX))

        @block.sync
        def _(sp):
            if act_t is not None:
                sp.dma_start(gp[:], gain_post.partition_broadcast(P)).then_inc(gains_in, 16)
            if h_t is not None:
                sp.dma_start(gn[:], gain_next).then_inc(gains_in, 16)

            def load(m):
                r = rows_of(m)
                if m >= NX:
                    if stores(m - NX):
                        sp.wait_ge(x_out_sem[m % NX], stored(m - NX))
                    if h_t is not None:
                        sp.wait_ge(xn_done, m - NX + 1)
                sp.dma_start(xt[0:r, m % NX, :], x_in[m * P:m * P + r, :]).then_inc(x_in_sem[m % NX], 16)

            def load_w(n_load):
                g, c = divmod(n_load, loads)
                if n_load >= NW:
                    pg, pc = divmod(n_load - NW, loads)
                    if pc == loads - 1:
                        sp.wait_ge(y_done, TG * (pg + 1))
                    else:
                        sp.wait_ge(w_used, pg * (loads - 1) + pc + 1)
                sp.dma_start(w_sb[:, n_load % NW], w_dram[:, c * WK:(c + 1) * WK, :]).then_inc(w_in[n_load % NW], 16)

            def load_ws(a, b):
                for n_load in range(a, min(b, loads * (NT // TG))):
                    load_w(n_load)

            if act_t is not None:
                load_ws(0, NW)
            for m in range(min(2, NT)):
                load(m)
            if act_t is not None:
                load_ws(NW, loads + NW)
            for m in range(NT):
                if act_t is not None and m % TG == 0 and m:
                    load_ws((m // TG) * loads + NW, (m // TG + 1) * loads + NW)
                if m + 2 < NT:
                    load(m + 2)
                if act_t is not None:
                    sp.wait_ge(x_new, m + 1)
                else:
                    sp.wait_ge(x_in_sem[m % NX], 16 * (m // NX + 1))
                for dst, r0, nr in stores(m):
                    sp.dma_start(dst, xt[r0:r0 + nr, m % NX, :]).then_inc(x_out_sem[m % NX], 16)
            for i in range(NX):
                last = (NT - 1 - i) // NX * NX + i
                if stores(last):
                    sp.wait_ge(x_out_sem[i], stored(last))

        @block.tensor
        def _(pe):
            def turn(m):
                r = rows_of(m)
                pe.wait_ge(xn_done, m + 1)
                if m >= 1:
                    pe.wait_ge(h_done, m)
                for k in range(KD):
                    t = pe.transpose(ps_t[:, k, 0:r], xn[0:r, m % 2, k * P:(k + 1) * P], ident[0:r, 0:r])
                t.then_inc(turned, 1)

            for g in range(NT // TG):
                tiles = range(TG * g, TG * g + TG)
                for c in range(loads if act_t is not None else 0):
                    n_load = g * loads + c
                    pe.wait_ge(w_in[n_load % NW], 16 * (n_load // NW + 1))
                    for k in range(c * WK, (c + 1) * WK):
                        for m in tiles:
                            r = rows_of(m)
                            if k == 0 and g:
                                pe.wait_ge(y_read, m - TG + 1)
                            for n in range(2):
                                mm = pe.matmul(ps_y[0:r, m % TG, n * 512:(n + 1) * 512], act_t(k, m * P, r),
                                               w_sb[:, n_load % NW, k % WK, n * 512:(n + 1) * 512],
                                               start=(k == 0), stop=(k == kb - 1))
                            if k == kb - 1:
                                mm.then_inc(y_done, 1)
                            elif k % WK == WK - 1 and m == tiles[-1]:
                                mm.then_inc(w_used, 1)
                    if h_t is not None and g and c in (1, 2, 3):
                        turn(TG * (g - 1) + c - 1)
                if h_t is not None and (act_t is None or g == NT // TG - 1):
                    for m in tiles:
                        turn(m)

        @block.scalar
        def _(act):
            for m in range(NT):
                r = rows_of(m)
                if act_t is not None:
                    act.wait_ge(y_done, m + 1)
                    if m and h_t is None:
                        act.wait_ge(ysq_done, m)
                    if m >= TG:
                        act.wait_ge(x_new, m - TG + 1)
                    nc.scalar.activation(yt[0:r, m % TG, :], ps_y[0:r, m % TG, :], ACT.Copy).then_inc(y_read, 1)
                    act.wait_ge(y_read, m + 1)
                    nc.scalar.activation(sq[0:r, :], yt[0:r, m % TG, :], ACT.Square,
                                         accum_out=stat[0:r, m, 0:1]).then_inc(ysq_done, 1)
                    act.wait_ge(yvar_done, m + 1)
                    nc.scalar.activation(stat[0:r, m, 2:3], stat[0:r, m, 1:2], ACT.Sqrt).then_inc(ystd_done, 1)
                if h_t is None:
                    continue
                if act_t is not None:
                    act.wait_ge(x_new, m + 1)
                    act.wait_ge(ysq_done, m + 1)
                else:
                    act.wait_ge(x_in_sem[m % NX], 16 * (m // NX + 1))
                if m:
                    act.wait_ge(xsq_done, m)
                nc.scalar.activation(sq[0:r, :], xt[0:r, m % NX, :], ACT.Square,
                                     accum_out=stat[0:r, m, 4:5]).then_inc(xsq_done, 1)
                act.wait_ge(xvar_done, m + 1)
                nc.scalar.activation(stat[0:r, m, 6:7], stat[0:r, m, 5:6], ACT.Sqrt).then_inc(xstd_done, 1)
                act.wait_ge(xrs_done, m + 1)
                if m >= 2:
                    act.wait_ge(turned, m - 1)
                nc.scalar.activation(xn[0:r, m % 2, :], xt[0:r, m % NX, :], ACT.Copy,
                                     scale=stat[0:r, m, 7:8]).then_inc(xn_done, 1)
                act.wait_ge(xsq_done, m + 1)

        @block.vector
        def _(dve):
            chain = [0]

            def link(ins):
                chain[0] += 1
                ins.then_inc(dve_chain, 1)
                dve.wait_ge(dve_chain, chain[0])

            dve.wait_ge(gains_in, 16 * ((act_t is not None) + (h_t is not None)))

            def spread(m):
                r = rows_of(m)
                dve.wait_ge(turned, m + 1)
                nc.vector.tensor_tensor(h_t[:, :, m * P:m * P + r], ps_t[:, :, 0:r],
                                        gn[:].unsqueeze(2).to_broadcast([P, KD, r]), ALU.mult).then_inc(h_done, 1)

            for m in range(NT):
                r = rows_of(m)
                if act_t is not None:
                    dve.wait_ge(ysq_done, m + 1)
                    nc.vector.tensor_scalar(stat[0:r, m, 1:2], stat[0:r, m, 0:1], 1.0 / D, EPS,
                                            ALU.mult, ALU.add).then_inc(yvar_done, 1)
                    dve.wait_ge(ystd_done, m + 1)
                    link(nc.vector.reciprocal(stat[0:r, m, 3:4], stat[0:r, m, 2:3]))
                    link(nc.vector.scalar_tensor_tensor(out=yt[0:r, m % TG, :], in0=yt[0:r, m % TG, :],
                                                        scalar=stat[0:r, m, 3:4], in1=gp[0:r, :],
                                                        op0=ALU.mult, op1=ALU.mult))
                    dve.wait_ge(x_in_sem[m % NX], 16 * (m // NX + 1))
                    nc.vector.tensor_tensor(xt[0:r, m % NX, :], xt[0:r, m % NX, :], yt[0:r, m % TG, :],
                                            ALU.add).then_inc(x_new, 1)
                if h_t is None:
                    dve.wait_ge(x_new, m + 1)
                    continue
                dve.wait_ge(xsq_done, m + 1)
                nc.vector.tensor_scalar(stat[0:r, m, 5:6], stat[0:r, m, 4:5], 1.0 / D, EPS,
                                        ALU.mult, ALU.add).then_inc(xvar_done, 1)
                dve.wait_ge(xstd_done, m + 1)
                nc.vector.reciprocal(stat[0:r, m, 7:8], stat[0:r, m, 6:7]).then_inc(xrs_done, 1)
                if m >= 1:
                    spread(m - 1)
            if h_t is not None:
                spread(NT - 1)


CHUNK_ENDS = [m * P + P - 1 for m in range(NT - 1)] + [TP - 1] + [TP + DT * b + DT - 1 for b in range(DB)]
LEVELS = 7
NU = 2 * H


def level_width(level):
    b = 64 >> level
    return (NT - 1) * P if b >= 16 else (TP if b >= 4 else T)


def gate_rows(nc, const, h_t, w_gates, b_gates, m0, lb_logits, rows, cols, lb, one_lb, m_out):
    ident = const["ident"]
    with ExitStack() as ctx:
        def sb(name, shape, dt=F32):
            return ctx.enter_context(nc.sbuf_tensor(f"g_{name}", shape, dt))

        used = []

        def sem(name):
            used.append(ctx.enter_context(nc.semaphore(f"g_{name}")))
            return used[-1]

        wg = sb("wg", [P, KD, 2 * H])
        bg = sb("bg", [P, 2 * H])
        m0s = sb("m0s", [H, DB])
        lg = sb("lg", [P, 2, H])
        lgx = sb("lgx", [P, 6, H])
        gc = sb("gc", [P, NT, 2 * H])
        ta = sb("ta", [P, NT, H])
        te = sb("te", [P, NT, H])
        lfc = sb("lfc", [P, NT, H])
        ir = sb("ir", [H, T])
        im = sb("im", [H, T])
        lf = sb("lf", [H, T])
        lfm = sb("lfm", [H, T])
        br = sb("br", [H, T])
        mr = sb("mr", [H, T])
        mp = sb("mp", [H, T])
        cs = sb("cs", [H, 3, T])
        ps_g = ctx.enter_context(nc.psum_tensor("g_psg", [P, NT, 2 * H], F32))
        ps_r = ctx.enter_context(nc.psum_tensor("g_psr", [H, 2, 3, 512], F32))
        ps_c = ctx.enter_context(nc.psum_tensor("g_psc", [P, NT, 3, H], F32))
        loaded, gates_done, biased, abs_done, exp_done, ln_done = (
            sem(x) for x in ("loaded", "gates_done", "biased", "abs_done", "exp_done", "ln_done"))
        lf_done, rows_done, expo_ready, rows_exp, cols_ready, cols_done = (
            sem(x) for x in ("lf_done", "rows_done", "expo_ready", "rows_exp", "cols_ready", "cols_done"))
        cols_out, lb_sub, lb_exp, chain_s, stored, achain = (
            sem(x) for x in ("cols_out", "lb_sub", "lb_exp", "chain", "stored", "achain"))
        reset = const["reset"]
        ctx.callback(clear_semaphores, nc, used)
        block = ctx.enter_context(nc.Block())

        @block.sync
        def _(sp):
            for dst, src in ((wg[:], w_gates), (bg[:], b_gates.partition_broadcast(P)), (m0s[:], m0), (lg[:], lb_logits)):
                sp.dma_start(dst, src).then_inc(loaded, 16)
            sp.wait_ge(cols_ready, 1)
            with nc.allow_non_contiguous_dma(reason="36 stabilisers"):
                sp.dma_start(m_out[:, 0:1], mr[:, TP - 1:TP]).then_inc(stored, 16)
                sp.dma_start(m_out[:, 1:1 + DB], mr[:, TP + DT - 1:T:DT]).then_inc(stored, 16)
            sp.wait_ge(stored, 32)

        @block.tensor
        def _(pe):
            pe.wait_ge(loaded, 64)
            for m in range(NT):
                for k in range(KD):
                    mm = pe.matmul(ps_g[0:rows_of(m), m, :], h_t[:, k, m * P:m * P + rows_of(m)], wg[:, k, :],
                                   start=(k == 0), stop=(k == KD - 1))
            mm.then_inc(gates_done, 1)
            pe.wait_ge(lf_done, 1)
            for m in range(NT):
                r = rows_of(m)
                for kind, src in ((0, gc[0:r, m, 0:H]), (1, lfc[0:r, m, :])):
                    t = pe.transpose(ps_r[:, kind, m // 4, (m % 4) * P:(m % 4) * P + r], src, ident[0:r, 0:r])
            t.then_inc(rows_done, 1)
            pe.wait_ge(cols_ready, 2)
            pe.wait_ge(rows_exp, 2)
            for m in range(NT):
                r = rows_of(m)
                for kind in range(3):
                    t = pe.transpose(ps_c[0:r, m, kind, :], cs[:, kind, m * P:m * P + r], ident[0:H, 0:H])
            t.then_inc(cols_done, 1)

        @block.scalar
        def _(act):
            act.wait_ge(lb_sub, 1)
            nc.scalar.activation(lgx[:, 1:3, :], lg[:], ACT.Exp).then_inc(lb_exp, 1)
            act.wait_ge(abs_done, 1)
            nc.scalar.activation(te[:], ta[:], ACT.Exp, scale=-1.0).then_inc(achain, 1)
            act.wait_ge(achain, 1)
            nc.scalar.activation(ta[:], te[:], ACT.Ln, bias=1.0).then_inc(ln_done, 1)
            act.wait_ge(expo_ready, 1)
            nc.scalar.activation(rows[:, 1, :], mp[:], ACT.Exp).then_inc(rows_exp, 1)
            act.wait_ge(cols_ready, 2)
            nc.scalar.activation(cs[:, 1, :], cs[:, 1, :], ACT.Exp).then_inc(achain, 1)
            nc.scalar.activation(cs[:, 2, :], mr[:], ACT.Exp, scale=-1.0).then_inc(achain, 1)
            act.wait_ge(achain, 3)
            nc.scalar.activation(te[:, 0, 0:1], ta[:, 0, 0:1], ACT.Copy).then_inc(rows_exp, 1)

        @block.vector
        def _(dve):
            n = [0]

            def link(ins):
                n[0] += 1
                ins.then_inc(chain_s, 1)
                dve.wait_ge(chain_s, n[0])

            dve.wait_ge(loaded, 64)
            link(nc.vector.tensor_tensor(lgx[:, 0, :], lg[:, 0, :], lg[:, 1, :], ALU.max))
            nc.vector.tensor_tensor(lg[:], lg[:], lgx[:, 0, :].unsqueeze(1).to_broadcast([P, 2, H]), ALU.subtract).then_inc(lb_sub, 1)
            dve.wait_ge(lb_exp, 1)
            link(nc.vector.tensor_tensor(lgx[:, 3, :], lgx[:, 1, :], lgx[:, 2, :], ALU.add))
            link(nc.vector.reciprocal(lgx[:, 4, :], lgx[:, 3, :]))
            link(nc.vector.tensor_tensor(lb[:], lgx[:, 1, :], lgx[:, 4, :], ALU.mult))
            link(nc.vector.tensor_scalar(one_lb[:], lb[:], -1.0, 1.0, ALU.mult, ALU.add))
            link(nc.vector.memset(gc[:], 0.0))
            dve.wait_ge(gates_done, 1)
            link(nc.vector.tensor_tensor(gc[:, 0:NT - 1, :], ps_g[:, 0:NT - 1, :],
                                         bg[:].unsqueeze(1).to_broadcast([P, NT - 1, 2 * H]), ALU.add))
            link(nc.vector.tensor_tensor(gc[0:LAST, NT - 1, :], ps_g[0:LAST, NT - 1, :], bg[0:LAST, :], ALU.add))
            f = gc[:, :, H:2 * H]
            nc.vector.scalar_tensor_tensor(out=ta[:], in0=f, scalar=-1.0, in1=f, op0=ALU.mult, op1=ALU.max).then_inc(abs_done, 1)
            dve.wait_ge(ln_done, 1)
            nc.vector.scalar_tensor_tensor(out=lfc[:], in0=f, scalar=0.0, in1=ta[:], op0=ALU.min, op1=ALU.subtract).then_inc(lf_done, 1)
            dve.wait_ge(rows_done, 1)
            for kind, dst in ((0, ir), (1, lf)):
                for c in range(3):
                    w = min(512, T - c * 512)
                    link(nc.vector.tensor_copy(dst[:, c * 512:c * 512 + w], ps_r[:, kind, c, 0:w]))
            starts = slice(TP, T, DT)
            link(nc.vector.tensor_tensor_scan(br[:], reset[0:H, :], lf[:], 0.0, ALU.mult, ALU.add))
            link(nc.vector.tensor_copy(im[:], ir[:]))
            link(nc.vector.tensor_copy(lfm[:], lf[:]))
            link(nc.vector.tensor_tensor(mp[:, 0:DB], lf[:, starts], m0s[:], ALU.add))
            link(nc.vector.tensor_tensor(im[:, starts], ir[:, starts], mp[:, 0:DB], ALU.max))
            link(nc.vector.memset(lfm[:, starts], NEG))
            link(nc.vector.tensor_tensor_scan(mr[:], lfm[:], im[:], 0.0, ALU.add, ALU.max))
            nc.vector.tensor_tensor(rows[:, 0, :], br[:], mr[:], ALU.subtract).then_inc(cols_ready, 1)
            dve.wait_ge(cols_ready, 1)
            full = (NT - 2) * P
            link(nc.vector.memset(mp[:, 0:P], 0.0))
            link(nc.vector.tensor_copy(mp[:, P:P + full].rearrange("h (m t) -> h m t", t=P),
                                       mr[:, P - 1:P - 1 + full:P].unsqueeze(2).to_broadcast([H, NT - 2, P])))
            link(nc.vector.tensor_copy(mp[:, (NT - 1) * P:TP], mr[:, (NT - 1) * P - 1:(NT - 1) * P].to_broadcast([H, PTAIL])))
            link(nc.vector.tensor_copy(mp[:, TP:T].rearrange("h (b t) -> h b t", t=DT),
                                       m0s[:].unsqueeze(2).to_broadcast([H, DB, DT])))
            nc.vector.tensor_tensor(mp[:], mp[:], rows[:, 0, :], ALU.add).then_inc(expo_ready, 1)
            link(nc.vector.tensor_tensor(cs[:, 0, :], ir[:], br[:], ALU.subtract))
            ra = rows[:, 0, :]
            nb = NT - 1
            link(nc.vector.tensor_tensor(cs[:, 1, 0:nb * P].rearrange("h (m t) -> h m t", t=P),
                                         cs[:, 0, 0:nb * P].rearrange("h (m t) -> h m t", t=P),
                                         ra[:, P - 1:nb * P:P].unsqueeze(2).to_broadcast([H, nb, P]), ALU.add))
            link(nc.vector.tensor_tensor(cs[:, 1, nb * P:TP], cs[:, 0, nb * P:TP],
                                         ra[:, TP - 1:TP].to_broadcast([H, PTAIL]), ALU.add))
            nc.vector.tensor_tensor(cs[:, 1, TP:T].rearrange("h (b t) -> h b t", t=DT),
                                    cs[:, 0, TP:T].rearrange("h (b t) -> h b t", t=DT),
                                    ra[:, TP + DT - 1:T:DT].unsqueeze(2).to_broadcast([H, DB, DT]), ALU.add).then_inc(cols_ready, 1)
            dve.wait_ge(cols_done, 1)
            link(nc.vector.memset(cols[:], 1.0))
            link(nc.vector.tensor_copy(cols[:, 0:nb, :, :], ps_c[:, 0:nb, :, :]))
            link(nc.vector.tensor_copy(cols[0:LAST, nb, :, :], ps_c[0:LAST, nb, :, :]))


def recurrent_mixers(nc, const, h_t, mix_t, w_units, states_a, states_b, rows, cols, lb, one_lb,
                     g_norms, new_a, new_b):
    ident = const["ident"]
    with ExitStack() as ctx:
        def sb(name, shape, dt=F32):
            return ctx.enter_context(nc.sbuf_tensor(f"r_{name}", shape, dt))

        def psum(name, shape):
            return ctx.enter_context(nc.psum_tensor(f"r_{name}", shape, F32))

        used = []

        def sem(name):
            used.append(ctx.enter_context(nc.semaphore(f"r_{name}")))
            return used[-1]

        E = P + 1
        w_sb = sb("w", [P, 2, KD, 2 * P])
        q_t = sb("q", [P, 2, T])
        k_t = sb("k", [P, 2, T])
        vg = sb("vg", [P, 2, NT, 2 * E])
        b_t = sb("b", [P, T])
        e1 = sb("e1", [P, T])
        dd = sb("dd", [P, 2, T])
        xx = sb("xx", [P, 2, T])
        at = sb("at", [P, NT, P])
        kh = sb("kh", [P, NT, P])
        khx = sb("khx", [LAST, DB + 1, P])
        qx = sb("qx", [P, DB + 1, LAST])
        s_pr = sb("s_pr", [P, NT + 1, E])
        s_in = sb("s_in", [P, DB, E])
        s_new = sb("s_new", [P, DB, E])
        o_sb = sb("o", [P, NT, E])
        sq = sb("sq", [P, NT, P])
        gno = sb("gno", [P, 2, P])
        st = sb("st", [P, 8, NT])
        masks, negm, negtail = const["level_masks"], const["neg_upper"], const["neg_tail"]
        row_mask, col_mask, reset, sel4 = const["row_mask"], const["col_mask"], const["reset"], const["sel4"]

        ps_p = psum("psp", [P, 2, 512])
        ps_a = psum("psa", [P, 2, 4, P])
        ps_at = psum("psat", [LAST, 512])
        ps_t = psum("pst", [P, 4, P])
        ps_u = psum("psu", [P, 512])
        ps_o = psum("pso", [P, 512])

        w_in = [sem("w_in0"), sem("w_in1")]
        s_ld = sem("s_ld")
        g_in, proj_done, proj_free = sem("g_in"), sem("proj_done"), sem("proj_free")
        dve_unit = sem("dve_unit")
        acts, achain, dchain = sem("acts"), sem("achain"), sem("dchain")
        lf_ready, b_ready, e1_ready, d_ready, e_ready, x_ready = (
            sem(x) for x in ("lf_ready", "b_ready", "e1_ready", "d_ready", "e_ready", "x_ready"))
        a_done, a_used, at_done, at_used = sem("a_done"), sem("a_used"), sem("at_done"), sem("at_used")
        kx_ready, kt_done, kt_used, khx_ready = sem("kx_ready"), sem("kt_done"), sem("kt_used"), sem("khx_ready")
        u_done, u_used, o_done, o_used = sem("u_done"), sem("u_used"), sem("o_done"), sem("o_used")
        sq_ready, std_in, std_out, y_ready = sem("sq_ready"), sem("std_in"), sem("std_out"), sem("y_ready")
        yt_done, yt_used, s_out, init = sem("yt_done"), sem("yt_used"), sem("s_out"), sem("init")
        bc_done, bc_a, bc_d, wm_ready, w_ready = sem("bc_done"), sem("bc_a"), sem("bc_d"), sem("wm_ready"), sem("w_ready")
        g_ready = sem("g_ready")
        ctx.callback(clear_semaphores, nc, used)
        block = ctx.enter_context(nc.Block())

        NG = 15
        KG = 3
        groups = [(0, 4), (4, 4), (8, 1)]
        UPD = NT + DB
        UG = [(i, min(3, UPD - i)) for i in range(0, UPD, 3)]
        OG = [(i, 3) for i in range(0, NT, 3)]
        tails = [i for i in range(LEVELS + 1) if i == LEVELS or level_width(i) > (NT - 1) * P]
        NTAIL = len(tails)

        @block.sync
        def _(sp):
            sp.dma_start(gno[:], g_norms.partition_broadcast(P)).then_inc(g_in, 16)
            for u in range(NU + 1):
                if u < NU:
                    for half in range(2):
                        if u:
                            sp.wait_ge(proj_done, NG * (u - 1) + (6 if half == 0 else NG))
                        sp.dma_start(w_sb[:, half], w_units[u, :, :, half * 2 * P:(half + 1) * 2 * P]).then_inc(w_in[half], 16)
                if u >= 1:
                    v = u - 1
                    sp.wait_ge(u_used, len(UG) * (v + 1))
                    e, out = (P, new_a[v]) if v < H else (E, new_b[v - H])
                    sp.dma_start(out[:, 0, :], s_pr[:, NT, 0:e]).then_inc(s_out, 16)
                    sp.dma_start(out[:, 1:1 + DB, :], s_new[:, :, 0:e]).then_inc(s_out, 16)
                if u < NU:
                    if u:
                        sp.wait_ge(o_done, len(OG) * u)
                    if u < H:
                        sp.dma_start(s_in[:, :, 0:P], states_a[u]).then_inc(s_ld, 16)
                    else:
                        sp.dma_start(s_in[:], states_b[u - H]).then_inc(s_ld, 16)
            sp.wait_ge(s_out, 32 * NU)

        @block.tensor
        def _(pe):
            def project(u, i):
                g = NG * u + i
                if i in (0, 6):
                    pe.wait_ge(w_in[i // 6], 16 * (u + 1))
                if g >= 2:
                    pe.wait_ge(proj_free, g - 1)
                for k in range(KD):
                    if i < 6:
                        t0, tw = CH[i % 3]
                        mm = pe.matmul(ps_p[:, g % 2, 0:tw], w_sb[:, 0, k, (i // 3) * P:(i // 3 + 1) * P],
                                       h_t[:, k, t0:t0 + tw], start=(k == 0), stop=(k == KD - 1))
                    else:
                        m = i - 6
                        mm = pe.matmul(ps_p[0:rows_of(m), g % 2, 0:2 * P], h_t[:, k, m * P:m * P + rows_of(m)],
                                       w_sb[:, 1, k, :], start=(k == 0), stop=(k == KD - 1))
                mm.then_inc(proj_done, 1)

            def level(u, lv):
                q, k = q_t[:, u % 2], k_t[:, u % 2]
                n = (LEVELS + 1) * u + lv
                if lv < LEVELS:
                    pe.wait_ge(x_ready, LEVELS * u + lv + 1)
                for g in range(2):
                    if n >= 1:
                        pe.wait_ge(a_used, 2 * (n - 1) + g + 1)
                    for j in range(4):
                        c = slice((4 * g + j) * P, (4 * g + j + 1) * P)
                        x = xx[:, lv % 2, c] if lv < LEVELS else None
                        mm = pe.matmul(ps_a[:, g, j, :], k[:, c] if x is None else x, q[:, c] if x is None else x,
                                       start=True, stop=True)
                    mm.then_inc(a_done, 1)
                if lv in tails:
                    n = NTAIL * u + tails.index(lv)
                    r = LAST if lv == LEVELS else level_width(lv) - (NT - 1) * P
                    c = slice((NT - 1) * P, (NT - 1) * P + r)
                    if n >= 1:
                        pe.wait_ge(at_used, n)
                    x = xx[:, lv % 2, c] if lv < LEVELS else None
                    pe.matmul(ps_at[0:r, 0:r], k[:, c] if x is None else x, q[:, c] if x is None else x,
                              start=True, stop=True).then_inc(at_done, 1)

            def spread_rows(h, c):
                t0, tw = CH[c]
                if c == 0 and h == 0:
                    pe.wait_ge(a_used, 2 * (LEVELS + 1) * H)
                if c == 0 and h > 0:
                    pe.wait_ge(a_used, 2 * (LEVELS + 1) * H + 2 * h)
                if c or h:
                    pe.wait_ge(bc_a, 3 * h + c)
                    pe.wait_ge(bc_d, 3 * h + c)
                for kind in range(2):
                    mm = pe.matmul(ps_a[:, kind].rearrange("p a b -> p (a b)")[:, 0:tw], sel4[:, h, :],
                                   rows[:, kind, t0:t0 + tw], start=True, stop=True)
                mm.then_inc(bc_done, 1)

            def scores(u):
                h = u - H
                q, k = q_t[:, u % 2], k_t[:, u % 2]
                pe.wait_ge(bc_a, 3 * h + 3)
                pe.wait_ge(bc_d, 3 * h + 3)
                for g in range(2):
                    for j in range(4):
                        c = slice((4 * g + j) * P, (4 * g + j + 1) * P)
                        mm = pe.matmul(ps_a[:, g, j, :], k[:, c], q[:, c], start=True, stop=True)
                    mm.then_inc(a_done, 1)
                pe.wait_ge(at_used, NTAIL * H + h)
                c = slice((NT - 1) * P, T)
                pe.matmul(ps_at[0:LAST, 0:LAST], k[:, c], q[:, c], start=True, stop=True).then_inc(at_done, 1)

            def turn_k(u):
                src = xx[:, 0, :] if u < H else k_t[:, u % 2]
                if u < H:
                    pe.wait_ge(kx_ready, u + 1)
                for gi, (m0, n) in enumerate(groups):
                    g = KG * u + gi
                    if g:
                        pe.wait_ge(kt_used, g)
                    if gi == 0 and u:
                        pe.wait_ge(yt_used, KG * u)
                    for j in range(n):
                        r = rows_of(m0 + j)
                        t = pe.transpose(ps_t[0:r, j, :], src[:, (m0 + j) * P:(m0 + j) * P + r], ident[:])
                    t.then_inc(kt_done, 1)

            def update(u):
                pe.wait_ge(kt_used, KG * (u + 1))
                pe.wait_ge(khx_ready, u + 1)
                e = P if u < H else E
                for gi, (i0, n) in enumerate(UG):
                    g = len(UG) * u + gi
                    if g:
                        pe.wait_ge(u_used, g)
                    for i in range(i0, i0 + n):
                        lhs = kh[:, i, :] if i < NT - 1 else khx[:, i - (NT - 1), :]
                        m = min(i, NT - 1)
                        mm = pe.matmul(ps_u[:, (i - i0) * E:(i - i0) * E + e], lhs, vg[0:rows_of(m), u % 2, m, 0:e],
                                       start=True, stop=True)
                    mm.then_inc(u_done, 1)

            def outputs(u):
                e = P if u < H else E
                pe.wait_ge(u_used, len(UG) * (u + 1))
                for gi, (m0, n) in enumerate(OG):
                    g = len(OG) * u + gi
                    if g:
                        pe.wait_ge(o_used, g)
                    for m in range(m0, m0 + n):
                        r = rows_of(m)
                        o = ps_o[0:r, (m - m0) * E:(m - m0) * E + e]
                        pe.matmul(o, at[0:r, m, 0:r], vg[0:r, u % 2, m, 0:e], start=True, stop=False)
                        if m < NT - 1:
                            mm = pe.matmul(o, e1[:, m * P:(m + 1) * P], s_pr[:, m, 0:e], start=False, stop=True)
                        else:
                            pe.matmul(o, qx[:, 0, :], s_pr[:, m, 0:e], start=False, stop=False)
                            for b in range(DB):
                                mm = pe.matmul(o, qx[:, 1 + b, :], s_in[:, b, 0:e], start=False,
                                               stop=(b == DB - 1))
                    mm.then_inc(o_done, 1)

            def turn_y(u):
                pe.wait_ge(y_ready, u + 1)
                for gi, (m0, n) in enumerate(groups):
                    if gi:
                        pe.wait_ge(yt_used, KG * u + gi)
                    for j in range(n):
                        r = rows_of(m0 + j)
                        t = pe.transpose(ps_t[:, j, 0:r], sq[0:r, m0 + j, :], ident[0:r, 0:r])
                    t.then_inc(yt_done, 1)

            pe.wait_ge(init, 1)
            for i in range(NG):
                project(0, i)
            for u in range(NU):
                for i in range(NG):
                    if u + 1 < NU:
                        project(u + 1, i)
                    if u < H and 3 <= i <= 3 + LEVELS:
                        if i == 3:
                            pe.wait_ge(acts, u + 1)
                        level(u, i - 3)
                    if u >= H and 1 <= i <= 3:
                        if i == 1:
                            pe.wait_ge(acts, u + 1)
                        spread_rows(u - H, i - 1)
                    if u >= H and i == 4:
                        scores(u)
                    if i == 10:
                        turn_k(u)
                    if i == 11:
                        update(u)
                    if i == 12:
                        outputs(u)
                    if i == 14:
                        turn_y(u)

        @block.scalar
        def _(act):
            n = [0]

            def link(ins):
                n[0] += 1
                ins.then_inc(achain, 1)
                act.wait_ge(achain, n[0])

            scale = float(P) ** -0.5

            def evacuate(u, i):
                g = NG * u + i
                if i == 0 and u >= 2:
                    act.wait_ge(dve_unit, u - 1)
                act.wait_ge(proj_done, g + 1)
                if i < 6:
                    t0, tw = CH[i % 3]
                    dst = (q_t if i < 3 else k_t)[:, u % 2, t0:t0 + tw]
                    s = scale if (i < 3) == (u < H) else 1.0
                    nc.scalar.activation(dst, ps_p[:, g % 2, 0:tw], ACT.Copy, scale=s).then_inc(proj_free, 1)
                else:
                    m = i - 6
                    r = rows_of(m)
                    nc.scalar.activation(vg[0:r, u % 2, m, :].rearrange("p (two e) -> p two e", e=E)[:, :, 0:P],
                                         ps_p[0:r, g % 2, 0:2 * P].rearrange("p (two e) -> p two e", e=P),
                                         ACT.Copy).then_inc(proj_free, 1)

            act.wait_ge(init, 1)
            for i in range(NG):
                evacuate(0, i)
            for u in range(NU):
                h = u - H
                q, k = q_t[:, u % 2], k_t[:, u % 2]
                act.wait_ge(proj_free, NG * (u + 1))
                g = vg[:, u % 2, :, E:E + P]
                if u < H:
                    link(nc.scalar.activation(k, k, ACT.Sigmoid))
                    nc.scalar.activation(sq[:], g, ACT.Sigmoid).then_inc(acts, 1)
                    nc.scalar.activation(b_t[:], k, ACT.Ln, bias=lb[:, u:u + 1], scale=one_lb[:, u:u + 1]).then_inc(lf_ready, 1)
                else:
                    nc.scalar.activation(sq[:], g, ACT.Sigmoid).then_inc(acts, 1)
                for i in range(NG):
                    if u + 1 < NU:
                        evacuate(u + 1, i)
                    if u < H:
                        if i == 1:
                            act.wait_ge(b_ready, u + 1)
                            nc.scalar.activation(e1[:], b_t[:], ACT.Exp).then_inc(e1_ready, 1)
                        if 2 <= i < 2 + LEVELS:
                            lv = i - 2
                            w = level_width(lv)
                            act.wait_ge(d_ready, LEVELS * u + lv + 1)
                            nc.scalar.activation(dd[:, lv % 2, 0:w], dd[:, lv % 2, 0:w], ACT.Exp).then_inc(e_ready, 1)
                        if i == 9:
                            act.wait_ge(wm_ready, u + 1)
                            nc.scalar.activation(dd[:, 1, :], dd[:, 1, :], ACT.Exp).then_inc(w_ready, 1)
                    else:
                        if 1 <= i <= 3:
                            t0, tw = CH[i - 1]
                            act.wait_ge(bc_done, 3 * h + i)
                            nc.scalar.activation(e1[:, t0:t0 + tw], ps_a[:, 1].rearrange("p a b -> p (a b)")[:, 0:tw],
                                                 ACT.Copy).then_inc(bc_a, 1)
                        if i == 4:
                            act.wait_ge(bc_d, 3 * h + 3)
                            for m in range(NT):
                                r = rows_of(m)
                                e = nc.scalar.activation(dd[0:r, 0, m * P:m * P + r], dd[0:r, 0, m * P:m * P + r],
                                                         ACT.Exp, bias=cols[0:r, m, 0, h:h + 1])
                            e.then_inc(wm_ready, 1)
                    if i == 10:
                        for gi, (m0, nn) in enumerate(groups):
                            act.wait_ge(kt_done, KG * u + gi + 1)
                            r = rows_of(m0)
                            if u < H:
                                nc.scalar.activation(kh[0:r, m0:m0 + nn, :], ps_t[0:r, 0:nn, :], ACT.Copy).then_inc(kt_used, 1)
                            else:
                                for j in range(nn):
                                    e = nc.scalar.activation(kh[0:r, m0 + j, :], ps_t[0:r, j, :], ACT.Copy,
                                                             scale=cols[0:r, m0 + j, 1, h:h + 1])
                                e.then_inc(kt_used, 1)
                    if i == 12:
                        e = P if u < H else E
                        for gi, (m0, nn) in enumerate(OG):
                            act.wait_ge(o_done, len(OG) * u + gi + 1)
                            src = ps_o[:, 0:3 * E].rearrange("p (m e) -> p m e", e=E)
                            if m0 + nn == NT:
                                link(nc.scalar.activation(o_sb[:, m0:NT - 1, 0:e], src[:, 0:nn - 1, 0:e], ACT.Copy))
                                nc.scalar.activation(o_sb[0:LAST, NT - 1, 0:e], src[0:LAST, nn - 1, 0:e], ACT.Copy).then_inc(o_used, 1)
                            else:
                                nc.scalar.activation(o_sb[:, m0:m0 + nn, 0:e], src[:, 0:nn, 0:e], ACT.Copy).then_inc(o_used, 1)
                    if i == 13:
                        act.wait_ge(g_ready, u + 1)
                        act.wait_ge(o_used, len(OG) * (u + 1))
                        nc.scalar.activation(sq[:], o_sb[:, :, 0:P], ACT.Square).then_inc(sq_ready, 1)
                        act.wait_ge(std_in, u + 1)
                        nc.scalar.activation(st[:, 2, :], st[:, 1, :], ACT.Sqrt).then_inc(std_out, 1)
                    if i == 14:
                        for gi, (m0, nn) in enumerate(groups):
                            act.wait_ge(yt_done, KG * u + gi + 1)
                            r = rows_of(m0)
                            nc.scalar.activation(mix_t[:, u, m0 * P:m0 * P + (nn - 1) * P + r].rearrange("p (m t) -> p m t", t=r),
                                                 ps_t[:, 0:nn, 0:r], ACT.Copy).then_inc(yt_used, 1)

        @block.vector
        def _(dve):
            n = [0]

            def link(ins):
                n[0] += 1
                ins.then_inc(dchain, 1)
                dve.wait_ge(dchain, n[0])

            link(nc.vector.memset(vg[:], 0.0))
            link(nc.vector.memset(vg[:, :, :, P:P + 1], 1.0))
            link(nc.vector.memset(at[:], 0.0))
            link(nc.vector.memset(o_sb[:], 0.0))
            nc.vector.memset(s_pr[:, 0, :], 0.0).then_inc(init, 1)
            dve.wait_ge(init, 1)
            dve.wait_ge(g_in, 16)

            def halves(x, w, b):
                v = x[:, 0:w].rearrange("p (n two b) -> p n two b", two=2, b=b)
                return v[:, :, 0, :], v[:, :, 1, :]

            def differences(u, lv):
                b, w = 64 >> lv, level_width(lv)
                left, right = halves(b_t, w, b)
                dl, dr = halves(dd[:, lv % 2], w, b)
                mid = left[:, :, b - 1:b].to_broadcast([P, w // (2 * b), b])
                link(nc.vector.tensor_tensor(dl, mid, left, ALU.subtract))
                nc.vector.tensor_tensor(dr, right, mid, ALU.subtract).then_inc(d_ready, 1)
                dve.wait_ge(d_ready, LEVELS * u + lv + 1)

            def decayed(u, lv):
                b, w = 64 >> lv, level_width(lv)
                el, er = halves(dd[:, lv % 2], w, b)
                xl, xr = halves(xx[:, lv % 2], w, b)
                kl, _ = halves(k_t[:, u % 2], w, b)
                _, qr = halves(q_t[:, u % 2], w, b)
                dve.wait_ge(e_ready, LEVELS * u + lv + 1)
                link(nc.vector.tensor_tensor(xl, el, kl, ALU.mult))
                nc.vector.tensor_tensor(xr, er, qr, ALU.mult).then_inc(x_ready, 1)
                dve.wait_ge(x_ready, LEVELS * u + lv + 1)

            def keep(u, lv):
                nn = (LEVELS + 1) * u + lv
                for g in range(2):
                    dve.wait_ge(a_done, 2 * nn + g + 1)
                    nc.vector.copy_predicated(at[:, 4 * g:4 * g + 4, :],
                                              masks[:, lv, :].bitcast(U32).unsqueeze(1).to_broadcast([P, 4, P]),
                                              ps_a[:, g]).then_inc(a_used, 1)
                    dve.wait_ge(a_used, 2 * nn + g + 1)
                if lv in tails:
                    nt = NTAIL * u + tails.index(lv)
                    r = LAST if lv == LEVELS else level_width(lv) - (NT - 1) * P
                    dve.wait_ge(at_done, nt + 1)
                    nc.vector.copy_predicated(at[0:r, NT - 1, 0:r], masks[0:r, lv, 0:r].bitcast(U32),
                                              ps_at[0:r, 0:r]).then_inc(at_used, 1)
                    dve.wait_ge(at_used, nt + 1)

            for u in range(NU):
                h = u - H
                q, k = q_t[:, u % 2], k_t[:, u % 2]
                dve.wait_ge(acts, u + 1)
                g = vg[:, u % 2, :, E:E + P]
                gain = gno[:, 0 if u < H else 1, :].unsqueeze(1).to_broadcast([P, NT, P])
                if u < H:
                    link(nc.vector.tensor_tensor(g, g, sq[:], ALU.mult))
                    nc.vector.tensor_tensor(g, g, gain, ALU.mult).then_inc(g_ready, 1)
                else:
                    nc.vector.tensor_tensor(g, sq[:], gain, ALU.mult).then_inc(g_ready, 1)
                if u < H:
                    dve.wait_ge(lf_ready, u + 1)
                    link(nc.vector.tensor_scalar(k, k, -1.0, 1.0, ALU.mult, ALU.add))
                    link(nc.vector.tensor_scalar(k, k, one_lb[:, u:u + 1], None, ALU.mult))
                    nc.vector.tensor_tensor_scan(b_t[:], reset[:], b_t[:], 0.0, ALU.mult, ALU.add).then_inc(b_ready, 1)
                    dve.wait_ge(b_ready, u + 1)
                    differences(u, 0)
                    for lv in range(LEVELS):
                        if lv + 1 < LEVELS:
                            differences(u, lv + 1)
                        decayed(u, lv)
                        if lv:
                            keep(u, lv - 1)
                    keep(u, LEVELS - 1)
                    keep(u, LEVELS)
                    nb = NT - 1
                    d2 = dd[:, 1]
                    link(nc.vector.tensor_tensor(d2[:, 0:nb * P].rearrange("p (m t) -> p m t", t=P),
                                                 b_t[:, P - 1:nb * P:P].unsqueeze(2).to_broadcast([P, nb, P]),
                                                 b_t[:, 0:nb * P].rearrange("p (m t) -> p m t", t=P), ALU.subtract))
                    link(nc.vector.tensor_tensor(d2[:, nb * P:TP], b_t[:, TP - 1:TP].to_broadcast([P, PTAIL]),
                                                 b_t[:, nb * P:TP], ALU.subtract))
                    nc.vector.tensor_tensor(d2[:, TP:T].rearrange("p (b t) -> p b t", t=DT),
                                            b_t[:, TP + DT - 1:T:DT].unsqueeze(2).to_broadcast([P, DB, DT]),
                                            b_t[:, TP:T].rearrange("p (b t) -> p b t", t=DT), ALU.subtract).then_inc(wm_ready, 1)
                    dve.wait_ge(w_ready, u + 1)
                    nc.vector.tensor_tensor(xx[:, 0, :], k, d2, ALU.mult).then_inc(kx_ready, 1)
                    dve.wait_ge(e1_ready, u + 1)
                else:
                    for c, (t0, tw) in enumerate(CH):
                        dve.wait_ge(bc_done, 3 * h + c + 1)
                        src = ps_a[:, 0].rearrange("p a b -> p (a b)")
                        full = tw // P * P
                        r = nc.vector.tensor_tensor(dd[:, 0, t0:t0 + full].rearrange("p (m t) -> p m t", t=P),
                                                    src[:, 0:full].rearrange("p (m t) -> p m t", t=P),
                                                    negm[:].unsqueeze(1).to_broadcast([P, full // P, P]), ALU.add)
                        if full < tw:
                            link(r)
                            r = nc.vector.tensor_tensor(dd[0:LAST, 0, t0 + full:T], src[0:LAST, full:tw], negtail[:], ALU.add)
                        r.then_inc(bc_d, 1)
                        dve.wait_ge(bc_d, 3 * h + c + 1)
                    dve.wait_ge(wm_ready, H + h + 1)
                    base = 2 * (LEVELS + 1) * H
                    for g in range(2):
                        dve.wait_ge(a_done, base + 2 * h + g + 1)
                        nc.vector.tensor_tensor(at[:, 4 * g:4 * g + 4, :],
                                                dd[:, 0, 4 * g * P:(4 * g + 4) * P].rearrange("p (m t) -> p m t", t=P),
                                                ps_a[:, g], ALU.mult).then_inc(a_used, 1)
                    dve.wait_ge(at_done, NTAIL * H + h + 1)
                    nc.vector.tensor_tensor(at[0:LAST, NT - 1, 0:LAST], dd[0:LAST, 0, (NT - 1) * P:T],
                                            ps_at[0:LAST, 0:LAST], ALU.mult).then_inc(at_used, 1)
                    dve.wait_ge(a_used, base + 2 * h + 2)
                    dve.wait_ge(at_used, NTAIL * H + h + 1)
                    dve.wait_ge(bc_a, 3 * h + 3)
                dec = st[:, 3:5, :].rearrange("p a b -> p (a b)")
                nb = NT - 1
                link(nc.vector.tensor_copy(dec[:, 0:nb], e1[:, P - 1:nb * P:P]))
                link(nc.vector.tensor_copy(dec[:, nb:nb + 1], e1[:, TP - 1:TP]))
                link(nc.vector.tensor_copy(dec[:, nb + 1:nb + 1 + DB], e1[:, TP + DT - 1:T:DT]))
                link(nc.vector.tensor_tensor(e1[:], e1[:], q, ALU.mult))
                link(nc.vector.tensor_tensor(qx[:], e1[:, nb * P:T].unsqueeze(1).to_broadcast([P, DB + 1, LAST]), col_mask[:], ALU.mult))
                dve.wait_ge(kt_used, KG * (u + 1))
                nc.vector.tensor_tensor(khx[:], kh[0:LAST, NT - 1, :].unsqueeze(1).to_broadcast([LAST, DB + 1, P]),
                                        row_mask[:].unsqueeze(2).to_broadcast([LAST, DB + 1, P]), ALU.mult).then_inc(khx_ready, 1)
                e = P if u < H else E
                dve.wait_ge(s_ld, 16 * (u + 1))
                if u:
                    dve.wait_ge(s_out, 32 * u)
                for gi, (i0, nn) in enumerate(UG):
                    dve.wait_ge(u_done, len(UG) * u + gi + 1)
                    for i in range(i0, i0 + nn):
                        src = s_pr[:, i, 0:e] if i < NT else s_in[:, i - NT, 0:e]
                        dst = s_pr[:, i + 1, 0:e] if i < NT else s_new[:, i - NT, 0:e]
                        ins = nc.vector.scalar_tensor_tensor(out=dst, in0=src, scalar=dec[:, i:i + 1],
                                                             in1=ps_u[:, (i - i0) * E:(i - i0) * E + e],
                                                             op0=ALU.mult, op1=ALU.add)
                        if i < i0 + nn - 1:
                            link(ins)
                    ins.then_inc(u_used, 1)
                    dve.wait_ge(u_used, len(UG) * u + gi + 1)
                dve.wait_ge(sq_ready, u + 1)
                link(nc.vector.tensor_reduce(st[:, 0, :], sq[:], AX.X, ALU.add))
                if u >= H:
                    den = o_sb[:, :, P:E].rearrange("p m o -> p (m o)")
                    link(nc.vector.scalar_tensor_tensor(out=st[:, 5, :], in0=den, scalar=-1.0, in1=den, op0=ALU.mult, op1=ALU.max))
                    link(nc.vector.tensor_tensor(st[:, 5, :], st[:, 5, :], cols[:, :, 2, h], ALU.max))
                    link(nc.vector.reciprocal(st[:, 6, :], st[:, 5, :]))
                    link(nc.vector.tensor_tensor(st[:, 0, :], st[:, 0, :], st[:, 6, :], ALU.mult))
                    link(nc.vector.tensor_tensor(st[:, 0, :], st[:, 0, :], st[:, 6, :], ALU.mult))
                nc.vector.tensor_scalar(st[:, 1, :], st[:, 0, :], 1.0 / P, EPS, ALU.mult, ALU.add).then_inc(std_in, 1)
                dve.wait_ge(std_out, u + 1)
                link(nc.vector.reciprocal(st[:, 7, :], st[:, 2, :]))
                if u >= H:
                    link(nc.vector.tensor_tensor(st[:, 7, :], st[:, 7, :], st[:, 6, :], ALU.mult))
                link(nc.vector.tensor_tensor(sq[:], o_sb[:, :, 0:P], st[:, 7, :].unsqueeze(2).to_broadcast([P, NT, P]), ALU.mult))
                nc.vector.tensor_tensor(sq[:], sq[:], vg[:, u % 2, :, E:E + P], ALU.mult).then_inc(y_ready, 1)
                dve.wait_ge(yt_done, KG * (u + 1))
                nc.vector.tensor_copy(st[:, 0, :], st[:, 7, :]).then_inc(dve_unit, 1)
                dve.wait_ge(dve_unit, u + 1)


GW = TP + 2 + DB * (DT + 2)


def ffn_up(nc, tag, h_t, a_t, w_up, conv, conv_state, conv_out):
    with ExitStack() as ctx:
        def sb(name, shape, dt=F32):
            return ctx.enter_context(nc.sbuf_tensor(f"{tag}_{name}", shape, dt))

        used = []

        def sem(name):
            used.append(ctx.enter_context(nc.semaphore(f"{tag}_{name}")))
            return used[-1]

        w_sb = sb("w", [P, 2, KD, 2, P])
        gate = sb("gate", [P, 2, GW])
        cv = sb("cv", [P, 2, GW])
        cw = sb("cw", [P, NF * 4])
        cb = sb("cb", [P, 2, 4])
        cst = sb("cst", [P, NF * DB * 2])
        ost = sb("ost", [P, NF * (DB + 1) * 2])
        ps = ctx.enter_context(nc.psum_tensor(f"{tag}_ps", [P, 3, 2, 512], F32))
        w_in = [sem("w_in0"), sem("w_in1")]
        c_in, zeroed = sem("c_in"), sem("zeroed")
        prod_done = sem("prod_done")
        gate_out = sem("gate_out")
        coef_in = sem("coef_in")
        past_in = sem("past_in")
        conv_done = sem("conv_done")
        silu_done = sem("silu_done")
        a_done = sem("a_done")
        kept = sem("kept")
        taps = sem("taps")
        stored = sem("stored")
        ctx.callback(clear_semaphores, nc, used)
        block = ctx.enter_context(nc.Block())
        STEPS = NF // 2

        @block.sync
        def _(sp):
            sp.dma_start(cw[:], conv).then_inc(c_in, 16)
            sp.dma_start(cst[:], conv_state).then_inc(c_in, 16)
            for s in range(2):
                sp.dma_start(w_sb[:, s], w_up[s * P:(s + 1) * P, :]).then_inc(w_in[s], 16)
            with sp.Fori(0, STEPS - 1) as i:
                for s in range(2):
                    sp.wait_ge(prod_done, 6 * i + 3 * (s + 1))
                    sp.dma_start(w_sb[:, s], w_up[bass.ds((2 * i + 2 + s) * P, P), :]).then_inc(w_in[s], 16)
            sp.wait_ge(kept, 2 * NF)
            sp.dma_start(conv_out, ost[:]).then_inc(stored, 16)
            sp.wait_ge(stored, 16)

        @block.tensor
        def _(pe):
            def one(j, w_value, free):
                for c, (t0, tw) in enumerate(CH):
                    if c == 0:
                        pe.wait_ge(w_in[j], w_value)
                    if free is not None:
                        pe.wait_ge(a_done, free + c)
                    for two in range(2):
                        for k in range(KD):
                            mm = pe.matmul(ps[:, c, two, 0:tw], w_sb[:, j, k, two, :], h_t[:, k, t0:t0 + tw],
                                           start=(k == 0), stop=(k == KD - 1))
                    mm.then_inc(prod_done, 1)

            one(0, 16, None)
            one(1, 16, 1)
            with pe.Fori(1, STEPS) as i:
                for s in range(2):
                    one(s, 16 * i + 16, 6 * i + 3 * s - 2)

        @block.gpsimd
        def _(pool):
            nc.gpsimd.memset(gate[:], 0.0).then_inc(zeroed, 1)

        @block.scalar
        def _(act):
            act.wait_ge(zeroed, 1)

            def take(s, c, n_prod, n_free):
                t0, tw = CH[c]
                act.wait_ge(prod_done, n_prod)
                if n_free is not None and c == 0:
                    act.wait_ge(conv_done, n_free)
                if n_free is not None and c == 2:
                    act.wait_ge(kept, n_free_kept[0])
                wp = min(tw, TP - t0)
                ins = nc.scalar.activation(gate[:, s, 2 + t0:2 + t0 + wp], ps[:, c, 0, 0:wp], ACT.Copy)
                if wp < tw:
                    ins = nc.scalar.activation(gate[:, s, TP + 2:].rearrange("p (b t) -> p b t", t=DT + 2)[:, :, 2:],
                                               ps[:, c, 0, wp:tw].rearrange("p (b t) -> p b t", t=DT), ACT.Copy)
                ins.then_inc(gate_out, 1)

            def silu(s, c, n):
                t0 = CH[c][0]
                w = CH[c][1] if c < 2 else GW - 2 - t0
                act.wait_ge(conv_done, n)
                nc.scalar.activation(cv[:, s, t0:t0 + w], cv[:, s, t0:t0 + w], ACT.Silu,
                                     bias=cb[:, s, 3:4]).then_inc(silu_done, 1)

            n_free_kept = [None]
            for s in range(2):
                for c in range(3):
                    take(s, c, 3 * s + c + 1, None)
                    silu(s, c, 3 * s + c + 1)
            with act.Fori(1, STEPS) as i:
                for s in range(2):
                    for c in range(3):
                        n_free_kept[0] = 4 * i + 2 * s - 2
                        take(s, c, 6 * i + 3 * s + c + 1, 6 * i + 3 * s - 3)
                        silu(s, c, 6 * i + 3 * s + c + 1)

        @block.vector
        def _(dve):
            dve.wait_ge(c_in, 32)
            dve.wait_ge(zeroed, 1)

            def copy(dst, src):
                return nc.vector.tensor_scalar(dst, src, 1.0, None, ALU.mult)

            def chunk(j, s, c, n):
                t0 = CH[c][0]
                w = CH[c][1] if c < 2 else GW - 2 - t0
                if c == 0:
                    copy(cb[:, s, :], cw[:, bass.ds(j * 4, 4)]).then_inc(coef_in, 1)
                    copy(gate[:, s, TP + 2:].rearrange("p (b t) -> p b t", t=DT + 2)[:, :, 0:2],
                         cst[:, bass.ds(j * DB * 2, DB * 2)].rearrange("p (b t) -> p b t", t=2)).then_inc(past_in, 1)
                    dve.wait_ge(coef_in, j + 1)
                dve.wait_ge(gate_out, n + 1)
                if c == 2:
                    dve.wait_ge(past_in, j + 1)
                    copy(ost[:, bass.ds(j * (DB + 1) * 2, 2)], gate[:, s, TP:TP + 2]).then_inc(kept, 1)
                    copy(ost[:, bass.ds(j * (DB + 1) * 2 + 2, DB * 2)].rearrange("p (b t) -> p b t", t=2),
                         gate[:, s, TP + 2:].rearrange("p (b t) -> p b t", t=DT + 2)[:, :, DT:]).then_inc(kept, 1)
                out = cv[:, s, t0:t0 + w]
                nc.vector.tensor_scalar(out, gate[:, s, t0 + 2:t0 + 2 + w], cb[:, s, 2:3], None,
                                        ALU.mult).then_inc(taps, 1)
                dve.wait_ge(taps, 2 * n + 1)
                nc.vector.scalar_tensor_tensor(out=out, in0=gate[:, s, t0 + 1:t0 + 1 + w], scalar=cb[:, s, 1:2],
                                               in1=out, op0=ALU.mult, op1=ALU.add).then_inc(taps, 1)
                dve.wait_ge(taps, 2 * n + 2)
                nc.vector.scalar_tensor_tensor(out=out, in0=gate[:, s, t0:t0 + w], scalar=cb[:, s, 0:1],
                                               in1=out, op0=ALU.mult, op1=ALU.add).then_inc(conv_done, 1)
                dve.wait_ge(silu_done, n + 1)
                wp = min(CH[c][1], TP - t0)
                ins = nc.vector.tensor_tensor(a_t[:, bass.ds(j * T + t0, wp)], cv[:, s, t0:t0 + wp], ps[:, c, 1, 0:wp], ALU.mult)
                if c == 2:
                    ins = nc.vector.tensor_tensor(a_t[:, bass.ds(j * T + TP, TS)].rearrange("p (b t) -> p b t", t=DT),
                                                  cv[:, s, TP + 2:].rearrange("p (b t) -> p b t", t=DT + 2)[:, :, 0:DT],
                                                  ps[:, c, 1, wp:wp + TS].rearrange("p (b t) -> p b t", t=DT), ALU.mult)
                ins.then_inc(a_done, 1)

            with dve.Fori(0, STEPS) as i:
                for s in range(2):
                    for c in range(3):
                        chunk(2 * i + s, s, c, 6 * i + 3 * s + c)


LAM_INIT = 0.8 - 0.6 * math.exp(-0.3)
KL = LAST


def att_project(nc, const, h_t, w_att, w_att_i, qc_t, kc_t, v_c, qd_t, kd_t, v_d, qi_t, ki_t, w_i, outs):
    ident = const["ident"]
    rope = const["rope"]
    with ExitStack() as ctx:
        def sb(name, shape):
            return ctx.enter_context(nc.sbuf_tensor(f"p_{name}", shape, F32))

        used = []

        def sem(name):
            used.append(ctx.enter_context(nc.semaphore(f"p_{name}")))
            return used[-1]

        NR, NP_ = 4, 4
        w_sb = sb("w", [P, 2, KD, 512])
        w_si = sb("wi", [P, KD, 68])
        row = sb("row", [P, NR, 512])
        t1 = sb("t1", [P, 256])
        t2 = sb("t2", [P, 256])
        ps = ctx.enter_context(nc.psum_tensor("p_ps", [P, NP_, 512], F32))
        ps_t = ctx.enter_context(nc.psum_tensor("p_pst", [P, 4, 4, P], F32))
        w_in = [sem("w_in0"), sem("w_in1")]
        wi_in = sem("wi_in")
        prod, taken, chain, rotated, turned, placed, done_v = (
            sem(x) for x in ("prod", "taken", "chain", "rotated", "turned", "placed", "done_v"))
        stored = [sem(f"stored{i}") for i in range(NR)]
        ctx.callback(clear_semaphores, nc, used)
        block = ctx.enter_context(nc.Block())
        NGR = 6
        items = [(g, m) for g in range(NGR) for m in range(NT)]
        rot = {0: [(0, 8, 64, 8, 0)], 1: [(0, 8, 64, 8, 0)], 2: [], 3: [(0, 4, 128, 16, 8)],
               4: [(0, 1, 128, 16, 8), (256, 4, 64, 8, 0)], 5: [(0, 1, 64, 8, 0)]}
        kc_o, vc_o, kd_o, vd_o, ki_o = outs

        def stores(g, m):
            r = rows_of(m)
            rr = slice(m * P, m * P + r)
            return {1: [(kc_o[rr, :], 0, 512)], 2: [(vc_o[rr, :], 0, 512)],
                    4: [(kd_o[rr, :], 0, P), (vd_o[rr, :], P, 2 * P)], 5: [(ki_o[rr, :], 0, 64)]}.get(g, [])

        def stored_upto(n):
            return 16 * sum(len(stores(*items[i])) for i in range(n % NR, n + 1, NR))

        turns = {0: 4, 1: 4, 2: 0, 3: 4, 4: 3, 5: 1}
        with_turn = [n for n, (g, m) in enumerate(items) if turns[g]]
        turn_no = {n: i for i, n in enumerate(with_turn)}

        def put(sp, n):
            g, m = items[n]
            if stores(g, m):
                sp.wait_ge(rotated, n + 1)
            for dst, c0, c1 in stores(g, m):
                sp.dma_start(dst, row[0:rows_of(m), n % NR, c0:c1]).then_inc(stored[n % NR], 16)

        @block.sync
        def _(sp):
            for g in range(NGR):
                if g < 5:
                    if g >= 2:
                        sp.wait_ge(prod, NT * (g - 1))
                    sp.dma_start(w_sb[:, g % 2], w_att[g]).then_inc(w_in[g % 2], 16)
                if g == 0:
                    sp.dma_start(w_si[:], w_att_i).then_inc(wi_in, 16)
                if g == 0:
                    continue
                for m in range(NT):
                    n = (g - 1) * NT + m
                    put(sp, n)
            for m in range(NT):
                put(sp, (NGR - 1) * NT + m)
            for i in range(NR):
                sp.wait_ge(stored[i], stored_upto(len(items) - 1 - (len(items) - 1 - i) % NR))

        @block.tensor
        def _(pe):
            def turn(n):
                g, m = items[n]
                if not turns[g]:
                    return
                r = rows_of(m)
                t = turn_no[n]
                pe.wait_ge(rotated, n + 1)
                if t >= 4:
                    pe.wait_ge(placed, t - 3)
                c0s = {4: [0, 256, 384], 5: [0]}.get(g, [0, 128, 256, 384])
                for i, c0 in enumerate(c0s):
                    x = pe.transpose(ps_t[:, t % 4, i, 0:r], row[0:r, n % NR, c0:c0 + P], ident[0:r, 0:r])
                x.then_inc(turned, 1)

            for n, (g, m) in enumerate(items):
                r = rows_of(m)
                if m == 0:
                    if g < 5:
                        pe.wait_ge(w_in[g % 2], 16 * (g // 2 + 1))
                    else:
                        pe.wait_ge(wi_in, 16)
                if n >= NP_:
                    pe.wait_ge(taken, n - NP_ + 1)
                for k in range(KD):
                    w = w_sb[:, g % 2, k, :] if g < 5 else w_si[:, k, :]
                    mm = pe.matmul(ps[0:r, n % NP_, 0:w.shape[-1]], h_t[:, k, m * P:m * P + r], w,
                                   start=(k == 0), stop=(k == KD - 1))
                mm.then_inc(prod, 1)
                if n >= 2:
                    turn(n - 2)
            turn(len(items) - 2)
            turn(len(items) - 1)

        @block.scalar
        def _(act):
            def place(n):
                g, m = items[n]
                if not turns[g]:
                    return
                r = rows_of(m)
                t = turn_no[n]
                act.wait_ge(turned, t + 1)
                c = slice(m * P, m * P + r)
                if g in (0, 1, 3):
                    dst = {0: qc_t, 1: kc_t, 3: qd_t}[g]
                    ins = nc.scalar.activation(dst[:, :, c], ps_t[:, t % 4, :, 0:r], ACT.Copy)
                elif g == 4:
                    nc.scalar.activation(kd_t[:, c], ps_t[:, t % 4, 0, 0:r], ACT.Copy)
                    ins = nc.scalar.activation(qi_t[:, :, c], ps_t[:, t % 4, 1:3, 0:r], ACT.Copy)
                else:
                    ins = nc.scalar.activation(ki_t[:, c], ps_t[:, t % 4, 0, 0:r], ACT.Copy)
                ins.then_inc(placed, 1)

            for n, (g, m) in enumerate(items):
                r = rows_of(m)
                w = 512 if g < 5 else 68
                act.wait_ge(prod, n + 1)
                if n >= NR:
                    if stored_upto(n - NR):
                        act.wait_ge(stored[n % NR], stored_upto(n - NR))
                    act.wait_ge(done_v, n - NR + 1)
                    if n - NR in turn_no:
                        act.wait_ge(turned, turn_no[n - NR] + 1)
                nc.scalar.activation(row[0:r, n % NR, 0:w], ps[0:r, n % NP_, 0:w], ACT.Copy).then_inc(taken, 1)
                if n >= 3:
                    place(n - 3)
            for n in range(len(items) - 3, len(items)):
                place(n)

        @block.vector
        def _(dve):
            cnt = [0]

            def link(ins):
                cnt[0] += 1
                ins.then_inc(chain, 1)
                dve.wait_ge(chain, cnt[0])

            for n, (g, m) in enumerate(items):
                r = rows_of(m)
                x = row[0:r, n % NR, :]
                dve.wait_ge(taken, n + 1)
                for c0, nh, d, half, tc in rot[g]:
                    v = x[:, c0:c0 + nh * d].rearrange("p (h d) -> p h d", d=d)[:, :, 0:2 * half] \
                        .rearrange("p h (two e) -> p h two e", two=2)
                    a = t1[0:r, 0:nh * 2 * half].rearrange("p (h two e) -> p h two e", two=2, e=half)
                    b = t2[0:r, 0:nh * 2 * half].rearrange("p (h two e) -> p h two e", two=2, e=half)
                    cos = rope[0:r, m, 0, tc:tc + half].unsqueeze(1).unsqueeze(1).to_broadcast([r, nh, 2, half])
                    sin = rope[0:r, m, 1, tc:tc + half].unsqueeze(1).unsqueeze(1).to_broadcast([r, nh, 2, half])
                    link(nc.vector.tensor_tensor(a, v, cos, ALU.mult))
                    link(nc.vector.tensor_tensor(b, v, sin, ALU.mult))
                    link(nc.vector.tensor_tensor(v[:, :, 0], a[:, :, 0], b[:, :, 1], ALU.subtract))
                    link(nc.vector.tensor_tensor(v[:, :, 1], b[:, :, 0], a[:, :, 1], ALU.add))
                if g == 5:
                    link(nc.vector.tensor_scalar(w_i[0:r, m, :], x[:, 64:68], H ** -0.5, None, ALU.mult))
                    link(nc.vector.tensor_copy(x[:, 64:P], x[:, 0:64]))
                nc.vector.tensor_copy(t1[0:1, 0:1], x[0:1, 0:1]).then_inc(rotated, 1)
                if g == 2:
                    nc.vector.tensor_copy(v_c[0:r, m, :], x).then_inc(done_v, 1)
                elif g == 4:
                    nc.vector.tensor_copy(v_d[0:r, m, :], x[:, P:2 * P]).then_inc(done_v, 1)
                else:
                    nc.vector.tensor_copy(t2[0:1, 0:1], x[0:1, 0:1]).then_inc(done_v, 1)
                dve.wait_ge(done_v, n + 1)
                dve.wait_ge(rotated, n + 1)


def prompt_attention(nc, const, qc_t, kc_t, v_c, qd_t, kd_t, v_d, qi_t, ki_t, w_i, o_t, neg_lam, diff_lambda, g_diff):
    ident, neg = const["ident"], const["neg_future"]
    with ExitStack() as ctx:
        def sb(name, shape):
            return ctx.enter_context(nc.sbuf_tensor(f"a_{name}", shape, F32))

        used = []

        def sem(name):
            used.append(ctx.enter_context(nc.semaphore(f"a_{name}")))
            return used[-1]

        lamp = sb("lamp", [P, 4, DC])
        lt = sb("lt", [P, 2, DC])
        le = sb("le", [P, 4])
        gd = sb("gd", [P, P])
        p_sb = sb("p", [P, 4, TP])
        score = sb("score", [P, TP])
        relu = sb("relu", [P, 2, TP])
        top = sb("top", [P, 8])
        stat = sb("stat", [P, 4, 8])
        a_t = sb("a_t", [P, 2, NT, P])
        o_sb = sb("o", [P, 2, 8, P])
        osq = sb("osq", [P, 4, P])
        ost = sb("ost", [P, 4, 4])
        ps_s = ctx.enter_context(nc.psum_tensor("a_pss", [P, 4 * 512], F32))
        ps_t = ctx.enter_context(nc.psum_tensor("a_pst", [P, 2, 4, P], F32))
        ps_o = ctx.enter_context(nc.psum_tensor("a_pso", [P, 2, 512], F32))
        loaded, lam_sum, lam_exp, chain, achain = (sem(x) for x in ("loaded", "lam_sum", "lam_exp", "chain", "achain"))
        s_done, max_done, exp_done, relu_done, relu_used, picked = (
            sem(x) for x in ("s_done", "max_done", "exp_done", "relu_done", "relu_used", "picked"))
        mixed, turned, placed, o_done, o_read, osq_done, ovar, ostd, normed = (
            sem(x) for x in ("mixed", "turned", "placed", "o_done", "o_read", "osq_done", "ovar", "ostd", "normed"))
        ctx.callback(clear_semaphores, nc, used)
        block = ctx.enter_context(nc.Block())

        def qrows(m):
            return P if m < NT - 1 else PTAIL

        def width(m):
            return min((m + 1) * P, TP)

        def indexed(m):
            return width(m) > TOPK

        units, softmaxes, relus, heads = [], [], [], []
        for m in range(NT):
            if indexed(m):
                for h in range(H):
                    units.append(("index", m, h, 0))
                    relus.append(len(units) - 1)
            for h in range(H):
                for c in range(2):
                    units.append(("diff", m, h, c))
                    softmaxes.append(len(units) - 1)
            for h in range(H):
                units.append(("dsa", m, h, 0))
                softmaxes.append(len(units) - 1)
        u_no = {u: n for n, u in enumerate(units)}
        k_no = {u: n for n, u in enumerate(softmaxes)}
        r_no = {u: n for n, u in enumerate(relus)}
        turn_list = []
        for m in range(NT):
            for hd in range(8):
                nk = -(-width(m) // P)
                for b0 in range(0, nk, 4):
                    turn_list.append((m, hd, b0, min(4, nk - b0)))
                if hd == 7:
                    turn_list += [(m, "out", 0, 4), (m, "out", 4, 4)]
        t_no = {t[:3]: n for n, t in enumerate(turn_list)}

        def region(n):
            m = units[n][1]
            o = (n % 2) * 1024 if m < NT - 1 else 0
            return o, width(m)

        @block.sync
        def _(sp):
            sp.dma_start(lamp[:], diff_lambda.partition_broadcast(P)).then_inc(loaded, 16)
            sp.dma_start(gd[:], g_diff.partition_broadcast(P)).then_inc(loaded, 16)
            sp.wait_ge(loaded, 32)

        @block.tensor
        def _(pe):
            def scores(n):
                kind, m, h, c = units[n]
                r, (o, w) = qrows(m), region(n)
                q = slice(m * P, m * P + r)
                last_tile = m == NT - 1
                if n >= 2:
                    old = n - 1 if last_tile else n - 2
                    if old in k_no:
                        pe.wait_ge(exp_done, k_no[old] + 1)
                    else:
                        pe.wait_ge(relu_done, r_no[old] + 1)
                mask = kind == "dsa" and indexed(m)
                d0 = w if mask or kind == "index" else m * P
                cuts = [(k0, min(512, d0 - k0)) for k0 in range(0, d0, 512)] + ([(d0, w - d0)] if d0 < w else [])
                for k0, kw in cuts:
                    out, k = ps_s[0:r, o + k0:o + k0 + kw], slice(k0, k0 + kw)
                    if kind == "dsa":
                        lhs, rhs = qd_t[:, h, q], kd_t[:, k]
                    elif kind == "diff":
                        lhs, rhs = qc_t[c * DC:(c + 1) * DC, h, q], kc_t[c * DC:(c + 1) * DC, h, k]
                    else:
                        p = slice((h % 2) * 64, (h % 2) * 64 + 64)
                        lhs, rhs = qi_t[p, h // 2, q], ki_t[p, k]
                    diag = k0 == d0
                    mm = pe.matmul(out, lhs, rhs, start=True, stop=not (mask or diag))
                    if mask or diag:
                        mm = pe.matmul(out, ident[0:r, 0:r], score[0:r, k] if mask else neg[0:r, 0:kw], start=False, stop=True)
                mm.then_inc(s_done, 1)

            def head_out(m, hd):
                r, j = qrows(m), 8 * m + hd
                k = k_no[u_no[("diff", m, hd, 1) if hd < 4 else ("dsa", m, hd - 4, 0)]]
                pe.wait_ge(mixed, j + 1)
                nk = -(-width(m) // P)
                for b0 in range(0, nk, 4):
                    t = t_no[(m, hd, b0)]
                    if t >= 2:
                        pe.wait_ge(placed, t - 1)
                    for b in range(b0, min(b0 + 4, nk)):
                        kw = min(P, width(m) - b * P)
                        x = pe.transpose(ps_t[0:kw, t % 2, b - b0, 0:r], p_sb[0:r, (k - (hd < 4)) % 4, b * P:b * P + kw],
                                         ident[0:r, 0:r])
                    x.then_inc(turned, 1)
                return j

            def values(m, hd):
                r, j = qrows(m), 8 * m + hd
                nk = -(-width(m) // P)
                pe.wait_ge(placed, t_no[(m, hd, (nk - 1) // 4 * 4)] + 1)
                if j >= 2:
                    pe.wait_ge(o_read, j - 1)
                for b in range(nk):
                    kw = min(P, width(m) - b * P)
                    v = v_c[0:kw, b, hd * P:(hd + 1) * P] if hd < 4 else v_d[0:kw, b, :]
                    mm = pe.matmul(ps_o[0:r, j % 2, 0:P], a_t[0:kw, j % 2, b, 0:r], v, start=(b == 0), stop=(b == nk - 1))
                mm.then_inc(o_done, 1)

            def outputs(m):
                r = qrows(m)
                pe.wait_ge(normed, m + 1)
                pe.wait_ge(o_read, 8 * m + 8)
                for i0 in (0, 4):
                    t = t_no[(m, "out", i0)]
                    pe.wait_ge(placed, t - 1)
                    for i in range(4):
                        x = pe.transpose(ps_t[:, t % 2, i, 0:r], o_sb[0:r, m % 2, i0 + i, :], ident[0:r, 0:r])
                    x.then_inc(turned, 1)

            for m in range(NT):
                if indexed(m):
                    for h in range(H):
                        scores(u_no[("index", m, h, 0)])
                for h in range(H):
                    for c in range(2):
                        scores(u_no[("diff", m, h, c)])
                    if h:
                        head_out(m, h - 1)
                        values(m, h - 1)
                head_out(m, 3)
                values(m, 3)
                if indexed(m):
                    pe.wait_ge(picked, sum(indexed(i) for i in range(m + 1)))
                for h in range(H):
                    scores(u_no[("dsa", m, h, 0)])
                    if h:
                        head_out(m, 3 + h)
                        values(m, 3 + h)
                head_out(m, 7)
                values(m, 7)
                outputs(m)

        @block.scalar
        def _(act):
            cnt = [0]

            def link(ins):
                cnt[0] += 1
                ins.then_inc(achain, 1)
                act.wait_ge(achain, cnt[0])

            act.wait_ge(lam_sum, 1)
            nc.scalar.activation(le[:, 2:4], le[:, 0:2], ACT.Exp).then_inc(lam_exp, 1)

            def softmax(n):
                kind, m, h, c = units[n]
                k = k_no[n]
                r, (o, w) = qrows(m), region(n)
                act.wait_ge(max_done, k + 1)
                if k >= 4:
                    old = units[softmaxes[k - 4]]
                    hd = old[2] + (4 if old[0] == "dsa" else 0)
                    nk = -(-width(old[1]) // P)
                    act.wait_ge(turned, t_no[(old[1], hd, (nk - 1) // 4 * 4)] + 1)
                scale = DC ** -0.5 if kind == "diff" else float(P) ** -0.5
                nc.scalar.activation(p_sb[0:r, k % 4, 0:w], ps_s[0:r, o:o + w], ACT.Exp, bias=stat[0:r, k % 4, 1:2],
                                     scale=scale, accum_out=stat[0:r, k % 4, 2:3]).then_inc(exp_done, 1)

            def index(n):
                kind, m, h, c = units[n]
                r, (o, w) = qrows(m), region(n)
                i = r_no[n]
                act.wait_ge(s_done, n + 1)
                if i >= 2:
                    act.wait_ge(relu_used, i - 1)
                nc.scalar.activation(relu[0:r, i % 2, 0:w], ps_s[0:r, o:o + w], ACT.Relu, scale=64 ** -0.5).then_inc(relu_done, 1)

            def head_out(m, hd):
                r, j = qrows(m), 8 * m + hd
                nk = -(-width(m) // P)
                if j >= 2:
                    act.wait_ge(o_done, j - 1)
                for b0 in range(0, nk, 4):
                    n = min(4, nk - b0)
                    act.wait_ge(turned, t_no[(m, hd, b0)] + 1)
                    t = t_no[(m, hd, b0)]
                    kw = min(P, width(m) - b0 * P)
                    nc.scalar.activation(a_t[0:kw, j % 2, b0:b0 + n, 0:r], ps_t[0:kw, t % 2, 0:n, 0:r], ACT.Copy).then_inc(placed, 1)

            def values(m, hd):
                r, j = qrows(m), 8 * m + hd
                k = k_no[u_no[("diff", m, hd, 0) if hd < 4 else ("dsa", m, hd - 4, 0)]]
                act.wait_ge(o_done, j + 1)
                nc.scalar.activation(o_sb[0:r, m % 2, hd, :], ps_o[0:r, j % 2, 0:P], ACT.Copy,
                                     scale=stat[0:r, k % 4, 3:4]).then_inc(o_read, 1)

            for m in range(NT):
                r = qrows(m)
                if indexed(m):
                    for h in range(H):
                        index(u_no[("index", m, h, 0)])
                for h in range(H):
                    for c in range(2):
                        softmax(u_no[("diff", m, h, c)])
                    if h:
                        head_out(m, h - 1)
                        values(m, h - 1)
                head_out(m, 3)
                values(m, 3)
                act.wait_ge(o_read, 8 * m + 4)
                if m:
                    act.wait_ge(normed, m)
                nc.scalar.activation(osq[0:r], o_sb[0:r, m % 2, 0:4, :], ACT.Square).then_inc(osq_done, 1)
                for h in range(H):
                    softmax(u_no[("dsa", m, h, 0)])
                    if h:
                        head_out(m, 3 + h)
                        values(m, 3 + h)
                head_out(m, 7)
                values(m, 7)
                act.wait_ge(ovar, m + 1)
                nc.scalar.activation(ost[0:r, 2, :], ost[0:r, 1, :], ACT.Sqrt).then_inc(ostd, 1)
                for i0 in (0, 4):
                    t = t_no[(m, "out", i0)]
                    act.wait_ge(turned, t + 1)
                    nc.scalar.activation(o_t[:, i0:i0 + 4, m * P:m * P + r], ps_t[:, t % 2, :, 0:r], ACT.Copy).then_inc(placed, 1)

        @block.vector
        def _(dve):
            cnt = [0]

            def link(ins):
                cnt[0] += 1
                ins.then_inc(chain, 1)
                dve.wait_ge(chain, cnt[0])

            dve.wait_ge(loaded, 32)
            lv = lamp[:].rearrange("p (two qk) d -> p two qk d", two=2)
            link(nc.vector.tensor_tensor(lt[:], lv[:, :, 0, :], lv[:, :, 1, :], ALU.mult))
            nc.vector.tensor_reduce(le[:, 0:2], lt[:], AX.X, ALU.add).then_inc(lam_sum, 1)
            dve.wait_ge(lam_exp, 1)
            link(nc.vector.tensor_tensor(neg_lam[:], le[:, 3:4], le[:, 2:3], ALU.subtract))
            link(nc.vector.tensor_scalar(neg_lam[:], neg_lam[:], LAM_INIT, None, ALU.subtract))
            link(nc.vector.tensor_scalar(gd[:], gd[:], 1.0 - LAM_INIT, None, ALU.mult))

            def maximum(n):
                kind, m, h, c = units[n]
                k = k_no[n]
                r, (o, w) = qrows(m), region(n)
                scale = DC ** -0.5 if kind == "diff" else float(P) ** -0.5
                dve.wait_ge(s_done, n + 1)
                if k >= 4:
                    old = units[softmaxes[k - 4]]
                    dve.wait_ge(o_read, 8 * old[1] + old[2] + (4 if old[0] == "dsa" else 0) + 1)
                link(nc.vector.tensor_reduce(stat[0:r, k % 4, 0:1], ps_s[0:r, o:o + w], AX.X, ALU.max))
                nc.vector.tensor_scalar(stat[0:r, k % 4, 1:2], stat[0:r, k % 4, 0:1], -scale, None, ALU.mult).then_inc(max_done, 1)

            def mix(m, hd):
                r, w, j = qrows(m), width(m), 8 * m + hd
                k = k_no[u_no[("diff", m, hd, 0) if hd < 4 else ("dsa", m, hd - 4, 0)]]
                s0 = stat[0:r, k % 4]
                dve.wait_ge(exp_done, k + 1)
                if hd >= 4:
                    nc.vector.reciprocal(s0[:, 3:4], s0[:, 2:3]).then_inc(mixed, 1)
                    dve.wait_ge(mixed, j + 1)
                    return
                s1 = stat[0:r, (k + 1) % 4]
                link(nc.vector.reciprocal(s0[:, 3:4], s0[:, 2:3]))
                dve.wait_ge(exp_done, k + 2)
                link(nc.vector.reciprocal(s1[:, 3:4], s1[:, 2:3]))
                link(nc.vector.tensor_tensor(s1[:, 4:5], s1[:, 3:4], s0[:, 2:3], ALU.mult))
                link(nc.vector.tensor_tensor(s1[:, 5:6], s1[:, 4:5], neg_lam[0:r, :], ALU.mult))
                nc.vector.scalar_tensor_tensor(out=p_sb[0:r, k % 4, 0:w], in0=p_sb[0:r, (k + 1) % 4, 0:w],
                                               scalar=s1[:, 5:6], in1=p_sb[0:r, k % 4, 0:w],
                                               op0=ALU.mult, op1=ALU.add).then_inc(mixed, 1)
                dve.wait_ge(mixed, j + 1)

            n_picked = 0
            for m in range(NT):
                r, w = qrows(m), width(m)
                if indexed(m):
                    if m:
                        dve.wait_ge(s_done, u_no[("dsa", m - 1, H - 1, 0)] + 1)
                    for h in range(H):
                        i = r_no[u_no[("index", m, h, 0)]]
                        dve.wait_ge(relu_done, i + 1)
                        wh = w_i[0:r, m, h:h + 1]
                        if h == 0:
                            x = nc.vector.tensor_scalar(score[0:r, 0:w], relu[0:r, i % 2, 0:w], wh, None, ALU.mult)
                        else:
                            x = nc.vector.scalar_tensor_tensor(out=score[0:r, 0:w], in0=relu[0:r, i % 2, 0:w], scalar=wh,
                                                               in1=score[0:r, 0:w], op0=ALU.mult, op1=ALU.add)
                        x.then_inc(relu_used, 1)
                        dve.wait_ge(relu_used, i + 1)
                    link(nc.vector.tensor_tensor(score[0:r, m * P:w], score[0:r, m * P:w], neg[0:r, 0:w - m * P], ALU.add))
                for h in range(H):
                    for c in range(2):
                        maximum(u_no[("diff", m, h, c)])
                    mix(m, h)
                if indexed(m):
                    for _ in range(TOPK // 8):
                        link(nc.vector.max(top[0:r, :], score[0:r, 0:w]))
                        link(nc.vector.match_replace(score[0:r, 0:w], top[0:r, :], score[0:r, 0:w], PICKED))
                    link(nc.vector.tensor_scalar(score[0:r, 0:w], score[0:r, 0:w], PICKED, NEG, ALU.not_equal, ALU.mult))
                    nc.vector.tensor_tensor(score[0:r, m * P:w], score[0:r, m * P:w], neg[0:r, 0:w - m * P],
                                            ALU.add).then_inc(picked, 1)
                    n_picked += 1
                    dve.wait_ge(picked, n_picked)
                for h in range(H):
                    maximum(u_no[("dsa", m, h, 0)])
                    mix(m, 4 + h)
                dve.wait_ge(osq_done, m + 1)
                link(nc.vector.tensor_reduce(ost[0:r, 0, :], osq[0:r], AX.X, ALU.add))
                nc.vector.tensor_scalar(ost[0:r, 1, :], ost[0:r, 0, :], 1.0 / P, EPS, ALU.mult, ALU.add).then_inc(ovar, 1)
                dve.wait_ge(ostd, m + 1)
                link(nc.vector.reciprocal(ost[0:r, 3, :], ost[0:r, 2, :]))
                o = o_sb[0:r, m % 2, 0:4, :]
                link(nc.vector.tensor_tensor(o, o, ost[0:r, 3, :].unsqueeze(2).to_broadcast([r, 4, P]), ALU.mult))
                nc.vector.tensor_tensor(o, o, gd[0:r, :].unsqueeze(1).to_broadcast([r, 4, P]), ALU.mult).then_inc(normed, 1)
                dve.wait_ge(normed, m + 1)


def sample_attention(nc, const, a, qc_t, kc_t, v_c, qd_t, kd_t, v_d, qi_t, ki_t, w_i, o_t, neg_lam):
    ident = const["ident"]
    NKC = PAST + KL
    NB = NPG + 1
    QP = 4
    NQ = NPG // QP
    with ExitStack() as ctx:
        def sb(name, shape, dt=F32):
            return ctx.enter_context(nc.sbuf_tensor(f"s_{name}", shape, dt))

        used = []

        def sem(name):
            used.append(ctx.enter_context(nc.semaphore(f"s_{name}")))
            return used[-1]

        RK = 2
        tbl = sb("tbl", [1, DB * NPG], I32)
        k_ring = sb("k_ring", [P, RK, QP, H * P])
        v_ring = sb("v_ring", [P, RK, QP, H * P])
        qx = sb("qx", [P, DB, H, 32])
        qdx = sb("qdx", [P, DB, 32])
        qix = sb("qix", [P, DB, 32])
        sc = sb("sc", [2 * 16, NKC])
        p_sb = sb("p", [P, NKC])
        rl = sb("rl", [P, NKC])
        a_t = sb("a_t", [P, NB, 4, 32])
        os_c = rl[:, 0:2 * H * P].rearrange("p (g e) -> p g e", g=2)
        o_s = rl[0:TS, 2 * H * P:4 * H * P].rearrange("p (k e) -> p k e", k=2)
        os_d = sb("os_d", [P, 2, P])
        osq = sb("osq", [TS, H, P])
        ost = sb("ost", [TS, 4, H])
        gd = sb("gd", [TS, P])
        wsel = sb("wsel", [P, 2, TS])
        wrow = sb("wrow", [P, 2, H])
        wr1 = sb("wr1", [P, 2])
        top = sb("top", [TS, 8])
        st = sb("st", [P, 8])
        half_c = sb("half_c", [P, 2])
        ps_s = ctx.enter_context(nc.psum_tensor("s_pss", [P, 5 * 512], F32))
        ps_t = ctx.enter_context(nc.psum_tensor("s_pst", [P, 2, 4, P], F32))
        ps_o = ctx.enter_context(nc.psum_tensor("s_pso", [P, 512], F32))
        names = ("t_in", "zeroed", "q_ready", "w_ps", "wsel_ready", "chain", "achain", "s_done", "relu_done", "sc_ps", "sc_out",
                 "picked", "max_done", "exp_done", "scaled", "turned", "placed", "o_done", "o_read", "sel_done", "sel_read",
                 "osq_done", "ovar", "ostd", "normed", "o_turned", "o_placed", "k_used", "v_used", "c_in")
        S = {n: sem(n) for n in names}
        k_in = [sem(f"k_in{i}") for i in range(RK)]
        v_in = [sem(f"v_in{i}") for i in range(RK)]
        ctx.callback(clear_semaphores, nc, used)
        block = ctx.enter_context(nc.Block())
        k_loads = [("ik", b, c) for b in range(DB) for c in range(NQ)]
        v_loads = []
        for kind in ("c", "d"):
            for g in range(2):
                k_loads += [(kind + "k", 4 * g + j, c) for j in range(4) for c in range(NQ)]
                v_loads += [(kind + "v", 4 * g + j, c) for j in range(4) for c in range(NQ)]
        kn = {x: n for n, x in enumerate(k_loads)}
        vn = {x: n for n, x in enumerate(v_loads)}
        stages = [("c", 0), ("c", 1), ("d", 0), ("d", 1)]

        def fetch(eng, ring, sems, used, loads, pool):
            eng.wait_ge(S["t_in"], 16)
            for n, (kind, b, c) in enumerate(loads):
                if n >= RK:
                    eng.wait_ge(used, n - RK + 1)
                for i in range(QP):
                    e = b * NPG + c * QP + i
                    page = eng.value_load(tbl[0:1, e:e + 1], min_val=0, max_val=pool["ik"].shape[0] // 64 - 1)
                    if kind == "ik":
                        for hf in range(2):
                            eng.dma_start(ring[hf * 64:(hf + 1) * 64, n % RK, i, 0:P], pool[kind][bass.ds(page * 64, 64), :]) \
                                .then_inc(sems[n % RK], 16)
                    else:
                        w = H * P if kind[0] == "c" else P
                        eng.dma_start(ring[:, n % RK, i, 0:w], pool[kind][bass.ds(page * P, P), :]).then_inc(sems[n % RK], 16)

        def arrived(loads, n):
            return 16 * sum(QP * (2 if loads[i][0] == "ik" else 1) for i in range(n % RK, n + 1, RK))

        @block.sync
        def _(sp):
            sp.dma_start(tbl[:], a["pages"]).then_inc(S["t_in"], 16)
            sp.dma_start(gd[:], a["g_diff"].partition_broadcast(TS)).then_inc(S["c_in"], 16)
            fetch(sp, k_ring, k_in, S["k_used"], k_loads, {"ik": a["pool_ik"], "ck": a["pool_ck"], "dk": a["pool_dk"]})

        @block.gpsimd
        def _(pool):
            nc.gpsimd.memset(a_t[:], 0.0).then_inc(S["zeroed"], 1)
            fetch(pool, v_ring, v_in, S["v_used"], v_loads, {"ik": a["pool_ik"], "cv": a["pool_cv"], "dv": a["pool_dv"]})

        @block.tensor
        def _(pe):
            last = slice(PTAIL + (NT - 1) * P - PTAIL, T)

            pe.wait_ge(S["q_ready"], 1)
            for g in range(2):
                mm = pe.matmul(ps_o[:, g * H:(g + 1) * H], const["sel_tok"][:, g, :], w_i[0:LAST, NT - 1, :], start=True, stop=True)
            mm.then_inc(S["w_ps"], 1)

            def k_scores(kind, g, j, c, extra):
                b = 4 * g + j
                n = kn[(kind, b, c)]
                pe.wait_ge(k_in[n % RK], arrived(k_loads, n))
                out = ps_s[32 * j:32 * j + 32, c * 512:(c + 1) * 512].rearrange("r (i k) -> r i k", k=P)
                if kind == "ck":
                    for h in range(H):
                        mm = pe.matmul(out, qx[:, b, h, :], k_ring[:, n % RK, :, h * P:(h + 1) * P], start=(h == 0), stop=(h == H - 1))
                else:
                    q = qix if kind == "ik" else qdx
                    mm = pe.matmul(out, q[:, b, :], k_ring[:, n % RK, :, 0:P], start=not extra, stop=True, skip_group_check=extra)
                mm.then_inc(S["k_used"], 1)

            new = slice(PAST, NKC)
            for g in range(2):
                if g:
                    pe.wait_ge(S["relu_done"], g)
                for j in range(4):
                    for c in range(NQ):
                        k_scores("ik", g, j, c, False)
                    mm = pe.matmul(ps_s[32 * j:32 * j + 32, new], qix[:, 4 * g + j, :], ki_t[:, last], start=True, stop=True)
                mm.then_inc(S["s_done"], 1)
                pe.wait_ge(S["relu_done"], g + 1)
                pe.wait_ge(S["wsel_ready"], 1)
                if g == 0:
                    continue
                for k0 in range(0, NKC, 512):
                    kw = min(512, NKC - k0)
                    for gg, r in ((0, p_sb), (1, rl)):
                        mm = pe.matmul(ps_s[0:TS, k0:k0 + kw], wsel[:, gg, :], r[:, k0:k0 + kw], start=(gg == 0), stop=(gg == 1))
                mm.then_inc(S["sc_ps"], 1)

            for si, (kind, g) in enumerate(stages):
                if si == 0:
                    pe.wait_ge(S["sc_out"], 1)
                else:
                    pe.wait_ge(S["exp_done"], si)
                if kind == "d":
                    pe.wait_ge(S["picked"], 1)
                    for k0 in range(0, NKC, 512):
                        kw = min(512, NKC - k0)
                        pe.matmul(ps_s[:, k0:k0 + kw], const["sel_back"][:, g, :], sc[:, k0:k0 + kw],
                                  start=True, stop=False, skip_group_check=True)
                for j in range(4):
                    b = 4 * g + j
                    for c in range(NQ):
                        k_scores(kind + "k", g, j, c, kind == "d")
                    out = ps_s[32 * j:32 * j + 32, new]
                    if kind == "c":
                        for h in range(H):
                            pe.matmul(out, qx[:, b, h, :], kc_t[:, h, last], start=(h == 0), stop=False)
                        mm = pe.matmul(out, ident[0:32, 0:32], const["negs"][:, b, :], start=False, stop=True)
                    else:
                        mm = pe.matmul(out, qdx[:, b, :], kd_t[:, last], start=False, stop=True, skip_group_check=True)
                mm.then_inc(S["s_done"], 1)
                pe.wait_ge(S["scaled"], si + 1)
                for b0 in range(0, NB, 4):
                    t = 5 * si + b0 // 4
                    if t >= 2:
                        pe.wait_ge(S["placed"], t - 1)
                    for kb in range(b0, min(NB, b0 + 4)):
                        kw = min(P, NKC - kb * P)
                        x = pe.transpose(ps_t[0:kw, t % 2, kb - b0, :], p_sb[:, kb * P:kb * P + kw], ident[:])
                    x.then_inc(S["turned"], 1)
                pe.wait_ge(S["placed"], 5 * (si + 1))
                if si:
                    pe.wait_ge(S["o_read"], si)
                else:
                    pe.wait_ge(S["wsel_ready"], 1)
                e = H * P if kind == "c" else P
                for j in range(4):
                    b = 4 * g + j
                    for kb in range(NPG):
                        n = vn[(kind + "v", b, kb // QP)]
                        if kb % QP == 0:
                            pe.wait_ge(v_in[n % RK], arrived(v_loads, n))
                        mm = pe.matmul(ps_o[32 * j:32 * j + 32, 0:e], a_t[:, kb, j, :], v_ring[:, n % RK, kb % QP, 0:e],
                                       start=(kb == 0), stop=False)
                        if kb % QP == QP - 1:
                            mm.then_inc(S["v_used"], 1)
                    v = v_c if kind == "c" else v_d
                    mm = pe.matmul(ps_o[32 * j:32 * j + 32, 0:e], a_t[0:KL, NPG, j, :], v[0:KL, NT - 1, :], start=False, stop=True)
                mm.then_inc(S["o_done"], 1)

            pe.wait_ge(S["o_read"], 4)
            for i, o in enumerate((os_c, os_d)):
                for h in range(H):
                    for g in range(2):
                        src = o[:, g, h * P:(h + 1) * P] if i == 0 else o[:, g, :]
                        mm = pe.matmul(ps_s[0:TS, i * 512 + h * P:i * 512 + (h + 1) * P], const["sel"][:, g, h, :], src,
                                       start=(g == 0), stop=(g == 1))
            mm.then_inc(S["sel_done"], 1)
            pe.wait_ge(S["normed"], 1)
            for i in range(8):
                x = pe.transpose(ps_t[:, i // 4, i % 4, 0:TS], o_s[:, i // 4, (i % 4) * P:(i % 4 + 1) * P], ident[0:TS, 0:TS])
            x.then_inc(S["o_turned"], 1)

        @block.scalar
        def _(act):
            for g, dst in ((0, p_sb), (1, rl)):
                act.wait_ge(S["s_done"], g + 1)
                nc.scalar.activation(dst[:], ps_s[:, 0:NKC], ACT.Relu, scale=64 ** -0.5).then_inc(S["relu_done"], 1)
            act.wait_ge(S["sc_ps"], 1)
            for si, (kind, g) in enumerate(stages):
                act.wait_ge(S["max_done"], si + 1)
                if si:
                    act.wait_ge(S["turned"], 5 * si)
                scale = DC ** -0.5 if kind == "c" else float(P) ** -0.5
                nc.scalar.activation(p_sb[:], ps_s[:, 0:NKC], ACT.Exp, bias=st[:, 1:2], scale=scale,
                                     accum_out=st[:, 2:3]).then_inc(S["exp_done"], 1)
                act.wait_ge(S["o_done"], si + 1)
                if kind == "c":
                    nc.scalar.activation(os_c[:, g, :], ps_o[:], ACT.Copy).then_inc(S["o_read"], 1)
                else:
                    nc.scalar.activation(os_d[:, g, :], ps_o[:, 0:P], ACT.Copy).then_inc(S["o_read"], 1)
            act.wait_ge(S["sel_done"], 1)
            nc.scalar.activation(o_s, ps_s[0:TS, 0:1024].rearrange("p (k e) -> p k e", k=2), ACT.Copy).then_inc(S["sel_read"], 1)
            act.wait_ge(S["sel_read"], 1)
            nc.scalar.activation(osq[:], o_s[:, 0, :], ACT.Square).then_inc(S["osq_done"], 1)
            act.wait_ge(S["ovar"], 1)
            nc.scalar.activation(ost[:, 2, :], ost[:, 1, :], ACT.Sqrt).then_inc(S["ostd"], 1)
            act.wait_ge(S["o_turned"], 1)
            nc.scalar.activation(o_t[:, :, TP:T], ps_t[:, :, :, 0:TS].rearrange("p a b t -> p (a b) t"), ACT.Copy).then_inc(S["o_placed"], 1)
            act.wait_ge(S["o_placed"], 1)

        @block.vector
        def _(dve):
            cnt = [0]

            def link(ins):
                cnt[0] += 1
                ins.then_inc(S["chain"], 1)
                dve.wait_ge(S["chain"], cnt[0])

            for x in (qx, qdx, qix):
                link(nc.vector.memset(x[:], 0.0))
            q_new = slice(TP, T)
            for h in range(H):
                for c in range(2):
                    p = slice(64 * c, 64 * c + 64)
                    o = h * 8 + c * 4
                    link(nc.vector.tensor_copy(qx[p, :, h, o:o + 4], qc_t[p, h, q_new].rearrange("p (b q) -> p b q", q=DT)))
                p = slice(64 * (h % 2), 64 * (h % 2) + 64)
                link(nc.vector.tensor_copy(qix[p, :, 4 * h:4 * h + 4], qi_t[p, h // 2, q_new].rearrange("p (b q) -> p b q", q=DT)))
                link(nc.vector.tensor_copy(qdx[:, :, 4 * h:4 * h + 4], qd_t[:, h, q_new].rearrange("p (b q) -> p b q", q=DT)))
            link(nc.vector.tensor_scalar(half_c[:, 1:2], const["second_half"][:], neg_lam[:], None, ALU.mult))
            nc.vector.tensor_tensor(half_c[:, 0:1], half_c[:, 1:2], const["first_half"][:], ALU.add).then_inc(S["q_ready"], 1)
            dve.wait_ge(S["w_ps"], 1)
            link(nc.vector.tensor_tensor(wrow[:], ps_o[:, 0:2 * H].rearrange("p (g h) -> p g h", g=2),
                                         const["hot"][:].unsqueeze(1).to_broadcast([P, 2, H]), ALU.mult))
            link(nc.vector.tensor_reduce(wr1[:], wrow[:], AX.X, ALU.add))
            nc.vector.tensor_tensor(wsel[:], const["sel_sum"][:], wr1[:].unsqueeze(2).to_broadcast([P, 2, TS]), ALU.mult).then_inc(S["wsel_ready"], 1)
            dve.wait_ge(S["sc_ps"], 1)
            link(nc.vector.tensor_copy(sc[:, 0:PAST], ps_s[0:TS, 0:PAST]))
            nc.vector.tensor_tensor(sc[:, PAST:NKC], ps_s[0:TS, PAST:NKC], const["neg_rows"][:], ALU.add).then_inc(S["sc_out"], 1)
            dve.wait_ge(S["sc_out"], 1)
            dve.wait_ge(S["zeroed"], 1)

            def rounds(n):
                for _ in range(n):
                    link(nc.vector.max(top[:], sc[:]))
                    link(nc.vector.match_replace(sc[:], top[:], sc[:], PICKED))

            for si, (kind, g) in enumerate(stages):
                if kind == "c":
                    rounds(TOPK // 16)
                    if g == 1:
                        link(nc.vector.tensor_scalar(sc[:], sc[:], PICKED, NEG, ALU.not_equal, ALU.mult))
                        nc.vector.tensor_tensor(sc[:, PAST:NKC], sc[:, PAST:NKC], const["neg_rows"][:], ALU.add).then_inc(S["picked"], 1)
                scale = DC ** -0.5 if kind == "c" else float(P) ** -0.5
                dve.wait_ge(S["s_done"], 2 + si + 1)
                link(nc.vector.tensor_reduce(st[:, 0:1], ps_s[:, 0:NKC], AX.X, ALU.max))
                nc.vector.tensor_scalar(st[:, 1:2], st[:, 0:1], -scale, None, ALU.mult).then_inc(S["max_done"], 1)
                dve.wait_ge(S["exp_done"], si + 1)
                link(nc.vector.reciprocal(st[:, 3:4], st[:, 2:3]))
                if kind == "c":
                    link(nc.vector.tensor_tensor(st[:, 3:4], st[:, 3:4], half_c[:, 0:1], ALU.mult))
                nc.vector.tensor_scalar(p_sb[:], p_sb[:], st[:, 3:4], None, ALU.mult).then_inc(S["scaled"], 1)
                if si:
                    dve.wait_ge(S["o_done"], si)
                for b0 in range(0, NB, 4):
                    t = 5 * si + b0 // 4
                    n = min(4, NB - b0)
                    kw = min(P, NKC - b0 * P)
                    dve.wait_ge(S["turned"], t + 1)
                    src = ps_t[0:kw, t % 2, 0:n, :]
                    if kind == "c":
                        x = [nc.vector.tensor_reduce(a_t[0:kw, b0 + i, :, 0:16].rearrange("k j (h q) -> k j h q", q=DT),
                                                     ps_t[0:kw, t % 2, i, :].rearrange("k (j h c q) -> k j h q c", j=4, h=H, c=2),
                                                     AX.X, ALU.add) for i in range(n)][-1]
                    else:
                        x = nc.vector.tensor_copy(a_t[0:kw, b0:b0 + n].rearrange("k b j r -> k b (j r)"), src)
                    x.then_inc(S["placed"], 1)
                dve.wait_ge(S["placed"], 5 * (si + 1))
            dve.wait_ge(S["c_in"], 16)
            link(nc.vector.tensor_scalar(gd[:], gd[:], 1.0 - LAM_INIT, None, ALU.mult))
            dve.wait_ge(S["osq_done"], 1)
            link(nc.vector.tensor_reduce(ost[:, 0, :], osq[:], AX.X, ALU.add))
            nc.vector.tensor_scalar(ost[:, 1, :], ost[:, 0, :], 1.0 / P, EPS, ALU.mult, ALU.add).then_inc(S["ovar"], 1)
            dve.wait_ge(S["ostd"], 1)
            link(nc.vector.reciprocal(ost[:, 3, :], ost[:, 2, :]))
            o = o_s[:, 0, :].rearrange("t (h e) -> t h e", e=P)
            link(nc.vector.tensor_tensor(o, o, ost[:, 3, :].unsqueeze(2).to_broadcast([TS, H, P]), ALU.mult))
            nc.vector.tensor_tensor(o, o, gd[:].unsqueeze(1).to_broadcast([TS, H, P]), ALU.mult).then_inc(S["normed"], 1)


def attention_layer(nc, sb, load_consts, const, a, h_t, x_mid, gain, gain_c):
    with ExitStack() as st:
        with ExitStack() as qs:
            def t(name, shape):
                return sb(qs, name, shape)

            kc_t, qd_t, qc_t = t("kc_t", [P, H, T]), t("qd_t", [P, H, T]), t("qc_t", [P, H, T])
            kd_t, ki_t, qi_t = t("kd_t", [P, T]), t("ki_t", [P, T]), t("qi_t", [P, 2, T])
            v_c, v_d, w_i = t("v_c", [P, NT, 512]), t("v_d", [P, NT, P]), t("w_i", [P, NT, H])
            neg_lam = t("neg_lam", [P, 1])
            with ExitStack() as rt:
                rc = dict(const, **load_consts(rt, "rope", ["rope"]))
                att_project(nc, rc, h_t, a["w_att"], a["w_att_i"], qc_t, kc_t, v_c, qd_t, kd_t, v_d, qi_t, ki_t, w_i,
                            (a["kc"], a["vc"], a["kd"], a["vd"], a["ki"]))
            o_t = h_t
            with ExitStack() as rt:
                rc = dict(const, **load_consts(rt, "prompt", ["neg_future"]))
                prompt_attention(nc, rc, qc_t, kc_t, v_c, qd_t, kd_t, v_d, qi_t, ki_t, w_i, o_t, neg_lam, a["diff_lambda"],
                                 a["g_diff"])
            with ExitStack() as rt:
                rc = dict(const, **load_consts(rt, "sample", ["sel", "sel_sum", "sel_tok", "sel_back", "hot", "negs", "neg_rows",
                                                              "first_half", "second_half"]))
                sample_attention(nc, rc, a, qc_t, kc_t, v_c, qd_t, kd_t, v_d, qi_t, ki_t, w_i, o_t, neg_lam)
        h_next = sb(st, "h_next", [P, KD, T])
        project_add_norm(nc, "r1", const, x_mid, lambda k, t0, n: o_t[:, k, t0:t0 + n], KD, a["w_out_att"],
                         gain[1, 1], x_mid, gain_c[1, 2], h_next)
        with nc.Block() as block:
            moved = st.enter_context(nc.semaphore("moved"))

            @block.vector
            def _(dve):
                nc.vector.tensor_copy(h_t[:], h_next[:]).then_inc(moved, 1)
                dve.wait_ge(moved, 1)
        clear_semaphores(nc, [moved])


def build(nc, a):
    x_mid = nc.dram_tensor("x_mid", (T, D), F32, kind="Internal").ap()
    with ExitStack() as ctx:
        def sb(stack, name, shape):
            return stack.enter_context(nc.sbuf_tensor(name, shape, F32))

        def load_consts(stack, tag, names):
            tiles = {n: sb(stack, f"c_{n}", list(a[n].shape)) for n in names}
            done = stack.enter_context(nc.semaphore(f"{tag}_consts"))
            with nc.Block() as block:
                @block.sync
                def _(sp):
                    for n in names:
                        sp.dma_start(tiles[n][:], a[n]).then_inc(done, 16)
                    sp.wait_ge(done, 16 * len(names))
            clear_semaphores(nc, [done])
            return tiles

        const = load_consts(ctx, "all", ["ident"])
        h_t = sb(ctx, "h_t", [P, KD, T])
        gain = a["gains_row"]
        gain_c = a["gains_col"]

        project_add_norm(nc, "n0", const, a["x"], None, 0, None, None, None, gain_c[0, 0], h_t)
        with ExitStack() as st:
            mix_t = sb(st, "mix_t", [P, KD, T])
            with ExitStack() as rt:
                names = ["level_masks", "neg_upper", "neg_tail", "row_mask", "col_mask", "reset", "sel4"]
                rc = dict(const, **load_consts(rt, "rec", names))
                rows = sb(rt, "rows", [H, 2, T])
                cols = sb(rt, "cols", [P, NT, 3, H])
                lb, one_lb = sb(rt, "lb", [P, H]), sb(rt, "one_lb", [P, H])
                gate_rows(nc, rc, h_t, a["w_gates"], a["b_gates"], a["m0"], a["lb_logits"], rows, cols, lb, one_lb,
                          a["m_new"])
                recurrent_mixers(nc, rc, h_t, mix_t, a["w_rec"], a["state_a"], a["state_b"], rows, cols, lb, one_lb,
                                 a["g_rec"], a["new_a"], a["new_b"])
            project_add_norm(nc, "r0", const, a["x"], lambda k, t0, n: mix_t[:, k, t0:t0 + n], KD, a["w_out_rec"],
                             gain[0, 1], x_mid, gain_c[0, 2], h_t)

        def ffn(layer, gain_next, y_out):
            with ExitStack() as st:
                a_t = sb(st, f"a_t{layer}", [P, NF * T])
                ffn_up(nc, f"f{layer}", h_t, a_t, a["w_up"][layer], a["conv"][layer], a["conv_state"][layer],
                       a["conv_new"][layer])
                project_add_norm(nc, f"d{layer}", const, x_mid, lambda k, t0, n: a_t[:, k * T + t0:k * T + t0 + n], NF,
                                 a["w_down"][layer], gain[layer, 3], y_out, gain_next, h_t if gain_next is not None else None)

        ffn(0, gain_c[1, 0], x_mid)
        if STOP == 1:
            return
        attention_layer(nc, sb, load_consts, const, a, h_t, x_mid, gain, gain_c)
        ffn(1, None, a["y"])


STOP = 0


def shape_tables():
    i = np.arange(P)
    s, t = i[:, None], i[None, :]
    masks = np.zeros((P, LEVELS + 1, P), np.float32)
    for lv in range(LEVELS):
        b = 64 >> lv
        masks[:, lv, :] = (s // (2 * b) == t // (2 * b)) & (s % (2 * b) < b) & (t % (2 * b) >= b)
    masks[:, LEVELS, :] = s == t
    tail = np.concatenate([np.zeros(PTAIL, int), 1 + np.arange(TS) // DT])
    r = np.arange(LAST)
    ok = (tail[:, None] == tail[None, :]) & (r[:, None] <= r[None, :])
    starts = np.ones(T, np.float32)
    starts[0:TP:P] = 0
    starts[TP::DT] = 0
    n = np.arange(DB + 1)
    sel4 = np.zeros((H, H, P), np.float32)
    sel4[np.arange(H), np.arange(H)] = 1
    pos = np.concatenate([np.arange(TP), np.tile(PAST + np.arange(DT), DB)]).astype(np.float32)
    rope = np.zeros((NT * P, 2, 24), np.float32)
    for off, d in ((0, 64), (8, 128)):
        rr = d // 4
        inv = np.float32(500000.0) ** (-np.arange(rr // 2, dtype=np.float32) * np.float32(2.0) / np.float32(rr))
        ang = (pos[:, None] * inv.astype(np.float32)[None, :]).astype(np.float32).astype(np.float64)
        rope[:T, 0, off:off + rr // 2] = np.cos(ang)
        rope[:T, 1, off:off + rr // 2] = np.sin(ang)
    row = np.arange(P)
    j, hq = row // 32, row % 32
    used = hq < 16
    sel = np.zeros((P, 2, H, TS), np.float32)
    for g in range(2):
        for rr in row[used]:
            sel[rr, g, hq[rr] // 4, (4 * g + j[rr]) * DT + hq[rr] % 4] = 1
    sel_sum = sel.sum(2)
    tok = np.zeros((LAST, 2, P), np.float32)
    tok[PTAIL:] = sel_sum.transpose(2, 1, 0)
    hot = np.zeros((P, H), np.float32)
    hot[row[used], hq[used] // 4] = 1
    q = np.arange(32) % DT
    negs = np.full((32, DB, LAST), NEG, np.float32)
    for b in range(DB):
        for c in range(DT):
            negs[q >= c, b, PTAIL + DT * b + c] = 0
    return {
        "ident": np.eye(P, dtype=np.float32),
        "level_masks": masks,
        "neg_upper": np.where(s <= t, 0, NEG).astype(np.float32),
        "neg_tail": np.where(ok, 0, NEG).astype(np.float32),
        "row_mask": (tail[:, None] == n[None, :]).astype(np.float32),
        "col_mask": np.broadcast_to((n[:, None] == tail[None, :]).astype(np.float32), (P, DB + 1, LAST)),
        "reset": np.broadcast_to(starts, (P, T)),
        "sel4": sel4,
        "rope": rope.reshape(NT, P, 2, 24).transpose(1, 0, 2, 3),
        "neg_future": np.where(t <= s, 0, NEG).astype(np.float32),
        "sel": sel,
        "sel_sum": sel_sum,
        "sel_tok": tok,
        "sel_back": sel_sum.transpose(2, 1, 0),
        "hot": hot,
        "negs": negs,
        "first_half": (hq % 8 < 4).astype(np.float32)[:, None],
        "second_half": (hq % 8 >= 4).astype(np.float32)[:, None],
        "neg_rows": negs[np.tile(np.arange(DT), DB), np.repeat(np.arange(DB), DT)],
    }


def kernel(**inputs):
    import concourse.bacc as _bacc
    from concourse.bass_utils import run_bass_kernel_spmd as _run

    x = {n: np.asarray(v) for n, v in inputs.items()}

    def blocks(w, n):
        return w.reshape(w.shape[0] // P, P, n, -1).transpose(2, 1, 0, 3)

    arrays = dict(shape_tables())
    arrays["x"] = np.concatenate([x["meta_tokens"], x["x_prompt"][0], x["x_sample"].reshape(TS, D)])
    arrays["gains_row"] = x["norm_gains"]
    arrays["gains_col"] = x["norm_gains"].reshape(2, 4, KD, P).transpose(0, 1, 3, 2)
    wr = x["w_in_rec"][0]
    heads = wr[:, :8 * 512].reshape(D, 8, H, P)
    arrays["w_rec"] = np.concatenate([heads[:, 0:4].transpose(2, 0, 1, 3), heads[:, 4:8].transpose(2, 0, 1, 3)]) \
        .reshape(NU, KD, P, 512).transpose(0, 2, 1, 3)
    arrays["w_gates"] = wr[:, 8 * 512:].reshape(KD, P, 2 * H).transpose(1, 0, 2)
    arrays["b_gates"] = x["b_gates_rec"][0].reshape(2 * H)
    arrays["m0"] = x["state_mlstm_m"][0].T
    arrays["lb_logits"] = x["lb_logits"].reshape(2, H, P).transpose(2, 0, 1)
    arrays["state_a"] = x["state_hgrn"][0].transpose(1, 2, 0, 3)
    arrays["state_b"] = np.concatenate([x["state_mlstm_C"][0], x["state_mlstm_n"][0][..., None]], -1).transpose(1, 2, 0, 3)
    arrays["g_rec"] = np.concatenate([x["g_norm_hgrn"], x["g_norm_mlstm"]])
    arrays["w_out_rec"] = x["w_out_rec"][0].reshape(KD, P, D).transpose(1, 0, 2)
    arrays["w_up"] = x["w_ffn_up"].reshape(2, KD, P, 2, NF, P).transpose(0, 4, 2, 1, 3, 5).reshape(2, NF * P, KD * 2 * P)
    arrays["w_down"] = x["w_ffn_down"].reshape(2, NF, P, D).transpose(0, 2, 1, 3)
    arrays["conv"] = np.concatenate([x["ffn_conv_w"], x["ffn_conv_b"][:, None]], 1).reshape(2, 4, NF, P) \
        .transpose(0, 3, 2, 1).reshape(2, P, NF * 4)
    arrays["conv_state"] = x["state_ffn_conv"].reshape(2, DB, 2, NF, P).transpose(0, 4, 3, 1, 2).reshape(2, P, NF * DB * 2)
    wa = x["w_in_att"][0]
    arrays["w_att"] = wa[:, :2560].reshape(KD, P, 5, 512).transpose(2, 1, 0, 3)
    arrays["w_att_i"] = wa[:, 2560:].reshape(KD, P, 68).transpose(1, 0, 2)
    arrays["w_out_att"] = x["w_out_att"][0].reshape(KD, P, D).transpose(1, 0, 2)
    arrays["diff_lambda"] = x["diff_lambda"][0].reshape(4 * DC)
    arrays["g_diff"] = x["g_norm_diff"][0]
    arrays["pages"] = x["page_table"].reshape(1, DB * NPG)
    npool = x["cache_diff_k"].shape[1]
    arrays["pool_ck"] = x["cache_diff_k"][0].transpose(0, 3, 2, 1).reshape(npool * P, H * P)
    arrays["pool_cv"] = x["cache_diff_v"][0].reshape(npool * P, H * P)
    arrays["pool_dk"] = x["cache_dsa_k"][0].transpose(0, 2, 1).reshape(npool * P, P)
    arrays["pool_dv"] = x["cache_dsa_v"][0].reshape(npool * P, P)
    arrays["pool_ik"] = x["cache_idx_k"][0].transpose(0, 2, 1).reshape(npool * 64, P)
    arrays = {n: np.ascontiguousarray(v) for n, v in arrays.items()}

    nc = _bacc.Bacc("TRN2", target_bir_lowering=False, num_devices=1)
    aps = {n: nc.dram_tensor(f"in_{n}", v.shape, mybir.dt.from_np(v.dtype), kind="ExternalInput").ap()
           for n, v in arrays.items()}
    outs = {"y": (T, D), "new_a": (H, P, DB + 1, P), "new_b": (H, P, DB + 1, P + 1), "m_new": (H, DB + 1),
            "conv_new": (2, P, NF * (DB + 1) * 2), "kc": (T, 512), "vc": (T, 512), "kd": (T, P), "vd": (T, P), "ki": (T, 64)}
    for n, s in outs.items():
        aps[n] = nc.dram_tensor(f"out_{n}", s, F32, kind="ExternalOutput").ap()
    build(nc, aps)
    r = _run(nc, [{f"in_{n}": v for n, v in arrays.items()}], core_ids=[0]).results[0]
    o = {n: r[f"out_{n}"] for n in outs}
    y = o["y"]
    sa = o["new_a"].transpose(2, 0, 1, 3)
    sbn = o["new_b"].transpose(2, 0, 1, 3)
    cv = o["conv_new"].reshape(2, P, NF, DB + 1, 2).transpose(0, 3, 4, 2, 1).reshape(2, DB + 1, 2, DFF)
    m = o["m_new"].T

    def both(v, tail):
        return v[:TP].reshape((1, 1, TP) + tail), v[TP:].reshape((1, DB, DT) + tail)

    c_k, c_v = both(o["kc"], (H, P)), both(o["vc"], (H, P))
    d_k, d_v, i_k = both(o["kd"], (P,)), both(o["vd"], (P,)), both(o["ki"], (64,))
    return (y[N_META:TP].reshape(1, SEQ, D), y[TP:].reshape(DB, DT, D),
            sa[None, 0:1], sa[None, 1:], sbn[None, 0:1, ..., :P], sbn[None, 1:, ..., :P],
            sbn[None, 0:1, ..., P], sbn[None, 1:, ..., P], m[None, 0:1], m[None, 1:],
            cv[:, 0:1], cv[:, 1:], *c_k, *c_v, *d_k, *d_v, *i_k)
```

```python
import math
from contextlib import ExitStack

import numpy as np

import concourse.bass as bass
from concourse import mybir

P = 128
F32 = mybir.dt.float32
F32R = mybir.dt.float32r
U32 = mybir.dt.uint32
I32 = mybir.dt.int32
ACT = mybir.ActivationFunctionType
ALU = mybir.AluOpType
AX = mybir.AxisListType

D = 1024
KD = D // P
SEQ, N_META = 1024, 16
TP = SEQ + N_META
DB, DT = 8, 4
TS = DB * DT
T = TP + TS
NT = (T + P - 1) // P
LAST = T - (NT - 1) * P
PTAIL = TP - (NT - 1) * P
CH = [(0, 384), (384, 384), (768, T - 768)]
H = 4
DFF = 2816
NF = DFF // P
PAST, PAGE = 2048, 128
NPG = PAST // PAGE
TOPK = 256
DC = 64
EPS = 1e-6
NEG = -1e30
PICKED = -3e38


def rows_of(m):
    return P if m < NT - 1 else LAST


def products(pe, out, lhs, rhs, first, last):
    pe.matmul(out, lhs[0], rhs[0], start=first, stop=False)
    pe.matmul(out, lhs[0], rhs[1], start=False, stop=False)
    return pe.matmul(out, lhs[1], rhs[0], start=False, stop=last)


def clear_semaphores(nc, handles):
    with nc.Block() as block:
        @block.gpsimd
        def _(pool):
            for s in handles:
                pool.sem_clear(s)


TG = 3
WK = 2
NW = 4


def project_add_norm(nc, tag, const, x_in, act_t, kb, w_dram, gain_post, x_out, gain_next, h_t, parts=False):
    ident = const["ident"]
    with ExitStack() as ctx:
        def sb(name, shape, dt=F32):
            return ctx.enter_context(nc.sbuf_tensor(f"{tag}_{name}", shape, dt))

        used = []

        def sem(name):
            used.append(ctx.enter_context(nc.semaphore(f"{tag}_{name}")))
            return used[-1]

        NX = 3
        loads = kb // WK
        xt = sb("xt", [P, NX, D])
        sq = sb("sq", [P, D])
        stat = sb("stat", [P, NT, 8])
        if act_t is not None:
            yt = sb("yt", [P, TG, D])
            gp = sb("gp", [P, D])
            w_sb = sb("w", [P, NW, WK, D])
            ps_y = ctx.enter_context(nc.psum_tensor(f"{tag}_psy", [P, TG, D], F32))
        w_in = [sem(f"w_in{i}") for i in range(NW)]
        w_used = sem("w_used")
        if h_t is not None:
            xn = sb("xn", [P, 2, D])
            gn = sb("gn", [P, KD])
            whole = sb("whole", [P, KD, P]) if parts else None
            ps_t = ctx.enter_context(nc.psum_tensor(f"{tag}_pst", [P, KD, P], F32))
        x_in_sem = [sem(f"x_in{i}") for i in range(NX)]
        gains_in = sem("gains_in")
        y_done = sem("y_done")
        y_read = sem("y_read")
        ysq_done = sem("ysq_done")
        yvar_done = sem("yvar_done")
        ystd_done = sem("ystd_done")
        x_new = sem("x_new")
        x_out_sem = [sem(f"x_out{i}") for i in range(NX)]
        xsq_done = sem("xsq_done")
        xvar_done = sem("xvar_done")
        xstd_done = sem("xstd_done")
        xrs_done = sem("xrs_done")
        xn_done = sem("xn_done")
        turned = sem("turned")
        h_done = sem("h_done")
        dve_chain = sem("dve_chain")

        ctx.callback(clear_semaphores, nc, used)
        block = ctx.enter_context(nc.Block())

        def stores(m):
            return [(x_out[m * P:m * P + rows_of(m), :], 0, rows_of(m))] if x_out is not None else []

        def stored(m):
            return 16 * sum(len(stores(i)) for i in range(m % NX, m + 1, NX))

        @block.sync
        def _(sp):
            if act_t is not None:
                sp.dma_start(gp[:], gain_post.partition_broadcast(P)).then_inc(gains_in, 16)
            if h_t is not None:
                sp.dma_start(gn[:], gain_next).then_inc(gains_in, 16)

            def load(m):
                r = rows_of(m)
                if m >= NX:
                    if stores(m - NX):
                        sp.wait_ge(x_out_sem[m % NX], stored(m - NX))
                    if h_t is not None:
                        sp.wait_ge(xn_done, m - NX + 1)
                sp.dma_start(xt[0:r, m % NX, :], x_in[m * P:m * P + r, :]).then_inc(x_in_sem[m % NX], 16)

            def load_w(n_load):
                g, c = divmod(n_load, loads)
                if n_load >= NW:
                    pg, pc = divmod(n_load - NW, loads)
                    if pc == loads - 1:
                        sp.wait_ge(y_done, TG * (pg + 1))
                    else:
                        sp.wait_ge(w_used, pg * (loads - 1) + pc + 1)
                sp.dma_start(w_sb[:, n_load % NW], w_dram[:, c * WK:(c + 1) * WK, :]).then_inc(w_in[n_load % NW], 16)

            def load_ws(a, b):
                for n_load in range(a, min(b, loads * (NT // TG))):
                    load_w(n_load)

            if act_t is not None:
                load_ws(0, NW)
            for m in range(min(2, NT)):
                load(m)
            if act_t is not None:
                load_ws(NW, loads + NW)
            for m in range(NT):
                if act_t is not None and m % TG == 0 and m:
                    load_ws((m // TG) * loads + NW, (m // TG + 1) * loads + NW)
                if m + 2 < NT:
                    load(m + 2)
                if act_t is not None:
                    sp.wait_ge(x_new, m + 1)
                else:
                    sp.wait_ge(x_in_sem[m % NX], 16 * (m // NX + 1))
                for dst, r0, nr in stores(m):
                    sp.dma_start(dst, xt[r0:r0 + nr, m % NX, :]).then_inc(x_out_sem[m % NX], 16)
            for i in range(NX):
                last = (NT - 1 - i) // NX * NX + i
                if stores(last):
                    sp.wait_ge(x_out_sem[i], stored(last))

        @block.tensor
        def _(pe):
            def turn(m):
                r = rows_of(m)
                pe.wait_ge(xn_done, m + 1)
                if m >= 1:
                    pe.wait_ge(h_done, m)
                for k in range(KD):
                    t = pe.transpose(ps_t[:, k, 0:r], xn[0:r, m % 2, k * P:(k + 1) * P], ident[0:r, 0:r])
                t.then_inc(turned, 1)

            for g in range(NT // TG):
                tiles = range(TG * g, TG * g + TG)
                for c in range(loads if act_t is not None else 0):
                    n_load = g * loads + c
                    pe.wait_ge(w_in[n_load % NW], 16 * (n_load // NW + 1))
                    for k in range(c * WK, (c + 1) * WK):
                        for m in tiles:
                            r = rows_of(m)
                            if k == 0 and g:
                                pe.wait_ge(y_read, m - TG + 1)
                            for n in range(2):
                                mm = pe.matmul(ps_y[0:r, m % TG, n * 512:(n + 1) * 512], act_t(k, m * P, r),
                                               w_sb[:, n_load % NW, k % WK, n * 512:(n + 1) * 512],
                                               start=(k == 0), stop=(k == kb - 1))
                            if k == kb - 1:
                                mm.then_inc(y_done, 1)
                            elif k % WK == WK - 1 and m == tiles[-1]:
                                mm.then_inc(w_used, 1)
                    if h_t is not None and g and c in (1, 2, 3):
                        turn(TG * (g - 1) + c - 1)
                if h_t is not None and (act_t is None or g == NT // TG - 1):
                    for m in tiles:
                        turn(m)

        @block.scalar
        def _(act):
            for m in range(NT):
                r = rows_of(m)
                if act_t is not None:
                    act.wait_ge(y_done, m + 1)
                    if m and h_t is None:
                        act.wait_ge(ysq_done, m)
                    if m >= TG:
                        act.wait_ge(x_new, m - TG + 1)
                    nc.scalar.activation(yt[0:r, m % TG, :], ps_y[0:r, m % TG, :], ACT.Copy).then_inc(y_read, 1)
                    act.wait_ge(y_read, m + 1)
                    nc.scalar.activation(sq[0:r, :], yt[0:r, m % TG, :], ACT.Square,
                                         accum_out=stat[0:r, m, 0:1]).then_inc(ysq_done, 1)
                    act.wait_ge(yvar_done, m + 1)
                    nc.scalar.activation(stat[0:r, m, 2:3], stat[0:r, m, 1:2], ACT.Sqrt).then_inc(ystd_done, 1)
                if h_t is None:
                    continue
                if act_t is not None:
                    act.wait_ge(x_new, m + 1)
                    act.wait_ge(ysq_done, m + 1)
                else:
                    act.wait_ge(x_in_sem[m % NX], 16 * (m // NX + 1))
                if m:
                    act.wait_ge(xsq_done, m)
                nc.scalar.activation(sq[0:r, :], xt[0:r, m % NX, :], ACT.Square,
                                     accum_out=stat[0:r, m, 4:5]).then_inc(xsq_done, 1)
                act.wait_ge(xvar_done, m + 1)
                nc.scalar.activation(stat[0:r, m, 6:7], stat[0:r, m, 5:6], ACT.Sqrt).then_inc(xstd_done, 1)
                act.wait_ge(xrs_done, m + 1)
                if m >= 2:
                    act.wait_ge(turned, m - 1)
                nc.scalar.activation(xn[0:r, m % 2, :], xt[0:r, m % NX, :], ACT.Copy,
                                     scale=stat[0:r, m, 7:8]).then_inc(xn_done, 1)
                act.wait_ge(xsq_done, m + 1)

        @block.vector
        def _(dve):
            chain = [0]

            def link(ins):
                chain[0] += 1
                ins.then_inc(dve_chain, 1)
                dve.wait_ge(dve_chain, chain[0])

            dve.wait_ge(gains_in, 16 * ((act_t is not None) + (h_t is not None)))

            def spread(m):
                r = rows_of(m)
                dve.wait_ge(turned, m + 1)
                c = slice(m * P, m * P + r)
                g = gn[:].unsqueeze(2).to_broadcast([P, KD, r])
                if not parts:
                    nc.vector.tensor_tensor(h_t[:, :, c], ps_t[:, :, 0:r], g, ALU.mult).then_inc(h_done, 1)
                    return
                x = nc.vector.tensor_tensor(whole[:, :, 0:r], ps_t[:, :, 0:r], g, ALU.mult)
                x.then_inc(h_done, 1)
                dve.wait_ge(h_done, m + 1)
                link(nc.vector.tensor_copy(h_t[:, 0, :, c], whole[:, :, 0:r]))
                link(nc.vector.tensor_tensor(h_t[:, 1, :, c], whole[:, :, 0:r], h_t[:, 0, :, c].bitcast(F32), ALU.subtract))

            for m in range(NT):
                r = rows_of(m)
                if act_t is not None:
                    dve.wait_ge(ysq_done, m + 1)
                    nc.vector.tensor_scalar(stat[0:r, m, 1:2], stat[0:r, m, 0:1], 1.0 / D, EPS,
                                            ALU.mult, ALU.add).then_inc(yvar_done, 1)
                    dve.wait_ge(ystd_done, m + 1)
                    link(nc.vector.reciprocal(stat[0:r, m, 3:4], stat[0:r, m, 2:3]))
                    link(nc.vector.scalar_tensor_tensor(out=yt[0:r, m % TG, :], in0=yt[0:r, m % TG, :],
                                                        scalar=stat[0:r, m, 3:4], in1=gp[0:r, :],
                                                        op0=ALU.mult, op1=ALU.mult))
                    dve.wait_ge(x_in_sem[m % NX], 16 * (m // NX + 1))
                    nc.vector.tensor_tensor(xt[0:r, m % NX, :], xt[0:r, m % NX, :], yt[0:r, m % TG, :],
                                            ALU.add).then_inc(x_new, 1)
                if h_t is None:
                    dve.wait_ge(x_new, m + 1)
                    continue
                dve.wait_ge(xsq_done, m + 1)
                nc.vector.tensor_scalar(stat[0:r, m, 5:6], stat[0:r, m, 4:5], 1.0 / D, EPS,
                                        ALU.mult, ALU.add).then_inc(xvar_done, 1)
                dve.wait_ge(xstd_done, m + 1)
                nc.vector.reciprocal(stat[0:r, m, 7:8], stat[0:r, m, 6:7]).then_inc(xrs_done, 1)
                if m >= 1:
                    spread(m - 1)
            if h_t is not None:
                spread(NT - 1)


CHUNK_ENDS = [m * P + P - 1 for m in range(NT - 1)] + [TP - 1] + [TP + DT * b + DT - 1 for b in range(DB)]
LEVELS = 7
NU = 2 * H


def level_width(level):
    b = 64 >> level
    return (NT - 1) * P if b >= 16 else (TP if b >= 4 else T)


def gate_rows(nc, const, h_t, w_gates, b_gates, m0, lb_logits, rows, cols, lb, one_lb, m_out):
    ident = const["ident"]
    with ExitStack() as ctx:
        def sb(name, shape, dt=F32):
            return ctx.enter_context(nc.sbuf_tensor(f"g_{name}", shape, dt))

        used = []

        def sem(name):
            used.append(ctx.enter_context(nc.semaphore(f"g_{name}")))
            return used[-1]

        wg = sb("wg", [P, KD, 2 * H])
        bg = sb("bg", [P, 2 * H])
        m0s = sb("m0s", [H, DB])
        lg = sb("lg", [P, 2, H])
        lgx = sb("lgx", [P, 6, H])
        gc = sb("gc", [P, NT, 2 * H])
        ta = sb("ta", [P, NT, H])
        te = sb("te", [P, NT, H])
        lfc = sb("lfc", [P, NT, H])
        ir = sb("ir", [H, T])
        im = sb("im", [H, T])
        lf = sb("lf", [H, T])
        lfm = sb("lfm", [H, T])
        br = sb("br", [H, T])
        mr = sb("mr", [H, T])
        mp = sb("mp", [H, T])
        cs = sb("cs", [H, 3, T])
        ps_g = ctx.enter_context(nc.psum_tensor("g_psg", [P, NT, 2 * H], F32))
        ps_r = ctx.enter_context(nc.psum_tensor("g_psr", [H, 2, 3, 512], F32))
        ps_c = ctx.enter_context(nc.psum_tensor("g_psc", [P, NT, 3, H], F32))
        loaded, gates_done, biased, abs_done, exp_done, ln_done = (
            sem(x) for x in ("loaded", "gates_done", "biased", "abs_done", "exp_done", "ln_done"))
        lf_done, rows_done, expo_ready, rows_exp, cols_ready, cols_done = (
            sem(x) for x in ("lf_done", "rows_done", "expo_ready", "rows_exp", "cols_ready", "cols_done"))
        cols_out, lb_sub, lb_exp, chain_s, stored, achain = (
            sem(x) for x in ("cols_out", "lb_sub", "lb_exp", "chain", "stored", "achain"))
        reset = const["reset"]
        ctx.callback(clear_semaphores, nc, used)
        block = ctx.enter_context(nc.Block())

        @block.sync
        def _(sp):
            for dst, src in ((wg[:], w_gates), (bg[:], b_gates.partition_broadcast(P)), (m0s[:], m0), (lg[:], lb_logits)):
                sp.dma_start(dst, src).then_inc(loaded, 16)
            sp.wait_ge(cols_ready, 1)
            with nc.allow_non_contiguous_dma(reason="36 stabilisers"):
                sp.dma_start(m_out[:, 0:1], mr[:, TP - 1:TP]).then_inc(stored, 16)
                sp.dma_start(m_out[:, 1:1 + DB], mr[:, TP + DT - 1:T:DT]).then_inc(stored, 16)
            sp.wait_ge(stored, 32)

        @block.tensor
        def _(pe):
            pe.wait_ge(loaded, 64)
            for m in range(NT):
                for k in range(KD):
                    mm = pe.matmul(ps_g[0:rows_of(m), m, :], h_t[:, k, m * P:m * P + rows_of(m)], wg[:, k, :],
                                   start=(k == 0), stop=(k == KD - 1))
            mm.then_inc(gates_done, 1)
            pe.wait_ge(lf_done, 1)
            for m in range(NT):
                r = rows_of(m)
                for kind, src in ((0, gc[0:r, m, 0:H]), (1, lfc[0:r, m, :])):
                    t = pe.transpose(ps_r[:, kind, m // 4, (m % 4) * P:(m % 4) * P + r], src, ident[0:r, 0:r])
            t.then_inc(rows_done, 1)
            pe.wait_ge(cols_ready, 2)
            pe.wait_ge(rows_exp, 2)
            for m in range(NT):
                r = rows_of(m)
                for kind in range(3):
                    t = pe.transpose(ps_c[0:r, m, kind, :], cs[:, kind, m * P:m * P + r], ident[0:H, 0:H])
            t.then_inc(cols_done, 1)

        @block.scalar
        def _(act):
            act.wait_ge(lb_sub, 1)
            nc.scalar.activation(lgx[:, 1:3, :], lg[:], ACT.Exp).then_inc(lb_exp, 1)
            act.wait_ge(abs_done, 1)
            nc.scalar.activation(te[:], ta[:], ACT.Exp, scale=-1.0).then_inc(achain, 1)
            act.wait_ge(achain, 1)
            nc.scalar.activation(ta[:], te[:], ACT.Ln, bias=1.0).then_inc(ln_done, 1)
            act.wait_ge(expo_ready, 1)
            nc.scalar.activation(rows[:, 1, :], mp[:], ACT.Exp).then_inc(rows_exp, 1)
            act.wait_ge(cols_ready, 2)
            nc.scalar.activation(cs[:, 1, :], cs[:, 1, :], ACT.Exp).then_inc(achain, 1)
            nc.scalar.activation(cs[:, 2, :], mr[:], ACT.Exp, scale=-1.0).then_inc(achain, 1)
            act.wait_ge(achain, 3)
            nc.scalar.activation(te[:, 0, 0:1], ta[:, 0, 0:1], ACT.Copy).then_inc(rows_exp, 1)

        @block.vector
        def _(dve):
            n = [0]

            def link(ins):
                n[0] += 1
                ins.then_inc(chain_s, 1)
                dve.wait_ge(chain_s, n[0])

            dve.wait_ge(loaded, 64)
            link(nc.vector.tensor_tensor(lgx[:, 0, :], lg[:, 0, :], lg[:, 1, :], ALU.max))
            nc.vector.tensor_tensor(lg[:], lg[:], lgx[:, 0, :].unsqueeze(1).to_broadcast([P, 2, H]), ALU.subtract).then_inc(lb_sub, 1)
            dve.wait_ge(lb_exp, 1)
            link(nc.vector.tensor_tensor(lgx[:, 3, :], lgx[:, 1, :], lgx[:, 2, :], ALU.add))
            link(nc.vector.reciprocal(lgx[:, 4, :], lgx[:, 3, :]))
            link(nc.vector.tensor_tensor(lb[:], lgx[:, 1, :], lgx[:, 4, :], ALU.mult))
            link(nc.vector.tensor_scalar(one_lb[:], lb[:], -1.0, 1.0, ALU.mult, ALU.add))
            link(nc.vector.memset(gc[:], 0.0))
            dve.wait_ge(gates_done, 1)
            link(nc.vector.tensor_tensor(gc[:, 0:NT - 1, :], ps_g[:, 0:NT - 1, :],
                                         bg[:].unsqueeze(1).to_broadcast([P, NT - 1, 2 * H]), ALU.add))
            link(nc.vector.tensor_tensor(gc[0:LAST, NT - 1, :], ps_g[0:LAST, NT - 1, :], bg[0:LAST, :], ALU.add))
            f = gc[:, :, H:2 * H]
            nc.vector.scalar_tensor_tensor(out=ta[:], in0=f, scalar=-1.0, in1=f, op0=ALU.mult, op1=ALU.max).then_inc(abs_done, 1)
            dve.wait_ge(ln_done, 1)
            nc.vector.scalar_tensor_tensor(out=lfc[:], in0=f, scalar=0.0, in1=ta[:], op0=ALU.min, op1=ALU.subtract).then_inc(lf_done, 1)
            dve.wait_ge(rows_done, 1)
            for kind, dst in ((0, ir), (1, lf)):
                for c in range(3):
                    w = min(512, T - c * 512)
                    link(nc.vector.tensor_copy(dst[:, c * 512:c * 512 + w], ps_r[:, kind, c, 0:w]))
            starts = slice(TP, T, DT)
            link(nc.vector.tensor_tensor_scan(br[:], reset[0:H, :], lf[:], 0.0, ALU.mult, ALU.add))
            link(nc.vector.tensor_copy(im[:], ir[:]))
            link(nc.vector.tensor_copy(lfm[:], lf[:]))
            link(nc.vector.tensor_tensor(mp[:, 0:DB], lf[:, starts], m0s[:], ALU.add))
            link(nc.vector.tensor_tensor(im[:, starts], ir[:, starts], mp[:, 0:DB], ALU.max))
            link(nc.vector.memset(lfm[:, starts], NEG))
            link(nc.vector.tensor_tensor_scan(mr[:], lfm[:], im[:], 0.0, ALU.add, ALU.max))
            nc.vector.tensor_tensor(rows[:, 0, :], br[:], mr[:], ALU.subtract).then_inc(cols_ready, 1)
            dve.wait_ge(cols_ready, 1)
            full = (NT - 2) * P
            link(nc.vector.memset(mp[:, 0:P], 0.0))
            link(nc.vector.tensor_copy(mp[:, P:P + full].rearrange("h (m t) -> h m t", t=P),
                                       mr[:, P - 1:P - 1 + full:P].unsqueeze(2).to_broadcast([H, NT - 2, P])))
            link(nc.vector.tensor_copy(mp[:, (NT - 1) * P:TP], mr[:, (NT - 1) * P - 1:(NT - 1) * P].to_broadcast([H, PTAIL])))
            link(nc.vector.tensor_copy(mp[:, TP:T].rearrange("h (b t) -> h b t", t=DT),
                                       m0s[:].unsqueeze(2).to_broadcast([H, DB, DT])))
            nc.vector.tensor_tensor(mp[:], mp[:], rows[:, 0, :], ALU.add).then_inc(expo_ready, 1)
            link(nc.vector.tensor_tensor(cs[:, 0, :], ir[:], br[:], ALU.subtract))
            ra = rows[:, 0, :]
            nb = NT - 1
            link(nc.vector.tensor_tensor(cs[:, 1, 0:nb * P].rearrange("h (m t) -> h m t", t=P),
                                         cs[:, 0, 0:nb * P].rearrange("h (m t) -> h m t", t=P),
                                         ra[:, P - 1:nb * P:P].unsqueeze(2).to_broadcast([H, nb, P]), ALU.add))
            link(nc.vector.tensor_tensor(cs[:, 1, nb * P:TP], cs[:, 0, nb * P:TP],
                                         ra[:, TP - 1:TP].to_broadcast([H, PTAIL]), ALU.add))
            nc.vector.tensor_tensor(cs[:, 1, TP:T].rearrange("h (b t) -> h b t", t=DT),
                                    cs[:, 0, TP:T].rearrange("h (b t) -> h b t", t=DT),
                                    ra[:, TP + DT - 1:T:DT].unsqueeze(2).to_broadcast([H, DB, DT]), ALU.add).then_inc(cols_ready, 1)
            dve.wait_ge(cols_done, 1)
            link(nc.vector.memset(cols[:], 1.0))
            link(nc.vector.tensor_copy(cols[:, 0:nb, :, :], ps_c[:, 0:nb, :, :]))
            link(nc.vector.tensor_copy(cols[0:LAST, nb, :, :], ps_c[0:LAST, nb, :, :]))


def recurrent_mixers(nc, const, h_t, mix_t, w_units, states_a, states_b, rows, cols, lb, one_lb,
                     g_norms, new_a, new_b):
    ident = const["ident"]
    with ExitStack() as ctx:
        def sb(name, shape, dt=F32):
            return ctx.enter_context(nc.sbuf_tensor(f"r_{name}", shape, dt))

        def psum(name, shape):
            return ctx.enter_context(nc.psum_tensor(f"r_{name}", shape, F32))

        used = []

        def sem(name):
            used.append(ctx.enter_context(nc.semaphore(f"r_{name}")))
            return used[-1]

        E = P + 1
        w_sb = sb("w", [P, 2, KD, 2 * P])
        q_t = sb("q", [P, 2, T])
        k_t = sb("k", [P, 2, T])
        vg = sb("vg", [P, 2, NT, 2 * E])
        b_t = sb("b", [P, T])
        e1 = sb("e1", [P, T])
        dd = sb("dd", [P, 2, T])
        xx = sb("xx", [P, 2, T])
        at = sb("at", [P, NT, P])
        kh = sb("kh", [P, NT, P])
        khx = sb("khx", [LAST, DB + 1, P])
        qx = sb("qx", [P, DB + 1, LAST])
        s_pr = sb("s_pr", [P, NT + 1, E])
        s_in = sb("s_in", [P, DB, E])
        s_new = sb("s_new", [P, DB, E])
        o_sb = sb("o", [P, NT, E])
        sq = sb("sq", [P, NT, P])
        gno = sb("gno", [P, 2, P])
        st = sb("st", [P, 8, NT])
        masks, negm, negtail = const["level_masks"], const["neg_upper"], const["neg_tail"]
        row_mask, col_mask, reset, sel4 = const["row_mask"], const["col_mask"], const["reset"], const["sel4"]

        ps_p = psum("psp", [P, 2, 512])
        ps_a = psum("psa", [P, 2, 4, P])
        ps_at = psum("psat", [LAST, 512])
        ps_t = psum("pst", [P, 4, P])
        ps_u = psum("psu", [P, 512])
        ps_o = psum("pso", [P, 512])

        w_in = [sem("w_in0"), sem("w_in1")]
        s_ld = sem("s_ld")
        g_in, proj_done, proj_free = sem("g_in"), sem("proj_done"), sem("proj_free")
        dve_unit = sem("dve_unit")
        acts, achain, dchain = sem("acts"), sem("achain"), sem("dchain")
        lf_ready, b_ready, e1_ready, d_ready, e_ready, x_ready = (
            sem(x) for x in ("lf_ready", "b_ready", "e1_ready", "d_ready", "e_ready", "x_ready"))
        a_done, a_used, at_done, at_used = sem("a_done"), sem("a_used"), sem("at_done"), sem("at_used")
        kx_ready, kt_done, kt_used, khx_ready = sem("kx_ready"), sem("kt_done"), sem("kt_used"), sem("khx_ready")
        u_done, u_used, o_done, o_used = sem("u_done"), sem("u_used"), sem("o_done"), sem("o_used")
        sq_ready, std_in, std_out, y_ready = sem("sq_ready"), sem("std_in"), sem("std_out"), sem("y_ready")
        yt_done, yt_used, s_out, init = sem("yt_done"), sem("yt_used"), sem("s_out"), sem("init")
        bc_done, bc_a, bc_d, wm_ready, w_ready = sem("bc_done"), sem("bc_a"), sem("bc_d"), sem("wm_ready"), sem("w_ready")
        g_ready = sem("g_ready")
        ctx.callback(clear_semaphores, nc, used)
        block = ctx.enter_context(nc.Block())

        NG = 15
        KG = 3
        groups = [(0, 4), (4, 4), (8, 1)]
        UPD = NT + DB
        UG = [(i, min(3, UPD - i)) for i in range(0, UPD, 3)]
        OG = [(i, 3) for i in range(0, NT, 3)]
        tails = [i for i in range(LEVELS + 1) if i == LEVELS or level_width(i) > (NT - 1) * P]
        NTAIL = len(tails)

        @block.sync
        def _(sp):
            sp.dma_start(gno[:], g_norms.partition_broadcast(P)).then_inc(g_in, 16)
            for u in range(NU + 1):
                if u < NU:
                    for half in range(2):
                        if u:
                            sp.wait_ge(proj_done, NG * (u - 1) + (6 if half == 0 else NG))
                        sp.dma_start(w_sb[:, half], w_units[u, :, :, half * 2 * P:(half + 1) * 2 * P]).then_inc(w_in[half], 16)
                if u >= 1:
                    v = u - 1
                    sp.wait_ge(u_used, len(UG) * (v + 1))
                    e, out = (P, new_a[v]) if v < H else (E, new_b[v - H])
                    sp.dma_start(out[:, 0, :], s_pr[:, NT, 0:e]).then_inc(s_out, 16)
                    sp.dma_start(out[:, 1:1 + DB, :], s_new[:, :, 0:e]).then_inc(s_out, 16)
                if u < NU:
                    if u:
                        sp.wait_ge(o_done, len(OG) * u)
                    if u < H:
                        sp.dma_start(s_in[:, :, 0:P], states_a[u]).then_inc(s_ld, 16)
                    else:
                        sp.dma_start(s_in[:], states_b[u - H]).then_inc(s_ld, 16)
            sp.wait_ge(s_out, 32 * NU)

        @block.tensor
        def _(pe):
            def project(u, i):
                g = NG * u + i
                if i in (0, 6):
                    pe.wait_ge(w_in[i // 6], 16 * (u + 1))
                if g >= 2:
                    pe.wait_ge(proj_free, g - 1)
                for k in range(KD):
                    if i < 6:
                        t0, tw = CH[i % 3]
                        mm = pe.matmul(ps_p[:, g % 2, 0:tw], w_sb[:, 0, k, (i // 3) * P:(i // 3 + 1) * P],
                                       h_t[:, k, t0:t0 + tw], start=(k == 0), stop=(k == KD - 1))
                    else:
                        m = i - 6
                        mm = pe.matmul(ps_p[0:rows_of(m), g % 2, 0:2 * P], h_t[:, k, m * P:m * P + rows_of(m)],
                                       w_sb[:, 1, k, :], start=(k == 0), stop=(k == KD - 1))
                mm.then_inc(proj_done, 1)

            def level(u, lv):
                q, k = q_t[:, u % 2], k_t[:, u % 2]
                n = (LEVELS + 1) * u + lv
                if lv < LEVELS:
                    pe.wait_ge(x_ready, LEVELS * u + lv + 1)
                for g in range(2):
                    if n >= 1:
                        pe.wait_ge(a_used, 2 * (n - 1) + g + 1)
                    for j in range(4):
                        c = slice((4 * g + j) * P, (4 * g + j + 1) * P)
                        x = xx[:, lv % 2, c] if lv < LEVELS else None
                        mm = pe.matmul(ps_a[:, g, j, :], k[:, c] if x is None else x, q[:, c] if x is None else x,
                                       start=True, stop=True)
                    mm.then_inc(a_done, 1)
                if lv in tails:
                    n = NTAIL * u + tails.index(lv)
                    r = LAST if lv == LEVELS else level_width(lv) - (NT - 1) * P
                    c = slice((NT - 1) * P, (NT - 1) * P + r)
                    if n >= 1:
                        pe.wait_ge(at_used, n)
                    x = xx[:, lv % 2, c] if lv < LEVELS else None
                    pe.matmul(ps_at[0:r, 0:r], k[:, c] if x is None else x, q[:, c] if x is None else x,
                              start=True, stop=True).then_inc(at_done, 1)

            def spread_rows(h, c):
                t0, tw = CH[c]
                if c == 0 and h == 0:
                    pe.wait_ge(a_used, 2 * (LEVELS + 1) * H)
                if c == 0 and h > 0:
                    pe.wait_ge(a_used, 2 * (LEVELS + 1) * H + 2 * h)
                if c or h:
                    pe.wait_ge(bc_a, 3 * h + c)
                    pe.wait_ge(bc_d, 3 * h + c)
                for kind in range(2):
                    mm = pe.matmul(ps_a[:, kind].rearrange("p a b -> p (a b)")[:, 0:tw], sel4[:, h, :],
                                   rows[:, kind, t0:t0 + tw], start=True, stop=True)
                mm.then_inc(bc_done, 1)

            def scores(u):
                h = u - H
                q, k = q_t[:, u % 2], k_t[:, u % 2]
                pe.wait_ge(bc_a, 3 * h + 3)
                pe.wait_ge(bc_d, 3 * h + 3)
                for g in range(2):
                    for j in range(4):
                        c = slice((4 * g + j) * P, (4 * g + j + 1) * P)
                        mm = pe.matmul(ps_a[:, g, j, :], k[:, c], q[:, c], start=True, stop=True)
                    mm.then_inc(a_done, 1)
                pe.wait_ge(at_used, NTAIL * H + h)
                c = slice((NT - 1) * P, T)
                pe.matmul(ps_at[0:LAST, 0:LAST], k[:, c], q[:, c], start=True, stop=True).then_inc(at_done, 1)

            def turn_k(u):
                src = xx[:, 0, :] if u < H else k_t[:, u % 2]
                if u < H:
                    pe.wait_ge(kx_ready, u + 1)
                for gi, (m0, n) in enumerate(groups):
                    g = KG * u + gi
                    if g:
                        pe.wait_ge(kt_used, g)
                    if gi == 0 and u:
                        pe.wait_ge(yt_used, KG * u)
                    for j in range(n):
                        r = rows_of(m0 + j)
                        t = pe.transpose(ps_t[0:r, j, :], src[:, (m0 + j) * P:(m0 + j) * P + r], ident[:])
                    t.then_inc(kt_done, 1)

            def update(u):
                pe.wait_ge(kt_used, KG * (u + 1))
                pe.wait_ge(khx_ready, u + 1)
                e = P if u < H else E
                for gi, (i0, n) in enumerate(UG):
                    g = len(UG) * u + gi
                    if g:
                        pe.wait_ge(u_used, g)
                    for i in range(i0, i0 + n):
                        lhs = kh[:, i, :] if i < NT - 1 else khx[:, i - (NT - 1), :]
                        m = min(i, NT - 1)
                        mm = pe.matmul(ps_u[:, (i - i0) * E:(i - i0) * E + e], lhs, vg[0:rows_of(m), u % 2, m, 0:e],
                                       start=True, stop=True)
                    mm.then_inc(u_done, 1)

            def outputs(u):
                e = P if u < H else E
                pe.wait_ge(u_used, len(UG) * (u + 1))
                for gi, (m0, n) in enumerate(OG):
                    g = len(OG) * u + gi
                    if g:
                        pe.wait_ge(o_used, g)
                    for m in range(m0, m0 + n):
                        r = rows_of(m)
                        o = ps_o[0:r, (m - m0) * E:(m - m0) * E + e]
                        pe.matmul(o, at[0:r, m, 0:r], vg[0:r, u % 2, m, 0:e], start=True, stop=False)
                        if m < NT - 1:
                            mm = pe.matmul(o, e1[:, m * P:(m + 1) * P], s_pr[:, m, 0:e], start=False, stop=True)
                        else:
                            pe.matmul(o, qx[:, 0, :], s_pr[:, m, 0:e], start=False, stop=False)
                            for b in range(DB):
                                mm = pe.matmul(o, qx[:, 1 + b, :], s_in[:, b, 0:e], start=False,
                                               stop=(b == DB - 1))
                    mm.then_inc(o_done, 1)

            def turn_y(u):
                pe.wait_ge(y_ready, u + 1)
                for gi, (m0, n) in enumerate(groups):
                    if gi:
                        pe.wait_ge(yt_used, KG * u + gi)
                    for j in range(n):
                        r = rows_of(m0 + j)
                        t = pe.transpose(ps_t[:, j, 0:r], sq[0:r, m0 + j, :], ident[0:r, 0:r])
                    t.then_inc(yt_done, 1)

            pe.wait_ge(init, 1)
            for i in range(NG):
                project(0, i)
            for u in range(NU):
                for i in range(NG):
                    if u + 1 < NU:
                        project(u + 1, i)
                    if u < H and 3 <= i <= 3 + LEVELS:
                        if i == 3:
                            pe.wait_ge(acts, u + 1)
                        level(u, i - 3)
                    if u >= H and 1 <= i <= 3:
                        if i == 1:
                            pe.wait_ge(acts, u + 1)
                        spread_rows(u - H, i - 1)
                    if u >= H and i == 4:
                        scores(u)
                    if i == 10:
                        turn_k(u)
                    if i == 11:
                        update(u)
                    if i == 12:
                        outputs(u)
                    if i == 14:
                        turn_y(u)

        @block.scalar
        def _(act):
            n = [0]

            def link(ins):
                n[0] += 1
                ins.then_inc(achain, 1)
                act.wait_ge(achain, n[0])

            scale = float(P) ** -0.5

            def evacuate(u, i):
                g = NG * u + i
                if i == 0 and u >= 2:
                    act.wait_ge(dve_unit, u - 1)
                act.wait_ge(proj_done, g + 1)
                if i < 6:
                    t0, tw = CH[i % 3]
                    dst = (q_t if i < 3 else k_t)[:, u % 2, t0:t0 + tw]
                    s = scale if (i < 3) == (u < H) else 1.0
                    nc.scalar.activation(dst, ps_p[:, g % 2, 0:tw], ACT.Copy, scale=s).then_inc(proj_free, 1)
                else:
                    m = i - 6
                    r = rows_of(m)
                    nc.scalar.activation(vg[0:r, u % 2, m, :].rearrange("p (two e) -> p two e", e=E)[:, :, 0:P],
                                         ps_p[0:r, g % 2, 0:2 * P].rearrange("p (two e) -> p two e", e=P),
                                         ACT.Copy).then_inc(proj_free, 1)

            act.wait_ge(init, 1)
            for i in range(NG):
                evacuate(0, i)
            for u in range(NU):
                h = u - H
                q, k = q_t[:, u % 2], k_t[:, u % 2]
                act.wait_ge(proj_free, NG * (u + 1))
                g = vg[:, u % 2, :, E:E + P]
                if u < H:
                    link(nc.scalar.activation(k, k, ACT.Sigmoid))
                    nc.scalar.activation(sq[:], g, ACT.Sigmoid).then_inc(acts, 1)
                    nc.scalar.activation(b_t[:], k, ACT.Ln, bias=lb[:, u:u + 1], scale=one_lb[:, u:u + 1]).then_inc(lf_ready, 1)
                else:
                    nc.scalar.activation(sq[:], g, ACT.Sigmoid).then_inc(acts, 1)
                for i in range(NG):
                    if u + 1 < NU:
                        evacuate(u + 1, i)
                    if u < H:
                        if i == 1:
                            act.wait_ge(b_ready, u + 1)
                            nc.scalar.activation(e1[:], b_t[:], ACT.Exp).then_inc(e1_ready, 1)
                        if 2 <= i < 2 + LEVELS:
                            lv = i - 2
                            w = level_width(lv)
                            act.wait_ge(d_ready, LEVELS * u + lv + 1)
                            nc.scalar.activation(dd[:, lv % 2, 0:w], dd[:, lv % 2, 0:w], ACT.Exp).then_inc(e_ready, 1)
                        if i == 9:
                            act.wait_ge(wm_ready, u + 1)
                            nc.scalar.activation(dd[:, 1, :], dd[:, 1, :], ACT.Exp).then_inc(w_ready, 1)
                    else:
                        if 1 <= i <= 3:
                            t0, tw = CH[i - 1]
                            act.wait_ge(bc_done, 3 * h + i)
                            nc.scalar.activation(e1[:, t0:t0 + tw], ps_a[:, 1].rearrange("p a b -> p (a b)")[:, 0:tw],
                                                 ACT.Copy).then_inc(bc_a, 1)
                        if i == 4:
                            act.wait_ge(bc_d, 3 * h + 3)
                            for m in range(NT):
                                r = rows_of(m)
                                e = nc.scalar.activation(dd[0:r, 0, m * P:m * P + r], dd[0:r, 0, m * P:m * P + r],
                                                         ACT.Exp, bias=cols[0:r, m, 0, h:h + 1])
                            e.then_inc(wm_ready, 1)
                    if i == 10:
                        for gi, (m0, nn) in enumerate(groups):
                            act.wait_ge(kt_done, KG * u + gi + 1)
                            r = rows_of(m0)
                            if u < H:
                                nc.scalar.activation(kh[0:r, m0:m0 + nn, :], ps_t[0:r, 0:nn, :], ACT.Copy).then_inc(kt_used, 1)
                            else:
                                for j in range(nn):
                                    e = nc.scalar.activation(kh[0:r, m0 + j, :], ps_t[0:r, j, :], ACT.Copy,
                                                             scale=cols[0:r, m0 + j, 1, h:h + 1])
                                e.then_inc(kt_used, 1)
                    if i == 12:
                        e = P if u < H else E
                        for gi, (m0, nn) in enumerate(OG):
                            act.wait_ge(o_done, len(OG) * u + gi + 1)
                            src = ps_o[:, 0:3 * E].rearrange("p (m e) -> p m e", e=E)
                            if m0 + nn == NT:
                                link(nc.scalar.activation(o_sb[:, m0:NT - 1, 0:e], src[:, 0:nn - 1, 0:e], ACT.Copy))
                                nc.scalar.activation(o_sb[0:LAST, NT - 1, 0:e], src[0:LAST, nn - 1, 0:e], ACT.Copy).then_inc(o_used, 1)
                            else:
                                nc.scalar.activation(o_sb[:, m0:m0 + nn, 0:e], src[:, 0:nn, 0:e], ACT.Copy).then_inc(o_used, 1)
                    if i == 13:
                        act.wait_ge(g_ready, u + 1)
                        act.wait_ge(o_used, len(OG) * (u + 1))
                        nc.scalar.activation(sq[:], o_sb[:, :, 0:P], ACT.Square).then_inc(sq_ready, 1)
                        act.wait_ge(std_in, u + 1)
                        nc.scalar.activation(st[:, 2, :], st[:, 1, :], ACT.Sqrt).then_inc(std_out, 1)
                    if i == 14:
                        for gi, (m0, nn) in enumerate(groups):
                            act.wait_ge(yt_done, KG * u + gi + 1)
                            r = rows_of(m0)
                            nc.scalar.activation(mix_t[:, u, m0 * P:m0 * P + (nn - 1) * P + r].rearrange("p (m t) -> p m t", t=r),
                                                 ps_t[:, 0:nn, 0:r], ACT.Copy).then_inc(yt_used, 1)

        @block.vector
        def _(dve):
            n = [0]

            def link(ins):
                n[0] += 1
                ins.then_inc(dchain, 1)
                dve.wait_ge(dchain, n[0])

            link(nc.vector.memset(vg[:], 0.0))
            link(nc.vector.memset(vg[:, :, :, P:P + 1], 1.0))
            link(nc.vector.memset(at[:], 0.0))
            link(nc.vector.memset(o_sb[:], 0.0))
            nc.vector.memset(s_pr[:, 0, :], 0.0).then_inc(init, 1)
            dve.wait_ge(init, 1)
            dve.wait_ge(g_in, 16)

            def halves(x, w, b):
                v = x[:, 0:w].rearrange("p (n two b) -> p n two b", two=2, b=b)
                return v[:, :, 0, :], v[:, :, 1, :]

            def differences(u, lv):
                b, w = 64 >> lv, level_width(lv)
                left, right = halves(b_t, w, b)
                dl, dr = halves(dd[:, lv % 2], w, b)
                mid = left[:, :, b - 1:b].to_broadcast([P, w // (2 * b), b])
                link(nc.vector.tensor_tensor(dl, mid, left, ALU.subtract))
                nc.vector.tensor_tensor(dr, right, mid, ALU.subtract).then_inc(d_ready, 1)
                dve.wait_ge(d_ready, LEVELS * u + lv + 1)

            def decayed(u, lv):
                b, w = 64 >> lv, level_width(lv)
                el, er = halves(dd[:, lv % 2], w, b)
                xl, xr = halves(xx[:, lv % 2], w, b)
                kl, _ = halves(k_t[:, u % 2], w, b)
                _, qr = halves(q_t[:, u % 2], w, b)
                dve.wait_ge(e_ready, LEVELS * u + lv + 1)
                link(nc.vector.tensor_tensor(xl, el, kl, ALU.mult))
                nc.vector.tensor_tensor(xr, er, qr, ALU.mult).then_inc(x_ready, 1)
                dve.wait_ge(x_ready, LEVELS * u + lv + 1)

            def keep(u, lv):
                nn = (LEVELS + 1) * u + lv
                for g in range(2):
                    dve.wait_ge(a_done, 2 * nn + g + 1)
                    nc.vector.copy_predicated(at[:, 4 * g:4 * g + 4, :],
                                              masks[:, lv, :].bitcast(U32).unsqueeze(1).to_broadcast([P, 4, P]),
                                              ps_a[:, g]).then_inc(a_used, 1)
                    dve.wait_ge(a_used, 2 * nn + g + 1)
                if lv in tails:
                    nt = NTAIL * u + tails.index(lv)
                    r = LAST if lv == LEVELS else level_width(lv) - (NT - 1) * P
                    dve.wait_ge(at_done, nt + 1)
                    nc.vector.copy_predicated(at[0:r, NT - 1, 0:r], masks[0:r, lv, 0:r].bitcast(U32),
                                              ps_at[0:r, 0:r]).then_inc(at_used, 1)
                    dve.wait_ge(at_used, nt + 1)

            for u in range(NU):
                h = u - H
                q, k = q_t[:, u % 2], k_t[:, u % 2]
                dve.wait_ge(acts, u + 1)
                g = vg[:, u % 2, :, E:E + P]
                gain = gno[:, 0 if u < H else 1, :].unsqueeze(1).to_broadcast([P, NT, P])
                if u < H:
                    link(nc.vector.tensor_tensor(g, g, sq[:], ALU.mult))
                    nc.vector.tensor_tensor(g, g, gain, ALU.mult).then_inc(g_ready, 1)
                else:
                    nc.vector.tensor_tensor(g, sq[:], gain, ALU.mult).then_inc(g_ready, 1)
                if u < H:
                    dve.wait_ge(lf_ready, u + 1)
                    link(nc.vector.tensor_scalar(k, k, -1.0, 1.0, ALU.mult, ALU.add))
                    link(nc.vector.tensor_scalar(k, k, one_lb[:, u:u + 1], None, ALU.mult))
                    nc.vector.tensor_tensor_scan(b_t[:], reset[:], b_t[:], 0.0, ALU.mult, ALU.add).then_inc(b_ready, 1)
                    dve.wait_ge(b_ready, u + 1)
                    differences(u, 0)
                    for lv in range(LEVELS):
                        if lv + 1 < LEVELS:
                            differences(u, lv + 1)
                        decayed(u, lv)
                        if lv:
                            keep(u, lv - 1)
                    keep(u, LEVELS - 1)
                    keep(u, LEVELS)
                    nb = NT - 1
                    d2 = dd[:, 1]
                    link(nc.vector.tensor_tensor(d2[:, 0:nb * P].rearrange("p (m t) -> p m t", t=P),
                                                 b_t[:, P - 1:nb * P:P].unsqueeze(2).to_broadcast([P, nb, P]),
                                                 b_t[:, 0:nb * P].rearrange("p (m t) -> p m t", t=P), ALU.subtract))
                    link(nc.vector.tensor_tensor(d2[:, nb * P:TP], b_t[:, TP - 1:TP].to_broadcast([P, PTAIL]),
                                                 b_t[:, nb * P:TP], ALU.subtract))
                    nc.vector.tensor_tensor(d2[:, TP:T].rearrange("p (b t) -> p b t", t=DT),
                                            b_t[:, TP + DT - 1:T:DT].unsqueeze(2).to_broadcast([P, DB, DT]),
                                            b_t[:, TP:T].rearrange("p (b t) -> p b t", t=DT), ALU.subtract).then_inc(wm_ready, 1)
                    dve.wait_ge(w_ready, u + 1)
                    nc.vector.tensor_tensor(xx[:, 0, :], k, d2, ALU.mult).then_inc(kx_ready, 1)
                    dve.wait_ge(e1_ready, u + 1)
                else:
                    for c, (t0, tw) in enumerate(CH):
                        dve.wait_ge(bc_done, 3 * h + c + 1)
                        src = ps_a[:, 0].rearrange("p a b -> p (a b)")
                        full = tw // P * P
                        r = nc.vector.tensor_tensor(dd[:, 0, t0:t0 + full].rearrange("p (m t) -> p m t", t=P),
                                                    src[:, 0:full].rearrange("p (m t) -> p m t", t=P),
                                                    negm[:].unsqueeze(1).to_broadcast([P, full // P, P]), ALU.add)
                        if full < tw:
                            link(r)
                            r = nc.vector.tensor_tensor(dd[0:LAST, 0, t0 + full:T], src[0:LAST, full:tw], negtail[:], ALU.add)
                        r.then_inc(bc_d, 1)
                        dve.wait_ge(bc_d, 3 * h + c + 1)
                    dve.wait_ge(wm_ready, H + h + 1)
                    base = 2 * (LEVELS + 1) * H
                    for g in range(2):
                        dve.wait_ge(a_done, base + 2 * h + g + 1)
                        nc.vector.tensor_tensor(at[:, 4 * g:4 * g + 4, :],
                                                dd[:, 0, 4 * g * P:(4 * g + 4) * P].rearrange("p (m t) -> p m t", t=P),
                                                ps_a[:, g], ALU.mult).then_inc(a_used, 1)
                    dve.wait_ge(at_done, NTAIL * H + h + 1)
                    nc.vector.tensor_tensor(at[0:LAST, NT - 1, 0:LAST], dd[0:LAST, 0, (NT - 1) * P:T],
                                            ps_at[0:LAST, 0:LAST], ALU.mult).then_inc(at_used, 1)
                    dve.wait_ge(a_used, base + 2 * h + 2)
                    dve.wait_ge(at_used, NTAIL * H + h + 1)
                    dve.wait_ge(bc_a, 3 * h + 3)
                dec = st[:, 3:5, :].rearrange("p a b -> p (a b)")
                nb = NT - 1
                link(nc.vector.tensor_copy(dec[:, 0:nb], e1[:, P - 1:nb * P:P]))
                link(nc.vector.tensor_copy(dec[:, nb:nb + 1], e1[:, TP - 1:TP]))
                link(nc.vector.tensor_copy(dec[:, nb + 1:nb + 1 + DB], e1[:, TP + DT - 1:T:DT]))
                link(nc.vector.tensor_tensor(e1[:], e1[:], q, ALU.mult))
                link(nc.vector.tensor_tensor(qx[:], e1[:, nb * P:T].unsqueeze(1).to_broadcast([P, DB + 1, LAST]), col_mask[:], ALU.mult))
                dve.wait_ge(kt_used, KG * (u + 1))
                nc.vector.tensor_tensor(khx[:], kh[0:LAST, NT - 1, :].unsqueeze(1).to_broadcast([LAST, DB + 1, P]),
                                        row_mask[:].unsqueeze(2).to_broadcast([LAST, DB + 1, P]), ALU.mult).then_inc(khx_ready, 1)
                e = P if u < H else E
                dve.wait_ge(s_ld, 16 * (u + 1))
                if u:
                    dve.wait_ge(s_out, 32 * u)
                for gi, (i0, nn) in enumerate(UG):
                    dve.wait_ge(u_done, len(UG) * u + gi + 1)
                    for i in range(i0, i0 + nn):
                        src = s_pr[:, i, 0:e] if i < NT else s_in[:, i - NT, 0:e]
                        dst = s_pr[:, i + 1, 0:e] if i < NT else s_new[:, i - NT, 0:e]
                        ins = nc.vector.scalar_tensor_tensor(out=dst, in0=src, scalar=dec[:, i:i + 1],
                                                             in1=ps_u[:, (i - i0) * E:(i - i0) * E + e],
                                                             op0=ALU.mult, op1=ALU.add)
                        if i < i0 + nn - 1:
                            link(ins)
                    ins.then_inc(u_used, 1)
                    dve.wait_ge(u_used, len(UG) * u + gi + 1)
                dve.wait_ge(sq_ready, u + 1)
                link(nc.vector.tensor_reduce(st[:, 0, :], sq[:], AX.X, ALU.add))
                if u >= H:
                    den = o_sb[:, :, P:E].rearrange("p m o -> p (m o)")
                    link(nc.vector.scalar_tensor_tensor(out=st[:, 5, :], in0=den, scalar=-1.0, in1=den, op0=ALU.mult, op1=ALU.max))
                    link(nc.vector.tensor_tensor(st[:, 5, :], st[:, 5, :], cols[:, :, 2, h], ALU.max))
                    link(nc.vector.reciprocal(st[:, 6, :], st[:, 5, :]))
                    link(nc.vector.tensor_tensor(st[:, 0, :], st[:, 0, :], st[:, 6, :], ALU.mult))
                    link(nc.vector.tensor_tensor(st[:, 0, :], st[:, 0, :], st[:, 6, :], ALU.mult))
                nc.vector.tensor_scalar(st[:, 1, :], st[:, 0, :], 1.0 / P, EPS, ALU.mult, ALU.add).then_inc(std_in, 1)
                dve.wait_ge(std_out, u + 1)
                link(nc.vector.reciprocal(st[:, 7, :], st[:, 2, :]))
                if u >= H:
                    link(nc.vector.tensor_tensor(st[:, 7, :], st[:, 7, :], st[:, 6, :], ALU.mult))
                link(nc.vector.tensor_tensor(sq[:], o_sb[:, :, 0:P], st[:, 7, :].unsqueeze(2).to_broadcast([P, NT, P]), ALU.mult))
                nc.vector.tensor_tensor(sq[:], sq[:], vg[:, u % 2, :, E:E + P], ALU.mult).then_inc(y_ready, 1)
                dve.wait_ge(yt_done, KG * (u + 1))
                nc.vector.tensor_copy(st[:, 0, :], st[:, 7, :]).then_inc(dve_unit, 1)
                dve.wait_ge(dve_unit, u + 1)


GW = TP + 2 + DB * (DT + 2)


def ffn_up(nc, tag, h2, a_t, w_up, conv, conv_state, conv_out):
    with ExitStack() as ctx:
        def sb(name, shape, dt=F32):
            return ctx.enter_context(nc.sbuf_tensor(f"{tag}_{name}", shape, dt))

        used = []

        def sem(name):
            used.append(ctx.enter_context(nc.semaphore(f"{tag}_{name}")))
            return used[-1]

        w_sb = sb("w", [P, KD, P])
        w2 = sb("w2", [P, 2, 2, KD, P], F32R)
        gate = sb("gate", [P, GW])
        cv = sb("cv", [P, GW])
        cw = sb("cw", [P, NF * 4])
        cb = sb("cb", [P, 4])
        one = sb("one", [P, P])
        cst = sb("cst", [P, NF * DB * 2])
        ost = sb("ost", [P, NF * (DB + 1) * 2])
        ps = ctx.enter_context(nc.psum_tensor(f"{tag}_ps", [P, 3, 2, 512], F32))
        w_in = sem("w_in")
        high_done = sem("high_done")
        split_done = sem("split_done")
        c_in, zeroed = sem("c_in"), sem("zeroed")
        prod_done = sem("prod_done")
        gate_out = sem("gate_out")
        coef_in = sem("coef_in")
        past_in = sem("past_in")
        conv_done = sem("conv_done")
        silu_done = sem("silu_done")
        a_done = sem("a_done")
        kept = sem("kept")
        taps = sem("taps")
        stored = sem("stored")
        ctx.callback(clear_semaphores, nc, used)
        block = ctx.enter_context(nc.Block())

        @block.sync
        def _(sp):
            sp.dma_start(w_sb[:], w_up[0:P, :]).then_inc(w_in, 16)
            sp.dma_start(cw[:], conv).then_inc(c_in, 16)
            sp.dma_start(cst[:], conv_state).then_inc(c_in, 16)
            with sp.Fori(1, 2 * NF) as u:
                sp.wait_ge(split_done, u)
                sp.dma_start(w_sb[:], w_up[bass.ds(u * P, P), :]).then_inc(w_in, 16)
            sp.wait_ge(kept, 2 * NF)
            sp.dma_start(conv_out, ost[:]).then_inc(stored, 16)
            sp.wait_ge(stored, 16)

        @block.tensor
        def _(pe):
            def one(j, first):
                for two in range(2):
                    for c, (t0, tw) in enumerate(CH):
                        if c == 0:
                            pe.wait_ge(split_done, 2 * j + two + 1)
                        if not first:
                            if two == 0:
                                pe.wait_ge(gate_out, 3 * j + c - 2)
                            else:
                                pe.wait_ge(a_done, 3 * j + c - 2)
                        for k in range(KD):
                            mm = products(pe, ps[:, c, two, 0:tw], [w2[:, two, i, k, :] for i in range(2)],
                                          [h2[:, i, k, t0:t0 + tw] for i in range(2)], k == 0, k == KD - 1)
                        mm.then_inc(prod_done, 1)

            one(0, True)
            with pe.Fori(1, NF) as j:
                one(j, False)

        @block.gpsimd
        def _(pool):
            nc.gpsimd.memset(gate[:], 0.0).then_inc(zeroed, 1)
            nc.gpsimd.memset(one[:], 1.0).then_inc(zeroed, 1)
            pool.wait_ge(zeroed, 2)

            def split(u, two, free):
                pool.wait_ge(w_in, 16 * u + 16)
                if free is not None:
                    pool.wait_ge(prod_done, free)
                nc.gpsimd.tensor_tensor(w2[:, two, 0], w_sb[:], one[:].unsqueeze(1).to_broadcast([P, KD, P]), ALU.mult).then_inc(high_done, 1)
                pool.wait_ge(high_done, u + 1)
                nc.gpsimd.tensor_tensor(w2[:, two, 1], w_sb[:], w2[:, two, 0].bitcast(F32), ALU.subtract).then_inc(split_done, 1)

            split(0, 0, None)
            split(1, 1, None)
            with pool.Fori(1, NF) as j:
                split(2 * j, 0, 6 * j - 3)
                split(2 * j + 1, 1, 6 * j)

        @block.scalar
        def _(act):
            act.wait_ge(zeroed, 2)

            def take(j, c, first):
                t0, tw = CH[c]
                act.wait_ge(prod_done, 6 * j + c + 1)
                if not first and c == 0:
                    act.wait_ge(conv_done, 3 * j)
                if not first and c == 2:
                    act.wait_ge(kept, 2 * j)
                wp = min(tw, TP - t0)
                ins = nc.scalar.activation(gate[:, 2 + t0:2 + t0 + wp], ps[:, c, 0, 0:wp], ACT.Copy)
                if wp < tw:
                    ins = nc.scalar.activation(gate[:, TP + 2:].rearrange("p (b t) -> p b t", t=DT + 2)[:, :, 2:],
                                               ps[:, c, 0, wp:tw].rearrange("p (b t) -> p b t", t=DT), ACT.Copy)
                ins.then_inc(gate_out, 1)

            def silu(j, c):
                t0 = CH[c][0]
                w = CH[c][1] if c < 2 else GW - 2 - t0
                act.wait_ge(conv_done, 3 * j + c + 1)
                nc.scalar.activation(cv[:, t0:t0 + w], cv[:, t0:t0 + w], ACT.Silu, bias=cb[:, 3:4]).then_inc(silu_done, 1)

            def block_of(j, first):
                for c in range(3):
                    take(j, c, first)
                    silu(j, c)

            block_of(0, True)
            with act.Fori(1, NF) as j:
                block_of(j, False)

        @block.vector
        def _(dve):
            dve.wait_ge(c_in, 32)
            dve.wait_ge(zeroed, 2)

            def copy(dst, src):
                return nc.vector.tensor_scalar(dst, src, 1.0, None, ALU.mult)

            def before(j):
                copy(cb[:], cw[:, bass.ds(j * 4, 4)]).then_inc(coef_in, 1)
                copy(gate[:, TP + 2:].rearrange("p (b t) -> p b t", t=DT + 2)[:, :, 0:2],
                     cst[:, bass.ds(j * DB * 2, DB * 2)].rearrange("p (b t) -> p b t", t=2)).then_inc(past_in, 1)
                dve.wait_ge(coef_in, j + 1)

            def convolve(j, c):
                n = 3 * j + c
                t0 = CH[c][0]
                w = CH[c][1] if c < 2 else GW - 2 - t0
                dve.wait_ge(gate_out, n + 1)
                if c == 2:
                    dve.wait_ge(past_in, j + 1)
                    copy(ost[:, bass.ds(j * (DB + 1) * 2, 2)], gate[:, TP:TP + 2]).then_inc(kept, 1)
                    copy(ost[:, bass.ds(j * (DB + 1) * 2 + 2, DB * 2)].rearrange("p (b t) -> p b t", t=2),
                         gate[:, TP + 2:].rearrange("p (b t) -> p b t", t=DT + 2)[:, :, DT:]).then_inc(kept, 1)
                out = cv[:, t0:t0 + w]
                nc.vector.tensor_scalar(out, gate[:, t0 + 2:t0 + 2 + w], cb[:, 2:3], None, ALU.mult).then_inc(taps, 1)
                dve.wait_ge(taps, 2 * n + 1)
                nc.vector.scalar_tensor_tensor(out=out, in0=gate[:, t0 + 1:t0 + 1 + w], scalar=cb[:, 1:2],
                                               in1=out, op0=ALU.mult, op1=ALU.add).then_inc(taps, 1)
                dve.wait_ge(taps, 2 * n + 2)
                nc.vector.scalar_tensor_tensor(out=out, in0=gate[:, t0:t0 + w], scalar=cb[:, 0:1],
                                               in1=out, op0=ALU.mult, op1=ALU.add).then_inc(conv_done, 1)

            def times_value(j, c):
                t0 = CH[c][0]
                wp = min(CH[c][1], TP - t0)
                dve.wait_ge(silu_done, 3 * j + c + 1)
                dve.wait_ge(prod_done, 6 * j + c + 4)
                ins = nc.vector.tensor_tensor(a_t[:, bass.ds(j * T + t0, wp)], cv[:, t0:t0 + wp], ps[:, c, 1, 0:wp], ALU.mult)
                if c == 2:
                    ins = nc.vector.tensor_tensor(a_t[:, bass.ds(j * T + TP, TS)].rearrange("p (b t) -> p b t", t=DT),
                                                  cv[:, TP + 2:].rearrange("p (b t) -> p b t", t=DT + 2)[:, :, 0:DT],
                                                  ps[:, c, 1, wp:wp + TS].rearrange("p (b t) -> p b t", t=DT), ALU.mult)
                ins.then_inc(a_done, 1)

            with dve.Fori(0, NF) as j:
                before(j)
                for c in range(3):
                    convolve(j, c)
                for c in range(3):
                    times_value(j, c)


LAM_INIT = 0.8 - 0.6 * math.exp(-0.3)
KL = LAST


def att_project(nc, const, h_t, w_att, w_att_i, qc_t, kc_t, v_c, qd_t, kd_t, v_d, qi_t, ki_t, w_i, outs):
    ident = const["ident"]
    rope = const["rope"]
    with ExitStack() as ctx:
        def sb(name, shape):
            return ctx.enter_context(nc.sbuf_tensor(f"p_{name}", shape, F32))

        used = []

        def sem(name):
            used.append(ctx.enter_context(nc.semaphore(f"p_{name}")))
            return used[-1]

        NR, NP_ = 4, 4
        w_sb = sb("w", [P, 2, KD, 512])
        w_si = sb("wi", [P, KD, 68])
        row = sb("row", [P, NR, 512])
        t1 = sb("t1", [P, 256])
        t2 = sb("t2", [P, 256])
        ps = ctx.enter_context(nc.psum_tensor("p_ps", [P, NP_, 512], F32))
        ps_t = ctx.enter_context(nc.psum_tensor("p_pst", [P, 4, 4, P], F32))
        w_in = [sem("w_in0"), sem("w_in1")]
        wi_in = sem("wi_in")
        prod, taken, chain, rotated, turned, placed, done_v = (
            sem(x) for x in ("prod", "taken", "chain", "rotated", "turned", "placed", "done_v"))
        stored = [sem(f"stored{i}") for i in range(NR)]
        ctx.callback(clear_semaphores, nc, used)
        block = ctx.enter_context(nc.Block())
        NGR = 6
        items = [(g, m) for g in range(NGR) for m in range(NT)]
        rot = {0: [(0, 8, 64, 8, 0)], 1: [(0, 8, 64, 8, 0)], 2: [], 3: [(0, 4, 128, 16, 8)],
               4: [(0, 1, 128, 16, 8), (256, 4, 64, 8, 0)], 5: [(0, 1, 64, 8, 0)]}
        kc_o, vc_o, kd_o, vd_o, ki_o = outs

        def stores(g, m):
            r = rows_of(m)
            rr = slice(m * P, m * P + r)
            return {1: [(kc_o[rr, :], 0, 512)], 2: [(vc_o[rr, :], 0, 512)],
                    4: [(kd_o[rr, :], 0, P), (vd_o[rr, :], P, 2 * P)], 5: [(ki_o[rr, :], 0, 64)]}.get(g, [])

        def stored_upto(n):
            return 16 * sum(len(stores(*items[i])) for i in range(n % NR, n + 1, NR))

        turns = {0: 4, 1: 4, 2: 0, 3: 4, 4: 3, 5: 1}
        with_turn = [n for n, (g, m) in enumerate(items) if turns[g]]
        turn_no = {n: i for i, n in enumerate(with_turn)}

        def put(sp, n):
            g, m = items[n]
            if stores(g, m):
                sp.wait_ge(rotated, n + 1)
            for dst, c0, c1 in stores(g, m):
                sp.dma_start(dst, row[0:rows_of(m), n % NR, c0:c1]).then_inc(stored[n % NR], 16)

        @block.sync
        def _(sp):
            for g in range(NGR):
                if g < 5:
                    if g >= 2:
                        sp.wait_ge(prod, NT * (g - 1))
                    sp.dma_start(w_sb[:, g % 2], w_att[g]).then_inc(w_in[g % 2], 16)
                if g == 0:
                    sp.dma_start(w_si[:], w_att_i).then_inc(wi_in, 16)
                if g == 0:
                    continue
                for m in range(NT):
                    n = (g - 1) * NT + m
                    put(sp, n)
            for m in range(NT):
                put(sp, (NGR - 1) * NT + m)
            for i in range(NR):
                sp.wait_ge(stored[i], stored_upto(len(items) - 1 - (len(items) - 1 - i) % NR))

        @block.tensor
        def _(pe):
            def turn(n):
                g, m = items[n]
                if not turns[g]:
                    return
                r = rows_of(m)
                t = turn_no[n]
                pe.wait_ge(rotated, n + 1)
                if t >= 4:
                    pe.wait_ge(placed, t - 3)
                c0s = {4: [0, 256, 384], 5: [0]}.get(g, [0, 128, 256, 384])
                for i, c0 in enumerate(c0s):
                    x = pe.transpose(ps_t[:, t % 4, i, 0:r], row[0:r, n % NR, c0:c0 + P], ident[0:r, 0:r])
                x.then_inc(turned, 1)

            for n, (g, m) in enumerate(items):
                r = rows_of(m)
                if m == 0:
                    if g < 5:
                        pe.wait_ge(w_in[g % 2], 16 * (g // 2 + 1))
                    else:
                        pe.wait_ge(wi_in, 16)
                if n >= NP_:
                    pe.wait_ge(taken, n - NP_ + 1)
                for k in range(KD):
                    w = w_sb[:, g % 2, k, :] if g < 5 else w_si[:, k, :]
                    mm = pe.matmul(ps[0:r, n % NP_, 0:w.shape[-1]], h_t[:, k, m * P:m * P + r], w,
                                   start=(k == 0), stop=(k == KD - 1))
                mm.then_inc(prod, 1)
                if n >= 2:
                    turn(n - 2)
            turn(len(items) - 2)
            turn(len(items) - 1)

        @block.scalar
        def _(act):
            def place(n):
                g, m = items[n]
                if not turns[g]:
                    return
                r = rows_of(m)
                t = turn_no[n]
                act.wait_ge(turned, t + 1)
                c = slice(m * P, m * P + r)
                if g in (0, 1, 3):
                    dst = {0: qc_t, 1: kc_t, 3: qd_t}[g]
                    ins = nc.scalar.activation(dst[:, :, c], ps_t[:, t % 4, :, 0:r], ACT.Copy)
                elif g == 4:
                    nc.scalar.activation(kd_t[:, c], ps_t[:, t % 4, 0, 0:r], ACT.Copy)
                    ins = nc.scalar.activation(qi_t[:, :, c], ps_t[:, t % 4, 1:3, 0:r], ACT.Copy)
                else:
                    ins = nc.scalar.activation(ki_t[:, c], ps_t[:, t % 4, 0, 0:r], ACT.Copy)
                ins.then_inc(placed, 1)

            for n, (g, m) in enumerate(items):
                r = rows_of(m)
                w = 512 if g < 5 else 68
                act.wait_ge(prod, n + 1)
                if n >= NR:
                    if stored_upto(n - NR):
                        act.wait_ge(stored[n % NR], stored_upto(n - NR))
                    act.wait_ge(done_v, n - NR + 1)
                    if n - NR in turn_no:
                        act.wait_ge(turned, turn_no[n - NR] + 1)
                nc.scalar.activation(row[0:r, n % NR, 0:w], ps[0:r, n % NP_, 0:w], ACT.Copy).then_inc(taken, 1)
                if n >= 3:
                    place(n - 3)
            for n in range(len(items) - 3, len(items)):
                place(n)

        @block.vector
        def _(dve):
            cnt = [0]

            def link(ins):
                cnt[0] += 1
                ins.then_inc(chain, 1)
                dve.wait_ge(chain, cnt[0])

            for n, (g, m) in enumerate(items):
                r = rows_of(m)
                x = row[0:r, n % NR, :]
                dve.wait_ge(taken, n + 1)
                for c0, nh, d, half, tc in rot[g]:
                    v = x[:, c0:c0 + nh * d].rearrange("p (h d) -> p h d", d=d)[:, :, 0:2 * half] \
                        .rearrange("p h (two e) -> p h two e", two=2)
                    a = t1[0:r, 0:nh * 2 * half].rearrange("p (h two e) -> p h two e", two=2, e=half)
                    b = t2[0:r, 0:nh * 2 * half].rearrange("p (h two e) -> p h two e", two=2, e=half)
                    cos = rope[0:r, m, 0, tc:tc + half].unsqueeze(1).unsqueeze(1).to_broadcast([r, nh, 2, half])
                    sin = rope[0:r, m, 1, tc:tc + half].unsqueeze(1).unsqueeze(1).to_broadcast([r, nh, 2, half])
                    link(nc.vector.tensor_tensor(a, v, cos, ALU.mult))
                    link(nc.vector.tensor_tensor(b, v, sin, ALU.mult))
                    link(nc.vector.tensor_tensor(v[:, :, 0], a[:, :, 0], b[:, :, 1], ALU.subtract))
                    link(nc.vector.tensor_tensor(v[:, :, 1], b[:, :, 0], a[:, :, 1], ALU.add))
                if g == 5:
                    link(nc.vector.tensor_scalar(w_i[0:r, m, :], x[:, 64:68], H ** -0.5, None, ALU.mult))
                    link(nc.vector.tensor_copy(x[:, 64:P], x[:, 0:64]))
                nc.vector.tensor_copy(t1[0:1, 0:1], x[0:1, 0:1]).then_inc(rotated, 1)
                if g == 2:
                    nc.vector.tensor_copy(v_c[0:r, m, :], x).then_inc(done_v, 1)
                elif g == 4:
                    nc.vector.tensor_copy(v_d[0:r, m, :], x[:, P:2 * P]).then_inc(done_v, 1)
                else:
                    nc.vector.tensor_copy(t2[0:1, 0:1], x[0:1, 0:1]).then_inc(done_v, 1)
                dve.wait_ge(done_v, n + 1)
                dve.wait_ge(rotated, n + 1)


def prompt_attention(nc, const, qc_t, kc_t, v_c, qd_t, kd_t, v_d, qi_t, ki_t, w_i, o_t, neg_lam, diff_lambda, g_diff):
    ident, neg = const["ident"], const["neg_future"]
    with ExitStack() as ctx:
        def sb(name, shape):
            return ctx.enter_context(nc.sbuf_tensor(f"a_{name}", shape, F32))

        used = []

        def sem(name):
            used.append(ctx.enter_context(nc.semaphore(f"a_{name}")))
            return used[-1]

        lamp = sb("lamp", [P, 4, DC])
        lt = sb("lt", [P, 2, DC])
        le = sb("le", [P, 4])
        gd = sb("gd", [P, P])
        p_sb = sb("p", [P, 4, TP])
        score = sb("score", [P, 2, TP])
        relu = sb("relu", [P, 2, TP])
        top = sb("top", [P, 8])
        stat = sb("stat", [P, 4, 8])
        a_t = sb("a_t", [P, 2, NT, P])
        o_sb = sb("o", [P, 2, 8, P])
        osq = sb("osq", [P, 4, P])
        ost = sb("ost", [P, 4, 4])
        ps_s = ctx.enter_context(nc.psum_tensor("a_pss", [P, 4 * 512], F32))
        ps_t = ctx.enter_context(nc.psum_tensor("a_pst", [P, 2, 4, P], F32))
        ps_o = ctx.enter_context(nc.psum_tensor("a_pso", [P, 2, 512], F32))
        loaded, lam_sum, lam_exp, chain, achain = (sem(x) for x in ("loaded", "lam_sum", "lam_exp", "chain", "achain"))
        s_done, max_done, exp_done, relu_done, relu_used, picked = (
            sem(x) for x in ("s_done", "max_done", "exp_done", "relu_done", "relu_used", "picked"))
        mixed, turned, placed, o_done, o_read, osq_done, ovar, ostd, normed = (
            sem(x) for x in ("mixed", "turned", "placed", "o_done", "o_read", "osq_done", "ovar", "ostd", "normed"))
        ctx.callback(clear_semaphores, nc, used)
        block = ctx.enter_context(nc.Block())

        def qrows(m):
            return P if m < NT - 1 else PTAIL

        def width(m):
            return min((m + 1) * P, TP)

        def indexed(m):
            return width(m) > TOPK

        units, softmaxes, relus, heads = [], [], [], []
        for m in range(NT):
            if m + 1 < NT and indexed(m + 1):
                for h in range(H):
                    units.append(("index", m + 1, h, 0))
                    relus.append(len(units) - 1)
            for h in range(H):
                for c in range(2):
                    units.append(("diff", m, h, c))
                    softmaxes.append(len(units) - 1)
            for h in range(H):
                units.append(("dsa", m, h, 0))
                softmaxes.append(len(units) - 1)
        u_no = {u: n for n, u in enumerate(units)}
        k_no = {u: n for n, u in enumerate(softmaxes)}
        r_no = {u: n for n, u in enumerate(relus)}
        turn_list = []
        for m in range(NT):
            for hd in range(8):
                nk = -(-width(m) // P)
                for b0 in range(0, nk, 4):
                    turn_list.append((m, hd, b0, min(4, nk - b0)))
                if hd == 0 and m:
                    turn_list += [(m - 1, "out", 0, 4), (m - 1, "out", 4, 4)]
        turn_list += [(NT - 1, "out", 0, 4), (NT - 1, "out", 4, 4)]
        t_no = {t[:3]: n for n, t in enumerate(turn_list)}

        def region(n):
            m = units[n][1]
            o = (n % 2) * 1024 if m < NT - 1 else 0
            return o, width(m)

        def head_scores(m, hd):
            return [u_no[("diff", m, hd, c)] for c in range(2)] if hd < 4 else [u_no[("dsa", m, hd - 4, 0)]]

        def before(m, hd):
            return (m, hd - 1) if hd else (m - 1, 7)

        @block.sync
        def _(sp):
            sp.dma_start(lamp[:], diff_lambda.partition_broadcast(P)).then_inc(loaded, 16)
            sp.dma_start(gd[:], g_diff.partition_broadcast(P)).then_inc(loaded, 16)
            sp.wait_ge(loaded, 32)

        @block.tensor
        def _(pe):
            def scores(n):
                kind, m, h, c = units[n]
                r, (o, w) = qrows(m), region(n)
                q = slice(m * P, m * P + r)
                wide = NT - 1 in (m, units[n - 1][1])
                old = n - 1 if wide else n - 2
                if old in k_no:
                    pe.wait_ge(exp_done, k_no[old] + 1)
                elif old in r_no:
                    pe.wait_ge(relu_done, r_no[old] + 1)
                mask = kind == "dsa" and indexed(m)
                d0 = w if mask or kind == "index" else m * P
                cuts = [(k0, min(512, d0 - k0)) for k0 in range(0, d0, 512)] + ([(d0, w - d0)] if d0 < w else [])
                for k0, kw in cuts:
                    out, k = ps_s[0:r, o + k0:o + k0 + kw], slice(k0, k0 + kw)
                    if kind == "dsa":
                        lhs, rhs = qd_t[:, h, q], kd_t[:, k]
                    elif kind == "diff":
                        lhs, rhs = qc_t[c * DC:(c + 1) * DC, h, q], kc_t[c * DC:(c + 1) * DC, h, k]
                    else:
                        p = slice((h % 2) * 64, (h % 2) * 64 + 64)
                        lhs, rhs = qi_t[p, h // 2, q], ki_t[p, k]
                    diag = k0 == d0
                    mm = pe.matmul(out, lhs, rhs, start=True, stop=not (mask or diag))
                    if mask or diag:
                        mm = pe.matmul(out, ident[0:r, 0:r], score[0:r, m % 2, k] if mask else neg[0:r, 0:kw], start=False, stop=True)
                mm.then_inc(s_done, 1)

            def head_out(m, hd):
                r, j = qrows(m), 8 * m + hd
                k = k_no[u_no[("diff", m, hd, 1) if hd < 4 else ("dsa", m, hd - 4, 0)]]
                pe.wait_ge(mixed, j + 1)
                nk = -(-width(m) // P)
                for b0 in range(0, nk, 4):
                    t = t_no[(m, hd, b0)]
                    if t >= 2:
                        pe.wait_ge(placed, t - 1)
                    for b in range(b0, min(b0 + 4, nk)):
                        kw = min(P, width(m) - b * P)
                        x = pe.transpose(ps_t[0:kw, t % 2, b - b0, 0:r], p_sb[0:r, (k - (hd < 4)) % 4, b * P:b * P + kw],
                                         ident[0:r, 0:r])
                    x.then_inc(turned, 1)
                return j

            def values(m, hd):
                r, j = qrows(m), 8 * m + hd
                nk = -(-width(m) // P)
                pe.wait_ge(placed, t_no[(m, hd, (nk - 1) // 4 * 4)] + 1)
                if j >= 2:
                    pe.wait_ge(o_read, j - 1)
                for b in range(nk):
                    kw = min(P, width(m) - b * P)
                    v = v_c[0:kw, b, hd * P:(hd + 1) * P] if hd < 4 else v_d[0:kw, b, :]
                    mm = pe.matmul(ps_o[0:r, j % 2, 0:P], a_t[0:kw, j % 2, b, 0:r], v, start=(b == 0), stop=(b == nk - 1))
                mm.then_inc(o_done, 1)

            def outputs(m):
                r = qrows(m)
                pe.wait_ge(normed, m + 1)
                pe.wait_ge(o_read, 8 * m + 8)
                for i0 in (0, 4):
                    t = t_no[(m, "out", i0)]
                    pe.wait_ge(placed, t - 1)
                    for i in range(4):
                        x = pe.transpose(ps_t[:, t % 2, i, 0:r], o_sb[0:r, m % 2, i0 + i, :], ident[0:r, 0:r])
                    x.then_inc(turned, 1)

            for m in range(NT):
                if m + 1 < NT and indexed(m + 1):
                    for h in range(H):
                        scores(u_no[("index", m + 1, h, 0)])
                for hd in range(8):
                    if hd == 4 and indexed(m):
                        pe.wait_ge(picked, sum(indexed(i) for i in range(m + 1)))
                    for n in head_scores(m, hd):
                        scores(n)
                    if m or hd:
                        head_out(*before(m, hd))
                        values(*before(m, hd))
                    if m and hd == 1:
                        outputs(m - 1)
            head_out(NT - 1, 7)
            values(NT - 1, 7)
            outputs(NT - 1)

        @block.scalar
        def _(act):
            cnt = [0]

            def link(ins):
                cnt[0] += 1
                ins.then_inc(achain, 1)
                act.wait_ge(achain, cnt[0])

            act.wait_ge(lam_sum, 1)
            nc.scalar.activation(le[:, 2:4], le[:, 0:2], ACT.Exp).then_inc(lam_exp, 1)

            def softmax(n):
                kind, m, h, c = units[n]
                k = k_no[n]
                r, (o, w) = qrows(m), region(n)
                act.wait_ge(max_done, k + 1)
                if k >= 4:
                    old = units[softmaxes[k - 4]]
                    hd = old[2] + (4 if old[0] == "dsa" else 0)
                    nk = -(-width(old[1]) // P)
                    act.wait_ge(turned, t_no[(old[1], hd, (nk - 1) // 4 * 4)] + 1)
                scale = DC ** -0.5 if kind == "diff" else float(P) ** -0.5
                nc.scalar.activation(p_sb[0:r, k % 4, 0:w], ps_s[0:r, o:o + w], ACT.Exp, bias=stat[0:r, k % 4, 1:2],
                                     scale=scale, accum_out=stat[0:r, k % 4, 2:3]).then_inc(exp_done, 1)

            def index(n):
                kind, m, h, c = units[n]
                r, (o, w) = qrows(m), region(n)
                i = r_no[n]
                act.wait_ge(s_done, n + 1)
                if i >= 2:
                    act.wait_ge(relu_used, i - 1)
                nc.scalar.activation(relu[0:r, i % 2, 0:w], ps_s[0:r, o:o + w], ACT.Relu, scale=64 ** -0.5).then_inc(relu_done, 1)

            def head_out(m, hd):
                r, j = qrows(m), 8 * m + hd
                nk = -(-width(m) // P)
                if j >= 2:
                    act.wait_ge(o_done, j - 1)
                for b0 in range(0, nk, 4):
                    n = min(4, nk - b0)
                    act.wait_ge(turned, t_no[(m, hd, b0)] + 1)
                    t = t_no[(m, hd, b0)]
                    kw = min(P, width(m) - b0 * P)
                    nc.scalar.activation(a_t[0:kw, j % 2, b0:b0 + n, 0:r], ps_t[0:kw, t % 2, 0:n, 0:r], ACT.Copy).then_inc(placed, 1)

            def values(m, hd):
                r, j = qrows(m), 8 * m + hd
                k = k_no[u_no[("diff", m, hd, 0) if hd < 4 else ("dsa", m, hd - 4, 0)]]
                act.wait_ge(o_done, j + 1)
                nc.scalar.activation(o_sb[0:r, m % 2, hd, :], ps_o[0:r, j % 2, 0:P], ACT.Copy,
                                     scale=stat[0:r, k % 4, 3:4]).then_inc(o_read, 1)

            def squares(m):
                r = qrows(m)
                act.wait_ge(o_read, 8 * m + 4)
                if m:
                    act.wait_ge(normed, m)
                nc.scalar.activation(osq[0:r], o_sb[0:r, m % 2, 0:4, :], ACT.Square).then_inc(osq_done, 1)

            def outputs(m):
                r = qrows(m)
                for i0 in (0, 4):
                    t = t_no[(m, "out", i0)]
                    act.wait_ge(turned, t + 1)
                    nc.scalar.activation(o_t[:, i0:i0 + 4, m * P:m * P + r], ps_t[:, t % 2, :, 0:r], ACT.Copy).then_inc(placed, 1)

            def finish(m, hd):
                r = qrows(m)
                head_out(m, hd)
                values(m, hd)
                if hd == 3:
                    squares(m)
                if hd == 5:
                    act.wait_ge(ovar, m + 1)
                    nc.scalar.activation(ost[0:r, 2, :], ost[0:r, 1, :], ACT.Sqrt).then_inc(ostd, 1)

            for m in range(NT):
                if m + 1 < NT and indexed(m + 1):
                    for h in range(H):
                        index(u_no[("index", m + 1, h, 0)])
                for hd in range(8):
                    for n in head_scores(m, hd):
                        softmax(n)
                    if m or hd:
                        finish(*before(m, hd))
                    if m and hd == 1:
                        outputs(m - 1)
            finish(NT - 1, 7)
            outputs(NT - 1)

        @block.vector
        def _(dve):
            cnt = [0]

            def link(ins):
                cnt[0] += 1
                ins.then_inc(chain, 1)
                dve.wait_ge(chain, cnt[0])

            dve.wait_ge(loaded, 32)
            lv = lamp[:].rearrange("p (two qk) d -> p two qk d", two=2)
            link(nc.vector.tensor_tensor(lt[:], lv[:, :, 0, :], lv[:, :, 1, :], ALU.mult))
            nc.vector.tensor_reduce(le[:, 0:2], lt[:], AX.X, ALU.add).then_inc(lam_sum, 1)
            dve.wait_ge(lam_exp, 1)
            link(nc.vector.tensor_tensor(neg_lam[:], le[:, 3:4], le[:, 2:3], ALU.subtract))
            link(nc.vector.tensor_scalar(neg_lam[:], neg_lam[:], LAM_INIT, None, ALU.subtract))
            link(nc.vector.tensor_scalar(gd[:], gd[:], 1.0 - LAM_INIT, None, ALU.mult))

            def maximum(n):
                kind, m, h, c = units[n]
                k = k_no[n]
                r, (o, w) = qrows(m), region(n)
                scale = DC ** -0.5 if kind == "diff" else float(P) ** -0.5
                dve.wait_ge(s_done, n + 1)
                if k >= 4:
                    old = units[softmaxes[k - 4]]
                    dve.wait_ge(o_read, 8 * old[1] + old[2] + (4 if old[0] == "dsa" else 0) + 1)
                link(nc.vector.tensor_reduce(stat[0:r, k % 4, 0:1], ps_s[0:r, o:o + w], AX.X, ALU.max))
                nc.vector.tensor_scalar(stat[0:r, k % 4, 1:2], stat[0:r, k % 4, 0:1], -scale, None, ALU.mult).then_inc(max_done, 1)

            def mix(m, hd):
                r, w, j = qrows(m), width(m), 8 * m + hd
                k = k_no[u_no[("diff", m, hd, 0) if hd < 4 else ("dsa", m, hd - 4, 0)]]
                s0 = stat[0:r, k % 4]
                dve.wait_ge(exp_done, k + 1)
                if hd >= 4:
                    nc.vector.reciprocal(s0[:, 3:4], s0[:, 2:3]).then_inc(mixed, 1)
                    dve.wait_ge(mixed, j + 1)
                    return
                s1 = stat[0:r, (k + 1) % 4]
                link(nc.vector.reciprocal(s0[:, 3:4], s0[:, 2:3]))
                dve.wait_ge(exp_done, k + 2)
                link(nc.vector.reciprocal(s1[:, 3:4], s1[:, 2:3]))
                link(nc.vector.tensor_tensor(s1[:, 4:5], s1[:, 3:4], s0[:, 2:3], ALU.mult))
                link(nc.vector.tensor_tensor(s1[:, 5:6], s1[:, 4:5], neg_lam[0:r, :], ALU.mult))
                nc.vector.scalar_tensor_tensor(out=p_sb[0:r, k % 4, 0:w], in0=p_sb[0:r, (k + 1) % 4, 0:w],
                                               scalar=s1[:, 5:6], in1=p_sb[0:r, k % 4, 0:w],
                                               op0=ALU.mult, op1=ALU.add).then_inc(mixed, 1)
                dve.wait_ge(mixed, j + 1)

            def index_sum(m):
                r, w = qrows(m), width(m)
                if indexed(m - 2):
                    dve.wait_ge(s_done, u_no[("dsa", m - 2, H - 1, 0)] + 1)
                out = score[0:r, m % 2, 0:w]
                for h in range(H):
                    i = r_no[u_no[("index", m, h, 0)]]
                    dve.wait_ge(relu_done, i + 1)
                    wh = w_i[0:r, m, h:h + 1]
                    if h == 0:
                        x = nc.vector.tensor_scalar(out, relu[0:r, i % 2, 0:w], wh, None, ALU.mult)
                    else:
                        x = nc.vector.scalar_tensor_tensor(out=out, in0=relu[0:r, i % 2, 0:w], scalar=wh,
                                                           in1=out, op0=ALU.mult, op1=ALU.add)
                    x.then_inc(relu_used, 1)
                    dve.wait_ge(relu_used, i + 1)
                diag = out[:, m * P:w]
                link(nc.vector.tensor_tensor(diag, diag, neg[0:r, 0:w - m * P], ALU.add))

            def rounds(m, n):
                x = score[0:qrows(m), m % 2, 0:width(m)]
                for _ in range(n):
                    link(nc.vector.max(top[0:qrows(m), :], x))
                    link(nc.vector.match_replace(x, top[0:qrows(m), :], x, PICKED))

            def mask(m):
                r, w = qrows(m), width(m)
                x = score[0:r, m % 2, 0:w]
                link(nc.vector.tensor_scalar(x, x, PICKED, NEG, ALU.not_equal, ALU.mult))
                nc.vector.tensor_tensor(x[:, m * P:w], x[:, m * P:w], neg[0:r, 0:w - m * P], ALU.add).then_inc(picked, 1)

            for m in range(NT):
                r = qrows(m)
                ahead = m + 1 < NT and indexed(m + 1)
                if ahead:
                    index_sum(m + 1)
                for hd in range(8):
                    for n in head_scores(m, hd):
                        maximum(n)
                    if ahead:
                        rounds(m + 1, TOPK // 64)
                    mix(m, hd)
                    if hd == 5:
                        dve.wait_ge(osq_done, m + 1)
                        link(nc.vector.tensor_reduce(ost[0:r, 0, :], osq[0:r], AX.X, ALU.add))
                        nc.vector.tensor_scalar(ost[0:r, 1, :], ost[0:r, 0, :], 1.0 / P, EPS, ALU.mult, ALU.add).then_inc(ovar, 1)
                if ahead:
                    mask(m + 1)
                dve.wait_ge(ostd, m + 1)
                link(nc.vector.reciprocal(ost[0:r, 3, :], ost[0:r, 2, :]))
                o = o_sb[0:r, m % 2, 0:4, :]
                link(nc.vector.tensor_tensor(o, o, ost[0:r, 3, :].unsqueeze(2).to_broadcast([r, 4, P]), ALU.mult))
                nc.vector.tensor_tensor(o, o, gd[0:r, :].unsqueeze(1).to_broadcast([r, 4, P]), ALU.mult).then_inc(normed, 1)
                dve.wait_ge(normed, m + 1)


def sample_queries(nc, new, qc_t, kc_t, v_c, qd_t, kd_t, v_d, qi_t, ki_t, w_i):
    with ExitStack() as ctx:
        qi_odd = ctx.enter_context(nc.sbuf_tensor("q_qi_odd", [64, 2, TS], F32))
        used = [ctx.enter_context(nc.semaphore(f"q_{n}")) for n in ("odd_in", "steps", "copied")]
        odd_in, steps, copied = used
        ctx.callback(clear_semaphores, nc, used)
        block = ctx.enter_context(nc.Block())

        @block.sync
        def _(sp):
            sp.dma_start(qi_odd[:], qi_t[64:P, :, TP:T]).then_inc(odd_in, 16)

        @block.scalar
        def _(act):
            last = slice((NT - 1) * P, T)
            for dst, src in (("kc", kc_t[:, :, last]), ("kd", kd_t[:, last]), ("ki", ki_t[0:64, last]),
                             ("vc", v_c[0:KL, NT - 1, :]), ("vd", v_d[0:KL, NT - 1, :]), ("w", w_i[0:KL, NT - 1, :])):
                nc.scalar.activation(new[dst][:], src, ACT.Copy).then_inc(copied, 1)
            act.wait_ge(copied, 6)

        @block.vector
        def _(dve):
            n = 3
            for x in ("qx", "qdx", "qix"):
                nc.vector.memset(new[x][:], 0.0).then_inc(steps, 1)
            dve.wait_ge(steps, 3)
            q_new = slice(TP, T)

            def place(dst, src):
                nc.vector.tensor_copy(dst, src.rearrange("p (b q) -> p b q", q=DT)).then_inc(steps, 1)

            for h in range(H):
                for c in range(2):
                    p = slice(64 * c, 64 * c + 64)
                    place(new["qx"][p, :, h, h * 8 + c * 4:h * 8 + c * 4 + 4], qc_t[p, h, q_new])
                place(new["qdx"][:, :, 4 * h:4 * h + 4], qd_t[:, h, q_new])
                if h % 2 == 0:
                    place(new["qix"][:, :, 4 * h:4 * h + 4], qi_t[0:64, h // 2, q_new])
                n += 3 + (h % 2 == 0)
            dve.wait_ge(odd_in, 16)
            for h in (1, 3):
                place(new["qix"][:, :, 4 * h:4 * h + 4], qi_odd[:, h // 2, :])
            dve.wait_ge(steps, n + 2)


def sample_attention(nc, const, a, new, o_t, neg_lam):
    ident = const["ident"]
    NKC = PAST + KL
    NB = NPG + 1
    QP = 4
    NQ = NPG // QP
    with ExitStack() as ctx:
        def sb(name, shape, dt=F32):
            return ctx.enter_context(nc.sbuf_tensor(f"s_{name}", shape, dt))

        used = []

        def sem(name):
            used.append(ctx.enter_context(nc.semaphore(f"s_{name}")))
            return used[-1]

        RI, RC = 8, 10
        tbl = sb("tbl", [1, DB * NPG], I32)
        ik_ring = sb("ik_ring", [64, RI, QP, P])
        ring = sb("ring", [P, RC, QP * H * P])
        qx, qdx, qix = new["qx"], new["qdx"], new["qix"]
        sc = sb("sc", [2 * 16, NKC])
        p_sb = sb("p", [P, NKC])
        rl = sb("rl", [P, NKC])
        a_t = sb("a_t", [P, NB, 4, 32])
        os_c = rl[:, 0:2 * H * P].rearrange("p (g e) -> p g e", g=2)
        o_s = rl[0:TS, 2 * H * P:4 * H * P].rearrange("p (k e) -> p k e", k=2)
        os_d = sb("os_d", [P, 2, P])
        osq = sb("osq", [TS, H, P])
        ost = sb("ost", [TS, 4, H])
        gd = sb("gd", [TS, P])
        wsel = sb("wsel", [P, 2, TS])
        wrow = sb("wrow", [P, 2, H])
        wr1 = sb("wr1", [P, 2])
        top = sb("top", [TS, 8])
        st = sb("st", [P, 8])
        half_c = sb("half_c", [P, 2])
        ps_s = ctx.enter_context(nc.psum_tensor("s_pss", [P, 5 * 512], F32))
        ps_t = ctx.enter_context(nc.psum_tensor("s_pst", [P, 2, 4, P], F32))
        ps_o = ctx.enter_context(nc.psum_tensor("s_pso", [P, 512], F32))
        names = ("t_in", "zeroed", "q_ready", "w_ps", "wsel_ready", "chain", "achain", "s_done", "relu_done", "sc_ps", "sc_out",
                 "picked", "max_done", "exp_done", "scaled", "turned", "placed", "o_done", "o_read", "sel_done", "sel_read",
                 "osq_done", "ovar", "ostd", "normed", "o_turned", "o_placed", "ik_used", "used", "c_in")
        S = {n: sem(n) for n in names}
        ik_in = [sem(f"ik_in{i}") for i in range(RI)]
        c_in = [sem(f"c_in{i}") for i in range(RC)]
        ctx.callback(clear_semaphores, nc, used)
        block = ctx.enter_context(nc.Block())
        ik_loads = [(b, c) for b in range(DB) for c in range(NQ)]
        loads = []
        for g in range(2):
            for kind in ("ck", "cv"):
                loads += [(kind, 4 * g + j, c) for j in range(4) for c in range(NQ)]
        loads += [("d", b, c) for b in range(DB) for c in range(NQ // 2)]
        at = {x: n for n, x in enumerate(loads)}
        stages = [("c", 0), ("c", 1), ("d", 0), ("d", 1)]

        def arrived(n):
            return 16 * sum(QP * (2 if loads[i][0] == "d" else 1) for i in range(n % RC, n + 1, RC))

        def fetch(eng, parity):
            eng.wait_ge(S["t_in"], 16)

            def page_of(b, i):
                e = b * NPG + i
                return eng.value_load(tbl[0:1, e:e + 1], min_val=0, max_val=a["pool_ck"].shape[0] // P - 1)

            for n in range(parity, len(ik_loads), 2):
                b, c = ik_loads[n]
                if n >= RI:
                    eng.wait_ge(S["ik_used"], n - RI + 1)
                for i in range(QP):
                    page = page_of(b, c * QP + i)
                    eng.dma_start(ik_ring[:, n % RI, i, :], a["pool_ik"][bass.ds(page * 64, 64), :]).then_inc(ik_in[n % RI], 16)
            for n in range(parity, len(loads), 2):
                kind, b, c = loads[n]
                if n >= RC:
                    eng.wait_ge(S["used"], n - RC + 1)
                pages, w, pool = (2 * QP, 2 * P, a["pool_d"]) if kind == "d" else (QP, H * P, a["pool_" + kind])
                for i in range(pages):
                    page = page_of(b, c * pages + i)
                    eng.dma_start(ring[:, n % RC, i * w:(i + 1) * w], pool[bass.ds(page * P, P), :]).then_inc(c_in[n % RC], 16)

        @block.sync
        def _(sp):
            sp.dma_start(tbl[:], a["pages"]).then_inc(S["t_in"], 16)
            sp.dma_start(gd[:], a["g_diff"].partition_broadcast(TS)).then_inc(S["c_in"], 16)
            fetch(sp, 0)

        @block.gpsimd
        def _(pool):
            nc.gpsimd.memset(a_t[:], 0.0).then_inc(S["zeroed"], 1)
            fetch(pool, 1)

        @block.tensor
        def _(pe):
            for g in range(2):
                mm = pe.matmul(ps_o[:, g * H:(g + 1) * H], const["sel_tok"][:, g, :], new["w"][:], start=True, stop=True)
            mm.then_inc(S["w_ps"], 1)

            def ik_scores(g, j, c):
                n = (4 * g + j) * NQ + c
                pe.wait_ge(ik_in[n % RI], 16 * QP * (n // RI + 1))
                out = ps_s[32 * j:32 * j + 32, c * 512:(c + 1) * 512]
                pe.matmul(out, qix[:, 4 * g + j, :], ik_ring[:, n % RI].rearrange("p i k -> p (i k)"),
                          start=True, stop=True).then_inc(S["ik_used"], 1)

            def k_scores(kind, g, j, c):
                b = 4 * g + j
                out = ps_s[32 * j:32 * j + 32, c * 512:(c + 1) * 512].rearrange("r (i k) -> r i k", k=P)
                if kind == "c":
                    n = at[("ck", b, c)]
                    pe.wait_ge(c_in[n % RC], arrived(n))
                    pages = ring[:, n % RC].rearrange("p (i h k) -> p i h k", i=QP, h=H)
                    for h in range(H):
                        mm = pe.matmul(out, qx[:, b, h, :], pages[:, :, h, :], start=(h == 0), stop=(h == H - 1))
                    mm.then_inc(S["used"], 1)
                else:
                    n = at[("d", b, c // 2)]
                    pe.wait_ge(c_in[n % RC], arrived(n))
                    pages = ring[:, n % RC].rearrange("p (i two k) -> p i two k", i=2 * QP, two=2)
                    pe.matmul(out, qdx[:, b, :], pages[:, (c % 2) * QP:(c % 2 + 1) * QP, 0, :], start=False, stop=True,
                              skip_group_check=True)

            tail = slice(PAST, NKC)
            for g in range(2):
                if g:
                    pe.wait_ge(S["relu_done"], g)
                for j in range(4):
                    for c in range(NQ):
                        ik_scores(g, j, c)
                    mm = pe.matmul(ps_s[32 * j:32 * j + 32, tail], qix[:, 4 * g + j, :], new["ki"][:], start=True, stop=True)
                mm.then_inc(S["s_done"], 1)
                pe.wait_ge(S["relu_done"], g + 1)
                pe.wait_ge(S["wsel_ready"], 1)
                if g == 0:
                    continue
                for k0 in range(0, NKC, 512):
                    kw = min(512, NKC - k0)
                    for gg, r in ((0, p_sb), (1, rl)):
                        mm = pe.matmul(ps_s[0:TS, k0:k0 + kw], wsel[:, gg, :], r[:, k0:k0 + kw], start=(gg == 0), stop=(gg == 1))
                mm.then_inc(S["sc_ps"], 1)

            for si, (kind, g) in enumerate(stages):
                if si == 0:
                    pe.wait_ge(S["sc_out"], 1)
                else:
                    pe.wait_ge(S["exp_done"], si)
                if kind == "d":
                    pe.wait_ge(S["picked"], 1)
                    for k0 in range(0, NKC, 512):
                        kw = min(512, NKC - k0)
                        pe.matmul(ps_s[:, k0:k0 + kw], const["sel_back"][:, g, :], sc[:, k0:k0 + kw],
                                  start=True, stop=False, skip_group_check=True)
                for j in range(4):
                    b = 4 * g + j
                    for c in range(NQ):
                        k_scores(kind, g, j, c)
                    out = ps_s[32 * j:32 * j + 32, tail]
                    if kind == "c":
                        for h in range(H):
                            pe.matmul(out, qx[:, b, h, :], new["kc"][:, h, :], start=(h == 0), stop=False)
                        mm = pe.matmul(out, ident[0:32, 0:32], const["negs"][:, b, :], start=False, stop=True)
                    else:
                        mm = pe.matmul(out, qdx[:, b, :], new["kd"][:], start=False, stop=True, skip_group_check=True)
                mm.then_inc(S["s_done"], 1)
                pe.wait_ge(S["scaled"], si + 1)
                for b0 in range(0, NB, 4):
                    t = 5 * si + b0 // 4
                    if t >= 2:
                        pe.wait_ge(S["placed"], t - 1)
                    for kb in range(b0, min(NB, b0 + 4)):
                        kw = min(P, NKC - kb * P)
                        x = pe.transpose(ps_t[0:kw, t % 2, kb - b0, :], p_sb[:, kb * P:kb * P + kw], ident[:])
                    x.then_inc(S["turned"], 1)
                pe.wait_ge(S["placed"], 5 * (si + 1))
                if si:
                    pe.wait_ge(S["o_read"], si)
                else:
                    pe.wait_ge(S["wsel_ready"], 1)
                e = H * P if kind == "c" else P
                for j in range(4):
                    b = 4 * g + j
                    per = QP if kind == "c" else 2 * QP
                    for kb in range(NPG):
                        n = at[("cv" if kind == "c" else "d", b, kb // per)]
                        if kind == "c":
                            if kb % per == 0:
                                pe.wait_ge(c_in[n % RC], arrived(n))
                            v = ring[:, n % RC, (kb % per) * H * P:(kb % per + 1) * H * P]
                        else:
                            v = ring[:, n % RC, (kb % per) * 2 * P + P:(kb % per + 1) * 2 * P]
                        mm = pe.matmul(ps_o[32 * j:32 * j + 32, 0:e], a_t[:, kb, j, :], v, start=(kb == 0), stop=False)
                        if kb % per == per - 1:
                            mm.then_inc(S["used"], 1)
                    mm = pe.matmul(ps_o[32 * j:32 * j + 32, 0:e], a_t[0:KL, NPG, j, :], new["vc" if kind == "c" else "vd"][:],
                                   start=False, stop=True)
                mm.then_inc(S["o_done"], 1)

            pe.wait_ge(S["o_read"], 4)
            for i, o in enumerate((os_c, os_d)):
                for h in range(H):
                    for g in range(2):
                        src = o[:, g, h * P:(h + 1) * P] if i == 0 else o[:, g, :]
                        mm = pe.matmul(ps_s[0:TS, i * 512 + h * P:i * 512 + (h + 1) * P], const["sel"][:, g, h, :], src,
                                       start=(g == 0), stop=(g == 1))
            mm.then_inc(S["sel_done"], 1)
            pe.wait_ge(S["normed"], 1)
            for i in range(8):
                x = pe.transpose(ps_t[:, i // 4, i % 4, 0:TS], o_s[:, i // 4, (i % 4) * P:(i % 4 + 1) * P], ident[0:TS, 0:TS])
            x.then_inc(S["o_turned"], 1)

        @block.scalar
        def _(act):
            for g, dst in ((0, p_sb), (1, rl)):
                act.wait_ge(S["s_done"], g + 1)
                nc.scalar.activation(dst[:], ps_s[:, 0:NKC], ACT.Relu, scale=64 ** -0.5).then_inc(S["relu_done"], 1)
            act.wait_ge(S["sc_ps"], 1)
            for si, (kind, g) in enumerate(stages):
                act.wait_ge(S["max_done"], si + 1)
                if si:
                    act.wait_ge(S["turned"], 5 * si)
                scale = DC ** -0.5 if kind == "c" else float(P) ** -0.5
                nc.scalar.activation(p_sb[:], ps_s[:, 0:NKC], ACT.Exp, bias=st[:, 1:2], scale=scale,
                                     accum_out=st[:, 2:3]).then_inc(S["exp_done"], 1)
                act.wait_ge(S["o_done"], si + 1)
                if kind == "c":
                    nc.scalar.activation(os_c[:, g, :], ps_o[:], ACT.Copy).then_inc(S["o_read"], 1)
                else:
                    nc.scalar.activation(os_d[:, g, :], ps_o[:, 0:P], ACT.Copy).then_inc(S["o_read"], 1)
            act.wait_ge(S["sel_done"], 1)
            nc.scalar.activation(o_s, ps_s[0:TS, 0:1024].rearrange("p (k e) -> p k e", k=2), ACT.Copy).then_inc(S["sel_read"], 1)
            act.wait_ge(S["sel_read"], 1)
            nc.scalar.activation(osq[:], o_s[:, 0, :], ACT.Square).then_inc(S["osq_done"], 1)
            act.wait_ge(S["ovar"], 1)
            nc.scalar.activation(ost[:, 2, :], ost[:, 1, :], ACT.Sqrt).then_inc(S["ostd"], 1)
            act.wait_ge(S["o_turned"], 1)
            nc.scalar.activation(o_t[:, :, TP:T], ps_t[:, :, :, 0:TS].rearrange("p a b t -> p (a b) t"), ACT.Copy).then_inc(S["o_placed"], 1)
            act.wait_ge(S["o_placed"], 1)

        @block.vector
        def _(dve):
            cnt = [0]

            def link(ins):
                cnt[0] += 1
                ins.then_inc(S["chain"], 1)
                dve.wait_ge(S["chain"], cnt[0])

            link(nc.vector.tensor_scalar(half_c[:, 1:2], const["second_half"][:], neg_lam[:], None, ALU.mult))
            nc.vector.tensor_tensor(half_c[:, 0:1], half_c[:, 1:2], const["first_half"][:], ALU.add).then_inc(S["q_ready"], 1)
            dve.wait_ge(S["q_ready"], 1)
            dve.wait_ge(S["w_ps"], 1)
            link(nc.vector.tensor_tensor(wrow[:], ps_o[:, 0:2 * H].rearrange("p (g h) -> p g h", g=2),
                                         const["hot"][:].unsqueeze(1).to_broadcast([P, 2, H]), ALU.mult))
            link(nc.vector.tensor_reduce(wr1[:], wrow[:], AX.X, ALU.add))
            nc.vector.tensor_tensor(wsel[:], const["sel_sum"][:], wr1[:].unsqueeze(2).to_broadcast([P, 2, TS]), ALU.mult).then_inc(S["wsel_ready"], 1)
            dve.wait_ge(S["sc_ps"], 1)
            link(nc.vector.tensor_copy(sc[:, 0:PAST], ps_s[0:TS, 0:PAST]))
            nc.vector.tensor_tensor(sc[:, PAST:NKC], ps_s[0:TS, PAST:NKC], const["neg_rows"][:], ALU.add).then_inc(S["sc_out"], 1)
            dve.wait_ge(S["sc_out"], 1)
            dve.wait_ge(S["zeroed"], 1)

            def rounds(n):
                for _ in range(n):
                    link(nc.vector.max(top[:], sc[:]))
                    link(nc.vector.match_replace(sc[:], top[:], sc[:], PICKED))

            for si, (kind, g) in enumerate(stages):
                if kind == "c":
                    rounds(TOPK // 16)
                    if g == 1:
                        link(nc.vector.tensor_scalar(sc[:], sc[:], PICKED, NEG, ALU.not_equal, ALU.mult))
                        nc.vector.tensor_tensor(sc[:, PAST:NKC], sc[:, PAST:NKC], const["neg_rows"][:], ALU.add).then_inc(S["picked"], 1)
                scale = DC ** -0.5 if kind == "c" else float(P) ** -0.5
                dve.wait_ge(S["s_done"], 2 + si + 1)
                link(nc.vector.tensor_reduce(st[:, 0:1], ps_s[:, 0:NKC], AX.X, ALU.max))
                nc.vector.tensor_scalar(st[:, 1:2], st[:, 0:1], -scale, None, ALU.mult).then_inc(S["max_done"], 1)
                dve.wait_ge(S["exp_done"], si + 1)
                link(nc.vector.reciprocal(st[:, 3:4], st[:, 2:3]))
                if kind == "c":
                    link(nc.vector.tensor_tensor(st[:, 3:4], st[:, 3:4], half_c[:, 0:1], ALU.mult))
                nc.vector.tensor_scalar(p_sb[:], p_sb[:], st[:, 3:4], None, ALU.mult).then_inc(S["scaled"], 1)
                if si:
                    dve.wait_ge(S["o_done"], si)
                for b0 in range(0, NB, 4):
                    t = 5 * si + b0 // 4
                    n = min(4, NB - b0)
                    kw = min(P, NKC - b0 * P)
                    dve.wait_ge(S["turned"], t + 1)
                    src = ps_t[0:kw, t % 2, 0:n, :]
                    if kind == "c":
                        x = [nc.vector.tensor_reduce(a_t[0:kw, b0 + i, :, 0:16].rearrange("k j (h q) -> k j h q", q=DT),
                                                     ps_t[0:kw, t % 2, i, :].rearrange("k (j h c q) -> k j h q c", j=4, h=H, c=2),
                                                     AX.X, ALU.add) for i in range(n)][-1]
                    else:
                        x = nc.vector.tensor_copy(a_t[0:kw, b0:b0 + n].rearrange("k b j r -> k b (j r)"), src)
                    x.then_inc(S["placed"], 1)
                dve.wait_ge(S["placed"], 5 * (si + 1))
            dve.wait_ge(S["c_in"], 16)
            link(nc.vector.tensor_scalar(gd[:], gd[:], 1.0 - LAM_INIT, None, ALU.mult))
            dve.wait_ge(S["osq_done"], 1)
            link(nc.vector.tensor_reduce(ost[:, 0, :], osq[:], AX.X, ALU.add))
            nc.vector.tensor_scalar(ost[:, 1, :], ost[:, 0, :], 1.0 / P, EPS, ALU.mult, ALU.add).then_inc(S["ovar"], 1)
            dve.wait_ge(S["ostd"], 1)
            link(nc.vector.reciprocal(ost[:, 3, :], ost[:, 2, :]))
            o = o_s[:, 0, :].rearrange("t (h e) -> t h e", e=P)
            link(nc.vector.tensor_tensor(o, o, ost[:, 3, :].unsqueeze(2).to_broadcast([TS, H, P]), ALU.mult))
            nc.vector.tensor_tensor(o, o, gd[:].unsqueeze(1).to_broadcast([TS, H, P]), ALU.mult).then_inc(S["normed"], 1)


def attention_mixer(nc, sb, load_consts, const, a, h_t):
    with ExitStack() as st:
        new_shapes = {"qx": [P, DB, H, 32], "qdx": [P, DB, 32], "qix": [64, DB, 32], "kc": [P, H, KL], "kd": [P, KL],
                      "ki": [64, KL], "vc": [KL, H * P], "vd": [KL, P], "w": [KL, H]}
        new = {n: sb(st, f"new_{n}", shape) for n, shape in new_shapes.items()}
        neg_lam = sb(st, "neg_lam", [P, 1])
        with ExitStack() as qs:
            def t(name, shape):
                return sb(qs, name, shape)

            kc_t, qd_t, qc_t = t("kc_t", [P, H, T]), t("qd_t", [P, H, T]), t("qc_t", [P, H, T])
            kd_t, ki_t, qi_t = t("kd_t", [P, T]), t("ki_t", [P, T]), t("qi_t", [P, 2, T])
            v_c, v_d, w_i = t("v_c", [P, NT, 512]), t("v_d", [P, NT, P]), t("w_i", [P, NT, H])
            with ExitStack() as rt:
                rc = dict(const, **load_consts(rt, "rope", ["rope"]))
                att_project(nc, rc, h_t, a["w_att"], a["w_att_i"], qc_t, kc_t, v_c, qd_t, kd_t, v_d, qi_t, ki_t, w_i,
                            (a["kc"], a["vc"], a["kd"], a["vd"], a["ki"]))
            o_t = h_t
            with ExitStack() as rt:
                rc = dict(const, **load_consts(rt, "prompt", ["neg_future"]))
                prompt_attention(nc, rc, qc_t, kc_t, v_c, qd_t, kd_t, v_d, qi_t, ki_t, w_i, o_t, neg_lam, a["diff_lambda"],
                                 a["g_diff"])
            sample_queries(nc, new, qc_t, kc_t, v_c, qd_t, kd_t, v_d, qi_t, ki_t, w_i)
        with ExitStack() as rt:
            rc = dict(const, **load_consts(rt, "sample", ["sel", "sel_sum", "sel_tok", "sel_back", "hot", "negs", "neg_rows",
                                                          "first_half", "second_half"]))
            sample_attention(nc, rc, a, new, o_t, neg_lam)


def build(nc, a):
    x_mid = nc.dram_tensor("x_mid", (T, D), F32, kind="Internal").ap()
    with ExitStack() as ctx:
        def sb(stack, name, shape, dtype=F32, side=None):
            return stack.enter_context(nc.sbuf_tensor(name, shape, dtype, side=side))

        def load_consts(stack, tag, names):
            tiles = {n: sb(stack, f"c_{n}", list(a[n].shape)) for n in names}
            done = stack.enter_context(nc.semaphore(f"{tag}_consts"))
            with nc.Block() as block:
                @block.sync
                def _(sp):
                    for n in names:
                        sp.dma_start(tiles[n][:], a[n]).then_inc(done, 16)
                    sp.wait_ge(done, 16 * len(names))
            clear_semaphores(nc, [done])
            return tiles

        const = load_consts(ctx, "all", ["ident"])
        gain = a["gains_row"]
        gain_c = a["gains_col"]
        h_mem, mid_mem = ExitStack(), ExitStack()

        h_t = sb(h_mem, "h_t0", [P, KD, T])
        project_add_norm(nc, "n0", const, a["x"], None, 0, None, None, None, gain_c[0, 0], h_t)
        mix_t = sb(mid_mem, "mix_t", [P, KD, T], side="right")
        with ExitStack() as rt:
            names = ["level_masks", "neg_upper", "neg_tail", "row_mask", "col_mask", "reset", "sel4"]
            rc = dict(const, **load_consts(rt, "rec", names))
            rows = sb(rt, "rows", [H, 2, T])
            cols = sb(rt, "cols", [P, NT, 3, H])
            lb, one_lb = sb(rt, "lb", [P, H]), sb(rt, "one_lb", [P, H])
            gate_rows(nc, rc, h_t, a["w_gates"], a["b_gates"], a["m0"], a["lb_logits"], rows, cols, lb, one_lb,
                      a["m_new"])
            recurrent_mixers(nc, rc, h_t, mix_t, a["w_rec"], a["state_a"], a["state_b"], rows, cols, lb, one_lb,
                             a["g_rec"], a["new_a"], a["new_b"])
        h_mem.close()
        h2 = sb(h_mem, "h2_0", [P, 2, KD, T], F32R)
        project_add_norm(nc, "r0", const, a["x"], lambda k, t0, n: mix_t[:, k, t0:t0 + n], KD, a["w_out_rec"],
                         gain[0, 1], x_mid, gain_c[0, 2], h2, parts=True)
        mid_mem.close()
        a_t = sb(mid_mem, "a_t0", [P, NF * T], side="right")
        ffn_up(nc, "f0", h2, a_t, a["w_up"][0], a["conv"][0], a["conv_state"][0], a["conv_new"][0])
        h_mem.close()
        h_t = sb(h_mem, "h_t1", [P, KD, T])
        project_add_norm(nc, "d0", const, x_mid, lambda k, t0, n: a_t[:, k * T + t0:k * T + t0 + n], NF, a["w_down"][0],
                         gain[0, 3], x_mid, gain_c[1, 0], h_t)
        mid_mem.close()

        attention_mixer(nc, sb, load_consts, const, a, h_t)
        h2 = sb(mid_mem, "h2_1", [P, 2, KD, T], F32R, side="right")
        project_add_norm(nc, "r1", const, x_mid, lambda k, t0, n: h_t[:, k, t0:t0 + n], KD, a["w_out_att"],
                         gain[1, 1], x_mid, gain_c[1, 2], h2, parts=True)
        h_mem.close()
        a_t = sb(h_mem, "a_t1", [P, NF * T])
        ffn_up(nc, "f1", h2, a_t, a["w_up"][1], a["conv"][1], a["conv_state"][1], a["conv_new"][1])
        mid_mem.close()
        project_add_norm(nc, "d1", const, x_mid, lambda k, t0, n: a_t[:, k * T + t0:k * T + t0 + n], NF, a["w_down"][1],
                         gain[1, 3], a["y"], None, None)
        h_mem.close()




def shape_tables():
    i = np.arange(P)
    s, t = i[:, None], i[None, :]
    masks = np.zeros((P, LEVELS + 1, P), np.float32)
    for lv in range(LEVELS):
        b = 64 >> lv
        masks[:, lv, :] = (s // (2 * b) == t // (2 * b)) & (s % (2 * b) < b) & (t % (2 * b) >= b)
    masks[:, LEVELS, :] = s == t
    tail = np.concatenate([np.zeros(PTAIL, int), 1 + np.arange(TS) // DT])
    r = np.arange(LAST)
    ok = (tail[:, None] == tail[None, :]) & (r[:, None] <= r[None, :])
    starts = np.ones(T, np.float32)
    starts[0:TP:P] = 0
    starts[TP::DT] = 0
    n = np.arange(DB + 1)
    sel4 = np.zeros((H, H, P), np.float32)
    sel4[np.arange(H), np.arange(H)] = 1
    pos = np.concatenate([np.arange(TP), np.tile(PAST + np.arange(DT), DB)]).astype(np.float32)
    rope = np.zeros((NT * P, 2, 24), np.float32)
    for off, d in ((0, 64), (8, 128)):
        rr = d // 4
        inv = np.float32(500000.0) ** (-np.arange(rr // 2, dtype=np.float32) * np.float32(2.0) / np.float32(rr))
        ang = (pos[:, None] * inv.astype(np.float32)[None, :]).astype(np.float32).astype(np.float64)
        rope[:T, 0, off:off + rr // 2] = np.cos(ang)
        rope[:T, 1, off:off + rr // 2] = np.sin(ang)
    row = np.arange(P)
    j, hq = row // 32, row % 32
    used = hq < 16
    sel = np.zeros((P, 2, H, TS), np.float32)
    for g in range(2):
        for rr in row[used]:
            sel[rr, g, hq[rr] // 4, (4 * g + j[rr]) * DT + hq[rr] % 4] = 1
    sel_sum = sel.sum(2)
    tok = np.zeros((LAST, 2, P), np.float32)
    tok[PTAIL:] = sel_sum.transpose(2, 1, 0)
    hot = np.zeros((P, H), np.float32)
    hot[row[used], hq[used] // 4] = 1
    q = np.arange(32) % DT
    negs = np.full((32, DB, LAST), NEG, np.float32)
    for b in range(DB):
        for c in range(DT):
            negs[q >= c, b, PTAIL + DT * b + c] = 0
    return {
        "ident": np.eye(P, dtype=np.float32),
        "level_masks": masks,
        "neg_upper": np.where(s <= t, 0, NEG).astype(np.float32),
        "neg_tail": np.where(ok, 0, NEG).astype(np.float32),
        "row_mask": (tail[:, None] == n[None, :]).astype(np.float32),
        "col_mask": np.broadcast_to((n[:, None] == tail[None, :]).astype(np.float32), (P, DB + 1, LAST)),
        "reset": np.broadcast_to(starts, (P, T)),
        "sel4": sel4,
        "rope": rope.reshape(NT, P, 2, 24).transpose(1, 0, 2, 3),
        "neg_future": np.where(t <= s, 0, NEG).astype(np.float32),
        "sel": sel,
        "sel_sum": sel_sum,
        "sel_tok": tok,
        "sel_back": sel_sum.transpose(2, 1, 0),
        "hot": hot,
        "negs": negs,
        "first_half": (hq % 8 < 4).astype(np.float32)[:, None],
        "second_half": (hq % 8 >= 4).astype(np.float32)[:, None],
        "neg_rows": negs[np.tile(np.arange(DT), DB), np.repeat(np.arange(DB), DT)],
    }


def kernel(**inputs):
    import concourse.bacc as _bacc
    from concourse.bass_utils import run_bass_kernel_spmd as _run

    x = {n: np.asarray(v) for n, v in inputs.items()}

    def blocks(w, n):
        return w.reshape(w.shape[0] // P, P, n, -1).transpose(2, 1, 0, 3)

    arrays = dict(shape_tables())
    arrays["x"] = np.concatenate([x["meta_tokens"], x["x_prompt"][0], x["x_sample"].reshape(TS, D)])
    arrays["gains_row"] = x["norm_gains"]
    arrays["gains_col"] = x["norm_gains"].reshape(2, 4, KD, P).transpose(0, 1, 3, 2)
    wr = x["w_in_rec"][0]
    heads = wr[:, :8 * 512].reshape(D, 8, H, P)
    arrays["w_rec"] = np.concatenate([heads[:, 0:4].transpose(2, 0, 1, 3), heads[:, 4:8].transpose(2, 0, 1, 3)]) \
        .reshape(NU, KD, P, 512).transpose(0, 2, 1, 3)
    arrays["w_gates"] = wr[:, 8 * 512:].reshape(KD, P, 2 * H).transpose(1, 0, 2)
    arrays["b_gates"] = x["b_gates_rec"][0].reshape(2 * H)
    arrays["m0"] = x["state_mlstm_m"][0].T
    arrays["lb_logits"] = x["lb_logits"].reshape(2, H, P).transpose(2, 0, 1)
    arrays["state_a"] = x["state_hgrn"][0].transpose(1, 2, 0, 3)
    arrays["state_b"] = np.concatenate([x["state_mlstm_C"][0], x["state_mlstm_n"][0][..., None]], -1).transpose(1, 2, 0, 3)
    arrays["g_rec"] = np.concatenate([x["g_norm_hgrn"], x["g_norm_mlstm"]])
    arrays["w_out_rec"] = x["w_out_rec"][0].reshape(KD, P, D).transpose(1, 0, 2)
    arrays["w_up"] = x["w_ffn_up"].reshape(2, KD, P, 2, NF, P).transpose(0, 4, 3, 2, 1, 5).reshape(2, NF * 2 * P, KD * P)
    arrays["w_down"] = x["w_ffn_down"].reshape(2, NF, P, D).transpose(0, 2, 1, 3)
    arrays["conv"] = np.concatenate([x["ffn_conv_w"], x["ffn_conv_b"][:, None]], 1).reshape(2, 4, NF, P) \
        .transpose(0, 3, 2, 1).reshape(2, P, NF * 4)
    arrays["conv_state"] = x["state_ffn_conv"].reshape(2, DB, 2, NF, P).transpose(0, 4, 3, 1, 2).reshape(2, P, NF * DB * 2)
    wa = x["w_in_att"][0]
    arrays["w_att"] = wa[:, :2560].reshape(KD, P, 5, 512).transpose(2, 1, 0, 3)
    arrays["w_att_i"] = wa[:, 2560:].reshape(KD, P, 68).transpose(1, 0, 2)
    arrays["w_out_att"] = x["w_out_att"][0].reshape(KD, P, D).transpose(1, 0, 2)
    arrays["diff_lambda"] = x["diff_lambda"][0].reshape(4 * DC)
    arrays["g_diff"] = x["g_norm_diff"][0]
    arrays["pages"] = x["page_table"].reshape(1, DB * NPG)
    npool = x["cache_diff_k"].shape[1]
    arrays["pool_ck"] = x["cache_diff_k"][0].transpose(0, 3, 2, 1).reshape(npool * P, H * P)
    arrays["pool_cv"] = x["cache_diff_v"][0].reshape(npool * P, H * P)
    arrays["pool_d"] = np.concatenate([x["cache_dsa_k"][0].transpose(0, 2, 1), x["cache_dsa_v"][0]], -1).reshape(npool * P, 2 * P)
    arrays["pool_ik"] = x["cache_idx_k"][0].transpose(0, 2, 1).reshape(npool * 64, P)
    arrays = {n: np.ascontiguousarray(v) for n, v in arrays.items()}

    nc = _bacc.Bacc("TRN2", target_bir_lowering=False, num_devices=1)
    aps = {n: nc.dram_tensor(f"in_{n}", v.shape, mybir.dt.from_np(v.dtype), kind="ExternalInput").ap()
           for n, v in arrays.items()}
    outs = {"y": (T, D), "new_a": (H, P, DB + 1, P), "new_b": (H, P, DB + 1, P + 1), "m_new": (H, DB + 1),
            "conv_new": (2, P, NF * (DB + 1) * 2), "kc": (T, 512), "vc": (T, 512), "kd": (T, P), "vd": (T, P), "ki": (T, 64)}
    for n, s in outs.items():
        aps[n] = nc.dram_tensor(f"out_{n}", s, F32, kind="ExternalOutput").ap()
    build(nc, aps)
    r = _run(nc, [{f"in_{n}": v for n, v in arrays.items()}], core_ids=[0]).results[0]
    o = {n: r[f"out_{n}"] for n in outs}
    y = o["y"]
    sa = o["new_a"].transpose(2, 0, 1, 3)
    sbn = o["new_b"].transpose(2, 0, 1, 3)
    cv = o["conv_new"].reshape(2, P, NF, DB + 1, 2).transpose(0, 3, 4, 2, 1).reshape(2, DB + 1, 2, DFF)
    m = o["m_new"].T

    def both(v, tail):
        return v[:TP].reshape((1, 1, TP) + tail), v[TP:].reshape((1, DB, DT) + tail)

    c_k, c_v = both(o["kc"], (H, P)), both(o["vc"], (H, P))
    d_k, d_v, i_k = both(o["kd"], (P,)), both(o["vd"], (P,)), both(o["ki"], (64,))
    return (y[N_META:TP].reshape(1, SEQ, D), y[TP:].reshape(DB, DT, D),
            sa[None, 0:1], sa[None, 1:], sbn[None, 0:1, ..., :P], sbn[None, 1:, ..., :P],
            sbn[None, 0:1, ..., P], sbn[None, 1:, ..., P], m[None, 0:1], m[None, 1:],
            cv[:, 0:1], cv[:, 1:], *c_k, *c_v, *d_k, *d_v, *i_k)
```

```python
import math
from contextlib import ExitStack

import numpy as np

import concourse.bass as bass
from concourse import mybir

P = 128
F32 = mybir.dt.float32
F32R = mybir.dt.float32r
U32 = mybir.dt.uint32
I32 = mybir.dt.int32
ACT = mybir.ActivationFunctionType
ALU = mybir.AluOpType
AX = mybir.AxisListType

D = 1024
KD = D // P
SEQ, N_META = 1024, 16
TP = SEQ + N_META
DB, DT = 8, 4
TS = DB * DT
T = TP + TS
NT = (T + P - 1) // P
LAST = T - (NT - 1) * P
PTAIL = TP - (NT - 1) * P
CH = [(0, 384), (384, 384), (768, T - 768)]
H = 4
DFF = 2816
NF = DFF // P
PAST, PAGE = 2048, 128
NPG = PAST // PAGE
TOPK = 256
DC = 64
EPS = 1e-6
NEG = -1e30
PICKED = -3e38


def rows_of(m):
    return P if m < NT - 1 else LAST


def products(pe, out, lhs, rhs, first, last):
    pe.matmul(out, lhs[0], rhs[0], start=first, stop=False)
    pe.matmul(out, lhs[0], rhs[1], start=False, stop=False)
    return pe.matmul(out, lhs[1], rhs[0], start=False, stop=last)


def clear_semaphores(nc, handles):
    with nc.Block() as block:
        @block.gpsimd
        def _(pool):
            for s in handles:
                pool.sem_clear(s)


TG = 3


def norm_rows(nc, tag, const, x_in, gain, h_t):
    ident = const["ident"]
    with ExitStack() as ctx:
        def sb(name, shape):
            return ctx.enter_context(nc.sbuf_tensor(f"{tag}_{name}", shape, F32))

        used = []

        def sem(name):
            used.append(ctx.enter_context(nc.semaphore(f"{tag}_{name}")))
            return used[-1]

        NX = 3
        xt = sb("xt", [P, NX, D])
        sq = sb("sq", [P, D])
        stat = sb("stat", [P, NT, 4])
        xn = sb("xn", [P, 2, D])
        gn = sb("gn", [P, KD])
        ps_t = ctx.enter_context(nc.psum_tensor(f"{tag}_pst", [P, 2, KD, P], F32))
        x_loaded = [sem(f"x_loaded{i}") for i in range(NX)]
        gain_in = sem("gain_in")
        sq_done = sem("sq_done")
        var_done = sem("var_done")
        std_done = sem("std_done")
        rs_done = sem("rs_done")
        xn_done = sem("xn_done")
        turned = sem("turned")
        h_done = sem("h_done")
        ctx.callback(clear_semaphores, nc, used)
        block = ctx.enter_context(nc.Block())

        @block.sync
        def _(sp):
            for m in range(NT):
                if m == 1:
                    sp.dma_start(gn[:], gain).then_inc(gain_in, 16)
                if m >= NX:
                    sp.wait_ge(xn_done, m - NX + 1)
                r = rows_of(m)
                sp.dma_start(xt[0:r, m % NX, :], x_in[m * P:m * P + r, :]).then_inc(x_loaded[m % NX], 16)

        @block.tensor
        def _(pe):
            for m in range(NT):
                r = rows_of(m)
                pe.wait_ge(xn_done, m + 1)
                if m >= 2:
                    pe.wait_ge(h_done, m - 1)
                for k in range(KD):
                    t = pe.transpose(ps_t[:, m % 2, k, 0:r], xn[0:r, m % 2, k * P:(k + 1) * P], ident[0:r, 0:r])
                t.then_inc(turned, 1)

        @block.scalar
        def _(act):
            def squares(m):
                r = rows_of(m)
                act.wait_ge(x_loaded[m % NX], 16 * (m // NX + 1))
                if m:
                    act.wait_ge(sq_done, m)
                nc.scalar.activation(sq[0:r, :], xt[0:r, m % NX, :], ACT.Square,
                                     accum_out=stat[0:r, m, 0:1]).then_inc(sq_done, 1)

            squares(0)
            for m in range(NT):
                r = rows_of(m)
                act.wait_ge(var_done, m + 1)
                nc.scalar.activation(stat[0:r, m, 2:3], stat[0:r, m, 1:2], ACT.Sqrt).then_inc(std_done, 1)
                if m + 1 < NT:
                    squares(m + 1)
                act.wait_ge(rs_done, m + 1)
                if m >= 2:
                    act.wait_ge(turned, m - 1)
                nc.scalar.activation(xn[0:r, m % 2, :], xt[0:r, m % NX, :], ACT.Copy,
                                     scale=stat[0:r, m, 3:4]).then_inc(xn_done, 1)

        @block.vector
        def _(dve):
            dve.wait_ge(gain_in, 16)

            def spread(m):
                r = rows_of(m)
                dve.wait_ge(turned, m + 1)
                nc.vector.tensor_tensor(h_t[:, :, m * P:m * P + r], ps_t[:, m % 2, :, 0:r],
                                        gn[:].unsqueeze(2).to_broadcast([P, KD, r]), ALU.mult).then_inc(h_done, 1)

            for m in range(NT):
                r = rows_of(m)
                dve.wait_ge(sq_done, m + 1)
                nc.vector.tensor_scalar(stat[0:r, m, 1:2], stat[0:r, m, 0:1], 1.0 / D, EPS,
                                        ALU.mult, ALU.add).then_inc(var_done, 1)
                dve.wait_ge(std_done, m + 1)
                nc.vector.reciprocal(stat[0:r, m, 3:4], stat[0:r, m, 2:3]).then_inc(rs_done, 1)
                if m >= 1:
                    spread(m - 1)
            spread(NT - 1)


def project_add_norm(nc, tag, const, x_in, act_t, kb, w_dram, gain_post, x_out, gain_next, h_t, parts=False, depth=3):
    ident = const["ident"]
    with ExitStack() as ctx:
        def sb(name, shape, dt=F32):
            return ctx.enter_context(nc.sbuf_tensor(f"{tag}_{name}", shape, dt))

        used = []

        def sem(name):
            used.append(ctx.enter_context(nc.semaphore(f"{tag}_{name}")))
            return used[-1]

        NX = 3
        NG = NT // TG
        STEPS = NG * kb
        w_sb = sb("w", [P, 2, D])
        w2 = sb("w2", [P, depth, 2, D], F32R)
        l2 = sb("l2", [P, depth, 2, TG * P], F32R)
        xt = sb("xt", [P, NX, D])
        sq = sb("sq", [P, D])
        stat = sb("stat", [P, NT, 8])
        yt = sb("yt", [P, TG, D])
        gp = sb("gp", [P, D])
        ps_y = ctx.enter_context(nc.psum_tensor(f"{tag}_psy", [P, TG, D], F32))
        if h_t is not None:
            xn = sb("xn", [P, 2, D])
            gn = sb("gn", [P, KD])
            whole = sb("whole", [P, KD, P]) if parts else None
            ps_t = ctx.enter_context(nc.psum_tensor(f"{tag}_pst", [P, KD, P], F32))
        w_in = [sem(f"w_in{i}") for i in range(2)]
        w_high = sem("w_high")
        w_split = sem("w_split")
        l_high = sem("l_high")
        l_split = sem("l_split")
        step_done = sem("step_done")
        x_loaded = [sem(f"x_loaded{i}") for i in range(NX)]
        gains_in = sem("gains_in")
        y_done = sem("y_done")
        y_read = sem("y_read")
        ysq_done = sem("ysq_done")
        yvar_done = sem("yvar_done")
        ystd_done = sem("ystd_done")
        x_new = sem("x_new")
        stored = [sem(f"stored{i}") for i in range(NX)]
        xsq_done = sem("xsq_done")
        xvar_done = sem("xvar_done")
        xstd_done = sem("xstd_done")
        xrs_done = sem("xrs_done")
        xn_done = sem("xn_done")
        turned = sem("turned")
        h_done = sem("h_done")
        dve_chain = sem("dve_chain")
        ctx.callback(clear_semaphores, nc, used)
        block = ctx.enter_context(nc.Block())

        END = STEPS + 16

        def tile_at(s, lag):
            for m in range(NT):
                if (m // TG + 1) * kb + lag + 2 * (m % TG) == s:
                    return m
            return None

        @block.sync
        def _(sp):
            sp.dma_start(w_sb[:, 0], w_dram[:, 0, :]).then_inc(w_in[0], 16)
            sp.dma_start(w_sb[:, 1], w_dram[:, 1, :]).then_inc(w_in[1], 16)
            sp.dma_start(gp[:], gain_post.partition_broadcast(P)).then_inc(gains_in, 16)
            if h_t is not None:
                sp.dma_start(gn[:], gain_next).then_inc(gains_in, 16)
            for s in range(2, END):
                if s < STEPS:
                    sp.wait_ge(w_split, s - 1)
                    sp.dma_start(w_sb[:, s % 2], w_dram[:, s % kb, :]).then_inc(w_in[s % 2], 16)
                m = tile_at(s, 1)
                if m is not None:
                    r = rows_of(m)
                    if m >= NX:
                        sp.wait_ge(stored[m % NX], 16 * (m // NX))
                        if h_t is not None:
                            sp.wait_ge(xn_done, m - NX + 1)
                    sp.dma_start(xt[0:r, m % NX, :], x_in[m * P:m * P + r, :]).then_inc(x_loaded[m % NX], 16)
                m = tile_at(s, 5)
                if m is not None:
                    r = rows_of(m)
                    sp.wait_ge(x_new, m + 1)
                    sp.dma_start(x_out[m * P:m * P + r, :], xt[0:r, m % NX, :]).then_inc(stored[m % NX], 16)
            for i in range(NX):
                sp.wait_ge(stored[i], 16 * ((NT - 1 - i) // NX + 1))

        @block.tensor
        def _(pe):
            for s in range(END):
                g, k = divmod(s, kb)
                if s < STEPS:
                    pe.wait_ge(w_split, s + 1)
                    pe.wait_ge(l_split, s + 1)
                    for t in range(TG):
                        if k == 0 and g:
                            pe.wait_ge(y_read, TG * (g - 1) + t + 1)
                        for n in range(2):
                            mm = products(pe, ps_y[:, t, n * 512:(n + 1) * 512],
                                          [l2[:, s % depth, i, t * P:(t + 1) * P] for i in range(2)],
                                          [w2[:, s % depth, i, n * 512:(n + 1) * 512] for i in range(2)], k == 0, k == kb - 1)
                        if k == kb - 1:
                            mm.then_inc(y_done, 1)
                        elif t == TG - 1:
                            mm.then_inc(step_done, 1)
                m = tile_at(s, 7)
                if h_t is not None and m is not None:
                    r = rows_of(m)
                    pe.wait_ge(xn_done, m + 1)
                    if m:
                        pe.wait_ge(h_done, m)
                    for i in range(KD):
                        x = pe.transpose(ps_t[:, i, 0:r], xn[0:r, m % 2, i * P:(i + 1) * P], ident[0:r, 0:r])
                    x.then_inc(turned, 1)

        def slot_free(eng, s):
            if s < depth:
                return
            g, k = divmod(s - depth, kb)
            if k == kb - 1:
                eng.wait_ge(y_done, TG * (g + 1))
            else:
                eng.wait_ge(step_done, g * (kb - 1) + k + 1)

        @block.gpsimd
        def _(pool):
            for s in range(STEPS):
                g, k = divmod(s, kb)
                t0 = g * TG * P
                n = min(TG * P, T - t0)
                slot_free(pool, s)
                nc.gpsimd.tensor_copy(l2[:, s % depth, 0, 0:n], act_t(k, t0, n)).then_inc(l_high, 1)
                pool.wait_ge(l_high, s + 1)
                nc.gpsimd.tensor_tensor(l2[:, s % depth, 1, 0:n], act_t(k, t0, n), l2[:, s % depth, 0, 0:n].bitcast(F32),
                                        ALU.subtract).then_inc(l_split, 1)

        @block.scalar
        def _(act):
            for s in range(END):
                if s < STEPS:
                    act.wait_ge(w_in[s % 2], 16 * (s // 2 + 1))
                    slot_free(act, s)
                    nc.scalar.activation(w2[:, s % depth, 0, :], w_sb[:, s % 2], ACT.Copy).then_inc(w_high, 1)
                if kb <= s < STEPS + kb and s % kb == depth - 2:
                    g = s // kb - 1
                    for m in range(TG * g, TG * g + TG):
                        act.wait_ge(y_done, m + 1)
                        if m >= TG:
                            act.wait_ge(x_new, m - TG + 1)
                        nc.scalar.activation(yt[0:rows_of(m), m % TG, :], ps_y[0:rows_of(m), m % TG, :],
                                             ACT.Copy).then_inc(y_read, 1)
                m = tile_at(s, 2)
                if m is not None:
                    r = rows_of(m)
                    act.wait_ge(y_read, m + 1)
                    if m:
                        act.wait_ge(ysq_done, m)
                        if h_t is not None and m > 1:
                            act.wait_ge(xsq_done, m - 1)
                    nc.scalar.activation(sq[0:r, :], yt[0:r, m % TG, :], ACT.Square,
                                         accum_out=stat[0:r, m, 0:1]).then_inc(ysq_done, 1)
                m = tile_at(s, 3)
                if m is not None:
                    r = rows_of(m)
                    act.wait_ge(yvar_done, m + 1)
                    nc.scalar.activation(stat[0:r, m, 2:3], stat[0:r, m, 1:2], ACT.Sqrt).then_inc(ystd_done, 1)
                if h_t is None:
                    continue
                m = tile_at(s, 4)
                if m is not None:
                    r = rows_of(m)
                    act.wait_ge(x_new, m + 1)
                    act.wait_ge(ysq_done, min(m + 1 + (m % TG < TG - 1), NT))
                    if m:
                        act.wait_ge(xsq_done, m)
                    nc.scalar.activation(sq[0:r, :], xt[0:r, m % NX, :], ACT.Square,
                                         accum_out=stat[0:r, m, 4:5]).then_inc(xsq_done, 1)
                m = tile_at(s, 5)
                if m is not None:
                    r = rows_of(m)
                    act.wait_ge(xvar_done, m + 1)
                    nc.scalar.activation(stat[0:r, m, 6:7], stat[0:r, m, 5:6], ACT.Sqrt).then_inc(xstd_done, 1)
                m = tile_at(s, 6)
                if m is not None:
                    r = rows_of(m)
                    act.wait_ge(xrs_done, m + 1)
                    if m >= 2:
                        act.wait_ge(turned, m - 1)
                    nc.scalar.activation(xn[0:r, m % 2, :], xt[0:r, m % NX, :], ACT.Copy,
                                         scale=stat[0:r, m, 7:8]).then_inc(xn_done, 1)

        @block.vector
        def _(dve):
            chain = [0]

            def link(ins):
                chain[0] += 1
                ins.then_inc(dve_chain, 1)
                dve.wait_ge(dve_chain, chain[0])

            for s in range(END):
                if s < STEPS:
                    dve.wait_ge(w_high, s + 1)
                    nc.vector.tensor_tensor(w2[:, s % depth, 1, :], w_sb[:, s % 2], w2[:, s % depth, 0, :].bitcast(F32),
                                            ALU.subtract).then_inc(w_split, 1)
                if s == 0:
                    dve.wait_ge(gains_in, 16 * (1 + (h_t is not None)))
                m = tile_at(s, 2)
                if m is not None:
                    r = rows_of(m)
                    dve.wait_ge(ysq_done, m + 1)
                    nc.vector.tensor_scalar(stat[0:r, m, 1:2], stat[0:r, m, 0:1], 1.0 / D, EPS,
                                            ALU.mult, ALU.add).then_inc(yvar_done, 1)
                m = tile_at(s, 3)
                if m is not None:
                    r = rows_of(m)
                    dve.wait_ge(ystd_done, m + 1)
                    link(nc.vector.reciprocal(stat[0:r, m, 3:4], stat[0:r, m, 2:3]))
                    link(nc.vector.scalar_tensor_tensor(out=yt[0:r, m % TG, :], in0=yt[0:r, m % TG, :],
                                                        scalar=stat[0:r, m, 3:4], in1=gp[0:r, :],
                                                        op0=ALU.mult, op1=ALU.mult))
                    dve.wait_ge(x_loaded[m % NX], 16 * (m // NX + 1))
                    nc.vector.tensor_tensor(xt[0:r, m % NX, :], xt[0:r, m % NX, :], yt[0:r, m % TG, :],
                                            ALU.add).then_inc(x_new, 1)
                if h_t is None:
                    continue
                m = tile_at(s, 4)
                if m is not None:
                    r = rows_of(m)
                    dve.wait_ge(xsq_done, m + 1)
                    nc.vector.tensor_scalar(stat[0:r, m, 5:6], stat[0:r, m, 4:5], 1.0 / D, EPS,
                                            ALU.mult, ALU.add).then_inc(xvar_done, 1)
                m = tile_at(s, 5)
                if m is not None:
                    r = rows_of(m)
                    dve.wait_ge(xstd_done, m + 1)
                    nc.vector.reciprocal(stat[0:r, m, 7:8], stat[0:r, m, 6:7]).then_inc(xrs_done, 1)
                m = tile_at(s, 9)
                if m is not None:
                    r = rows_of(m)
                    c = slice(m * P, m * P + r)
                    g = gn[:].unsqueeze(2).to_broadcast([P, KD, r])
                    dve.wait_ge(turned, m + 1)
                    if not parts:
                        nc.vector.tensor_tensor(h_t[:, :, c], ps_t[:, :, 0:r], g, ALU.mult).then_inc(h_done, 1)
                        continue
                    nc.vector.tensor_tensor(whole[:, :, 0:r], ps_t[:, :, 0:r], g, ALU.mult).then_inc(h_done, 1)
                    dve.wait_ge(h_done, m + 1)
                    link(nc.vector.tensor_copy(h_t[:, 0, :, c], whole[:, :, 0:r]))
                    link(nc.vector.tensor_tensor(h_t[:, 1, :, c], whole[:, :, 0:r], h_t[:, 0, :, c].bitcast(F32), ALU.subtract))


CHUNK_ENDS = [m * P + P - 1 for m in range(NT - 1)] + [TP - 1] + [TP + DT * b + DT - 1 for b in range(DB)]
LEVELS = 7
NU = 2 * H


def level_width(level):
    b = 64 >> level
    return (NT - 1) * P if b >= 16 else (TP if b >= 4 else T)


def gate_rows(nc, const, h_t, w_gates, b_gates, m0, lb_logits, rows, cols, lb, one_lb, m_out):
    ident = const["ident"]
    with ExitStack() as ctx:
        def sb(name, shape, dt=F32):
            return ctx.enter_context(nc.sbuf_tensor(f"g_{name}", shape, dt))

        used = []

        def sem(name):
            used.append(ctx.enter_context(nc.semaphore(f"g_{name}")))
            return used[-1]

        wg = sb("wg", [P, KD, 2 * H])
        bg = sb("bg", [P, 2 * H])
        m0s = sb("m0s", [H, DB])
        lg = sb("lg", [P, 2, H])
        lgx = sb("lgx", [P, 6, H])
        gc = sb("gc", [P, NT, 2 * H])
        ta = sb("ta", [P, NT, H])
        te = sb("te", [P, NT, H])
        lfc = sb("lfc", [P, NT, H])
        ir = sb("ir", [H, T])
        im = sb("im", [H, T])
        lf = sb("lf", [H, T])
        lfm = sb("lfm", [H, T])
        br = sb("br", [H, T])
        mr = sb("mr", [H, T])
        mp = sb("mp", [H, T])
        cs = sb("cs", [H, 3, T])
        ps_g = ctx.enter_context(nc.psum_tensor("g_psg", [P, NT, 2 * H], F32))
        ps_r = ctx.enter_context(nc.psum_tensor("g_psr", [H, 2, 3, 512], F32))
        ps_c = ctx.enter_context(nc.psum_tensor("g_psc", [P, NT, 3, H], F32))
        loaded, gates_done, biased, abs_done, exp_done, ln_done = (
            sem(x) for x in ("loaded", "gates_done", "biased", "abs_done", "exp_done", "ln_done"))
        lf_done, rows_done, expo_ready, rows_exp, cols_ready, cols_done = (
            sem(x) for x in ("lf_done", "rows_done", "expo_ready", "rows_exp", "cols_ready", "cols_done"))
        cols_out, lb_sub, lb_exp, chain_s, stored, achain = (
            sem(x) for x in ("cols_out", "lb_sub", "lb_exp", "chain", "stored", "achain"))
        reset = const["reset"]
        ctx.callback(clear_semaphores, nc, used)
        block = ctx.enter_context(nc.Block())

        @block.sync
        def _(sp):
            for dst, src in ((wg[:], w_gates), (bg[:], b_gates.partition_broadcast(P)), (m0s[:], m0), (lg[:], lb_logits)):
                sp.dma_start(dst, src).then_inc(loaded, 16)
            sp.wait_ge(cols_ready, 1)
            with nc.allow_non_contiguous_dma(reason="36 stabilisers"):
                sp.dma_start(m_out[:, 0:1], mr[:, TP - 1:TP]).then_inc(stored, 16)
                sp.dma_start(m_out[:, 1:1 + DB], mr[:, TP + DT - 1:T:DT]).then_inc(stored, 16)
            sp.wait_ge(stored, 32)

        @block.tensor
        def _(pe):
            pe.wait_ge(loaded, 64)
            for m in range(NT):
                for k in range(KD):
                    mm = pe.matmul(ps_g[0:rows_of(m), m, :], h_t[:, k, m * P:m * P + rows_of(m)], wg[:, k, :],
                                   start=(k == 0), stop=(k == KD - 1))
            mm.then_inc(gates_done, 1)
            pe.wait_ge(lf_done, 1)
            for m in range(NT):
                r = rows_of(m)
                for kind, src in ((0, gc[0:r, m, 0:H]), (1, lfc[0:r, m, :])):
                    t = pe.transpose(ps_r[:, kind, m // 4, (m % 4) * P:(m % 4) * P + r], src, ident[0:r, 0:r])
            t.then_inc(rows_done, 1)
            pe.wait_ge(cols_ready, 2)
            pe.wait_ge(rows_exp, 2)
            for m in range(NT):
                r = rows_of(m)
                for kind in range(3):
                    t = pe.transpose(ps_c[0:r, m, kind, :], cs[:, kind, m * P:m * P + r], ident[0:H, 0:H])
            t.then_inc(cols_done, 1)

        @block.scalar
        def _(act):
            act.wait_ge(lb_sub, 1)
            nc.scalar.activation(lgx[:, 1:3, :], lg[:], ACT.Exp).then_inc(lb_exp, 1)
            act.wait_ge(abs_done, 1)
            nc.scalar.activation(te[:], ta[:], ACT.Exp, scale=-1.0).then_inc(achain, 1)
            act.wait_ge(achain, 1)
            nc.scalar.activation(ta[:], te[:], ACT.Ln, bias=1.0).then_inc(ln_done, 1)
            act.wait_ge(expo_ready, 1)
            nc.scalar.activation(rows[:, 1, :], mp[:], ACT.Exp).then_inc(rows_exp, 1)
            act.wait_ge(cols_ready, 2)
            nc.scalar.activation(cs[:, 1, :], cs[:, 1, :], ACT.Exp).then_inc(achain, 1)
            nc.scalar.activation(cs[:, 2, :], mr[:], ACT.Exp, scale=-1.0).then_inc(achain, 1)
            act.wait_ge(achain, 3)
            nc.scalar.activation(te[:, 0, 0:1], ta[:, 0, 0:1], ACT.Copy).then_inc(rows_exp, 1)

        @block.vector
        def _(dve):
            n = [0]

            def link(ins):
                n[0] += 1
                ins.then_inc(chain_s, 1)
                dve.wait_ge(chain_s, n[0])

            dve.wait_ge(loaded, 64)
            link(nc.vector.tensor_tensor(lgx[:, 0, :], lg[:, 0, :], lg[:, 1, :], ALU.max))
            nc.vector.tensor_tensor(lg[:], lg[:], lgx[:, 0, :].unsqueeze(1).to_broadcast([P, 2, H]), ALU.subtract).then_inc(lb_sub, 1)
            dve.wait_ge(lb_exp, 1)
            link(nc.vector.tensor_tensor(lgx[:, 3, :], lgx[:, 1, :], lgx[:, 2, :], ALU.add))
            link(nc.vector.reciprocal(lgx[:, 4, :], lgx[:, 3, :]))
            link(nc.vector.tensor_tensor(lb[:], lgx[:, 1, :], lgx[:, 4, :], ALU.mult))
            link(nc.vector.tensor_scalar(one_lb[:], lb[:], -1.0, 1.0, ALU.mult, ALU.add))
            link(nc.vector.memset(gc[:], 0.0))
            dve.wait_ge(gates_done, 1)
            link(nc.vector.tensor_tensor(gc[:, 0:NT - 1, :], ps_g[:, 0:NT - 1, :],
                                         bg[:].unsqueeze(1).to_broadcast([P, NT - 1, 2 * H]), ALU.add))
            link(nc.vector.tensor_tensor(gc[0:LAST, NT - 1, :], ps_g[0:LAST, NT - 1, :], bg[0:LAST, :], ALU.add))
            f = gc[:, :, H:2 * H]
            nc.vector.scalar_tensor_tensor(out=ta[:], in0=f, scalar=-1.0, in1=f, op0=ALU.mult, op1=ALU.max).then_inc(abs_done, 1)
            dve.wait_ge(ln_done, 1)
            nc.vector.scalar_tensor_tensor(out=lfc[:], in0=f, scalar=0.0, in1=ta[:], op0=ALU.min, op1=ALU.subtract).then_inc(lf_done, 1)
            dve.wait_ge(rows_done, 1)
            for kind, dst in ((0, ir), (1, lf)):
                for c in range(3):
                    w = min(512, T - c * 512)
                    link(nc.vector.tensor_copy(dst[:, c * 512:c * 512 + w], ps_r[:, kind, c, 0:w]))
            starts = slice(TP, T, DT)
            link(nc.vector.tensor_tensor_scan(br[:], reset[0:H, :], lf[:], 0.0, ALU.mult, ALU.add))
            link(nc.vector.tensor_copy(im[:], ir[:]))
            link(nc.vector.tensor_copy(lfm[:], lf[:]))
            link(nc.vector.tensor_tensor(mp[:, 0:DB], lf[:, starts], m0s[:], ALU.add))
            link(nc.vector.tensor_tensor(im[:, starts], ir[:, starts], mp[:, 0:DB], ALU.max))
            link(nc.vector.memset(lfm[:, starts], NEG))
            link(nc.vector.tensor_tensor_scan(mr[:], lfm[:], im[:], 0.0, ALU.add, ALU.max))
            nc.vector.tensor_tensor(rows[:, 0, :], br[:], mr[:], ALU.subtract).then_inc(cols_ready, 1)
            dve.wait_ge(cols_ready, 1)
            full = (NT - 2) * P
            link(nc.vector.memset(mp[:, 0:P], 0.0))
            link(nc.vector.tensor_copy(mp[:, P:P + full].rearrange("h (m t) -> h m t", t=P),
                                       mr[:, P - 1:P - 1 + full:P].unsqueeze(2).to_broadcast([H, NT - 2, P])))
            link(nc.vector.tensor_copy(mp[:, (NT - 1) * P:TP], mr[:, (NT - 1) * P - 1:(NT - 1) * P].to_broadcast([H, PTAIL])))
            link(nc.vector.tensor_copy(mp[:, TP:T].rearrange("h (b t) -> h b t", t=DT),
                                       m0s[:].unsqueeze(2).to_broadcast([H, DB, DT])))
            nc.vector.tensor_tensor(mp[:], mp[:], rows[:, 0, :], ALU.add).then_inc(expo_ready, 1)
            link(nc.vector.tensor_tensor(cs[:, 0, :], ir[:], br[:], ALU.subtract))
            ra = rows[:, 0, :]
            nb = NT - 1
            link(nc.vector.tensor_tensor(cs[:, 1, 0:nb * P].rearrange("h (m t) -> h m t", t=P),
                                         cs[:, 0, 0:nb * P].rearrange("h (m t) -> h m t", t=P),
                                         ra[:, P - 1:nb * P:P].unsqueeze(2).to_broadcast([H, nb, P]), ALU.add))
            link(nc.vector.tensor_tensor(cs[:, 1, nb * P:TP], cs[:, 0, nb * P:TP],
                                         ra[:, TP - 1:TP].to_broadcast([H, PTAIL]), ALU.add))
            nc.vector.tensor_tensor(cs[:, 1, TP:T].rearrange("h (b t) -> h b t", t=DT),
                                    cs[:, 0, TP:T].rearrange("h (b t) -> h b t", t=DT),
                                    ra[:, TP + DT - 1:T:DT].unsqueeze(2).to_broadcast([H, DB, DT]), ALU.add).then_inc(cols_ready, 1)
            dve.wait_ge(cols_done, 1)
            link(nc.vector.memset(cols[:], 1.0))
            link(nc.vector.tensor_copy(cols[:, 0:nb, :, :], ps_c[:, 0:nb, :, :]))
            link(nc.vector.tensor_copy(cols[0:LAST, nb, :, :], ps_c[0:LAST, nb, :, :]))


def recurrent_mixers(nc, const, h_t, mix_t, w_units, states_a, states_b, rows, cols, lb, one_lb,
                     g_norms, new_a, new_b):
    ident = const["ident"]
    with ExitStack() as ctx:
        def sb(name, shape, dt=F32):
            return ctx.enter_context(nc.sbuf_tensor(f"r_{name}", shape, dt))

        def psum(name, shape):
            return ctx.enter_context(nc.psum_tensor(f"r_{name}", shape, F32))

        used = []

        def sem(name):
            used.append(ctx.enter_context(nc.semaphore(f"r_{name}")))
            return used[-1]

        E = P + 1
        w_sb = sb("w", [P, 2, KD, 2 * P])
        q_t = sb("q", [P, 2, T])
        k_t = sb("k", [P, 2, T])
        vg = sb("vg", [P, 2, NT, 2 * E])
        b_t = sb("b", [P, T])
        e1 = sb("e1", [P, T])
        dd = sb("dd", [P, 2, T])
        xx = sb("xx", [P, 2, T])
        at = sb("at", [P, NT, P])
        kh = sb("kh", [P, NT, P])
        khx = sb("khx", [LAST, DB + 1, P])
        qx = sb("qx", [P, DB + 1, LAST])
        s_pr = sb("s_pr", [P, NT + 1, E])
        s_in = sb("s_in", [P, DB, E])
        s_new = sb("s_new", [P, DB, E])
        o_sb = sb("o", [P, NT, E])
        sq = sb("sq", [P, NT, P])
        gno = sb("gno", [P, 2, P])
        st = sb("st", [P, 8, NT])
        masks, negm, negtail = const["level_masks"], const["neg_upper"], const["neg_tail"]
        row_mask, col_mask, reset, sel4 = const["row_mask"], const["col_mask"], const["reset"], const["sel4"]

        ps_p = psum("psp", [P, 2, 512])
        ps_a = psum("psa", [P, 2, 4, P])
        ps_at = psum("psat", [LAST, 512])
        ps_t = psum("pst", [P, 4, P])
        ps_u = psum("psu", [P, 512])
        ps_o = psum("pso", [P, 512])

        w_in = [sem("w_in0"), sem("w_in1")]
        s_ld = sem("s_ld")
        g_in, proj_done, proj_free = sem("g_in"), sem("proj_done"), sem("proj_free")
        dve_unit = sem("dve_unit")
        acts, achain, dchain = sem("acts"), sem("achain"), sem("dchain")
        lf_ready, b_ready, e1_ready, d_ready, e_ready, x_ready = (
            sem(x) for x in ("lf_ready", "b_ready", "e1_ready", "d_ready", "e_ready", "x_ready"))
        a_done, a_used, at_done, at_used = sem("a_done"), sem("a_used"), sem("at_done"), sem("at_used")
        kx_ready, kt_done, kt_used, khx_ready = sem("kx_ready"), sem("kt_done"), sem("kt_used"), sem("khx_ready")
        u_done, u_used, o_done, o_used = sem("u_done"), sem("u_used"), sem("o_done"), sem("o_used")
        sq_ready, std_in, std_out, y_ready = sem("sq_ready"), sem("std_in"), sem("std_out"), sem("y_ready")
        yt_done, yt_used, s_out, init = sem("yt_done"), sem("yt_used"), sem("s_out"), sem("init")
        bc_done, bc_a, bc_d, wm_ready, w_ready = sem("bc_done"), sem("bc_a"), sem("bc_d"), sem("wm_ready"), sem("w_ready")
        g_ready = sem("g_ready")
        ctx.callback(clear_semaphores, nc, used)
        block = ctx.enter_context(nc.Block())

        NG = 15
        KG = 3
        groups = [(0, 4), (4, 4), (8, 1)]
        UPD = NT + DB
        UG = [(i, min(3, UPD - i)) for i in range(0, UPD, 3)]
        OG = [(i, 3) for i in range(0, NT, 3)]
        tails = [i for i in range(LEVELS + 1) if i == LEVELS or level_width(i) > (NT - 1) * P]
        NTAIL = len(tails)

        @block.sync
        def _(sp):
            sp.dma_start(gno[:], g_norms.partition_broadcast(P)).then_inc(g_in, 16)

            def load_w(u, half):
                if u >= NU:
                    return
                if u:
                    sp.wait_ge(proj_done, NG * (u - 1) + (6 if half == 0 else NG))
                sp.dma_start(w_sb[:, half], w_units[u, :, :, half * 2 * P:(half + 1) * 2 * P]).then_inc(w_in[half], 16)

            def load_states(u):
                if u:
                    sp.wait_ge(o_done, len(OG) * u)
                if u < H:
                    sp.dma_start(s_in[:, :, 0:P], states_a[u]).then_inc(s_ld, 16)
                else:
                    sp.dma_start(s_in[:], states_b[u - H]).then_inc(s_ld, 16)

            load_w(0, 0)
            load_w(0, 1)
            load_states(0)
            load_w(1, 0)
            load_w(1, 1)
            for u in range(NU):
                load_w(u + 2, 0)
                sp.wait_ge(u_used, len(UG) * (u + 1))
                e, out = (P, new_a[u]) if u < H else (E, new_b[u - H])
                sp.dma_start(out[:, 0, :], s_pr[:, NT, 0:e]).then_inc(s_out, 16)
                sp.dma_start(out[:, 1:1 + DB, :], s_new[:, :, 0:e]).then_inc(s_out, 16)
                load_w(u + 2, 1)
                if u + 1 < NU:
                    load_states(u + 1)
            sp.wait_ge(s_out, 32 * NU)

        @block.tensor
        def _(pe):
            def project(u, i, midway):
                g = NG * u + i
                if i in (0, 6):
                    pe.wait_ge(w_in[i // 6], 16 * (u + 1))
                if g >= 2:
                    pe.wait_ge(proj_free, g - 1)
                for k in range(KD):
                    if k == KD // 2:
                        midway()
                    if i < 6:
                        t0, tw = CH[i % 3]
                        mm = pe.matmul(ps_p[:, g % 2, 0:tw], w_sb[:, 0, k, (i // 3) * P:(i // 3 + 1) * P],
                                       h_t[:, k, t0:t0 + tw], start=(k == 0), stop=(k == KD - 1))
                    else:
                        m = i - 6
                        mm = pe.matmul(ps_p[0:rows_of(m), g % 2, 0:2 * P], h_t[:, k, m * P:m * P + rows_of(m)],
                                       w_sb[:, 1, k, :], start=(k == 0), stop=(k == KD - 1))
                mm.then_inc(proj_done, 1)

            def level(u, lv):
                q, k = q_t[:, u % 2], k_t[:, u % 2]
                n = (LEVELS + 1) * u + lv
                if lv < LEVELS:
                    pe.wait_ge(x_ready, LEVELS * u + lv + 1)
                for g in range(2):
                    if n >= 1:
                        pe.wait_ge(a_used, 2 * (n - 1) + g + 1)
                    for j in range(4):
                        c = slice((4 * g + j) * P, (4 * g + j + 1) * P)
                        x = xx[:, lv % 2, c] if lv < LEVELS else None
                        mm = pe.matmul(ps_a[:, g, j, :], k[:, c] if x is None else x, q[:, c] if x is None else x,
                                       start=True, stop=True)
                    mm.then_inc(a_done, 1)
                if lv in tails:
                    n = NTAIL * u + tails.index(lv)
                    r = LAST if lv == LEVELS else level_width(lv) - (NT - 1) * P
                    c = slice((NT - 1) * P, (NT - 1) * P + r)
                    if n >= 1:
                        pe.wait_ge(at_used, n)
                    x = xx[:, lv % 2, c] if lv < LEVELS else None
                    pe.matmul(ps_at[0:r, 0:r], k[:, c] if x is None else x, q[:, c] if x is None else x,
                              start=True, stop=True).then_inc(at_done, 1)

            def spread_rows(h, c):
                t0, tw = CH[c]
                if c == 0 and h == 0:
                    pe.wait_ge(a_used, 2 * (LEVELS + 1) * H)
                if c == 0 and h > 0:
                    pe.wait_ge(a_used, 2 * (LEVELS + 1) * H + 2 * h)
                if c or h:
                    pe.wait_ge(bc_a, 3 * h + c)
                    pe.wait_ge(bc_d, 3 * h + c)
                for kind in range(2):
                    mm = pe.matmul(ps_a[:, kind].rearrange("p a b -> p (a b)")[:, 0:tw], sel4[:, h, :],
                                   rows[:, kind, t0:t0 + tw], start=True, stop=True)
                mm.then_inc(bc_done, 1)

            def scores(u):
                h = u - H
                q, k = q_t[:, u % 2], k_t[:, u % 2]
                pe.wait_ge(bc_a, 3 * h + 3)
                pe.wait_ge(bc_d, 3 * h + 3)
                for g in range(2):
                    for j in range(4):
                        c = slice((4 * g + j) * P, (4 * g + j + 1) * P)
                        mm = pe.matmul(ps_a[:, g, j, :], k[:, c], q[:, c], start=True, stop=True)
                    mm.then_inc(a_done, 1)
                pe.wait_ge(at_used, NTAIL * H + h)
                c = slice((NT - 1) * P, T)
                pe.matmul(ps_at[0:LAST, 0:LAST], k[:, c], q[:, c], start=True, stop=True).then_inc(at_done, 1)

            def turn_k(u):
                src = xx[:, 0, :] if u < H else k_t[:, u % 2]
                if u < H:
                    pe.wait_ge(kx_ready, u + 1)
                for gi, (m0, n) in enumerate(groups):
                    g = KG * u + gi
                    if g:
                        pe.wait_ge(kt_used, g)
                    if gi == 0 and u:
                        pe.wait_ge(yt_used, KG * u)
                    for j in range(n):
                        r = rows_of(m0 + j)
                        t = pe.transpose(ps_t[0:r, j, :], src[:, (m0 + j) * P:(m0 + j) * P + r], ident[:])
                    t.then_inc(kt_done, 1)

            def update(u, gi):
                pe.wait_ge(kt_used, KG * (u + 1))
                pe.wait_ge(khx_ready, u + 1)
                e = P if u < H else E
                i0, n = UG[gi]
                g = len(UG) * u + gi
                if g:
                    pe.wait_ge(u_used, g)
                for i in range(i0, i0 + n):
                    lhs = kh[:, i, :] if i < NT - 1 else khx[:, i - (NT - 1), :]
                    m = min(i, NT - 1)
                    mm = pe.matmul(ps_u[:, (i - i0) * E:(i - i0) * E + e], lhs, vg[0:rows_of(m), u % 2, m, 0:e],
                                   start=True, stop=True)
                mm.then_inc(u_done, 1)

            def outputs(u, gi):
                e = P if u < H else E
                pe.wait_ge(u_used, len(UG) * (u + 1))
                m0, n = OG[gi]
                g = len(OG) * u + gi
                if g:
                    pe.wait_ge(o_used, g)
                for m in range(m0, m0 + n):
                    r = rows_of(m)
                    o = ps_o[0:r, (m - m0) * E:(m - m0) * E + e]
                    pe.matmul(o, at[0:r, m, 0:r], vg[0:r, u % 2, m, 0:e], start=True, stop=False)
                    if m < NT - 1:
                        mm = pe.matmul(o, e1[:, m * P:(m + 1) * P], s_pr[:, m, 0:e], start=False, stop=True)
                    else:
                        pe.matmul(o, qx[:, 0, :], s_pr[:, m, 0:e], start=False, stop=False)
                        for b in range(DB):
                            mm = pe.matmul(o, qx[:, 1 + b, :], s_in[:, b, 0:e], start=False,
                                           stop=(b == DB - 1))
                mm.then_inc(o_done, 1)

            def turn_y(u):
                pe.wait_ge(y_ready, u + 1)
                for gi, (m0, n) in enumerate(groups):
                    if gi:
                        pe.wait_ge(yt_used, KG * u + gi)
                    for j in range(n):
                        r = rows_of(m0 + j)
                        t = pe.transpose(ps_t[:, j, 0:r], sq[0:r, m0 + j, :], ident[0:r, 0:r])
                    t.then_inc(yt_done, 1)

            pe.wait_ge(init, 1)
            for i in range(NG):
                project(0, i, lambda: None)
            for u in range(NU):
                steps = {(11 + n // 2, n % 2): (update, n) for n in range(len(UG))}
                steps[(14, 0)], steps[(14, 1)] = (outputs, 0), (outputs, 1)

                def piece(i, after):
                    if (i, after) in steps:
                        f, n = steps[(i, after)]
                        f(u, n)

                for i in range(NG):
                    if u + 1 < NU:
                        project(u + 1, i, lambda: piece(i, 0))
                    else:
                        piece(i, 0)
                    if u and i == 1:
                        turn_y(u - 1)
                    if u < H and 3 <= i <= 3 + LEVELS:
                        if i == 3:
                            pe.wait_ge(acts, u + 1)
                        level(u, i - 3)
                    if u >= H and 1 <= i <= 3:
                        if i == 1:
                            pe.wait_ge(acts, u + 1)
                        spread_rows(u - H, i - 1)
                    if u >= H and i == 4:
                        scores(u)
                    if i == 10:
                        turn_k(u)
                    piece(i, 1)
                outputs(u, 2)
            turn_y(NU - 1)

        @block.scalar
        def _(act):
            n = [0]

            def link(ins):
                n[0] += 1
                ins.then_inc(achain, 1)
                act.wait_ge(achain, n[0])

            scale = float(P) ** -0.5

            def evacuate(u, i):
                g = NG * u + i
                if i == 0 and u >= 2:
                    act.wait_ge(dve_unit, u - 1)
                act.wait_ge(proj_done, g + 1)
                if i < 6:
                    t0, tw = CH[i % 3]
                    dst = (q_t if i < 3 else k_t)[:, u % 2, t0:t0 + tw]
                    s = scale if (i < 3) == (u < H) else 1.0
                    nc.scalar.activation(dst, ps_p[:, g % 2, 0:tw], ACT.Copy, scale=s).then_inc(proj_free, 1)
                else:
                    m = i - 6
                    r = rows_of(m)
                    nc.scalar.activation(vg[0:r, u % 2, m, :].rearrange("p (two e) -> p two e", e=E)[:, :, 0:P],
                                         ps_p[0:r, g % 2, 0:2 * P].rearrange("p (two e) -> p two e", e=P),
                                         ACT.Copy).then_inc(proj_free, 1)

            act.wait_ge(init, 1)
            for i in range(NG):
                evacuate(0, i)
            for u in range(NU):
                h = u - H
                q, k = q_t[:, u % 2], k_t[:, u % 2]
                act.wait_ge(proj_free, NG * (u + 1))
                g = vg[:, u % 2, :, E:E + P]
                if u < H:
                    link(nc.scalar.activation(k, k, ACT.Sigmoid))
                    nc.scalar.activation(sq[:], g, ACT.Sigmoid).then_inc(acts, 1)
                    nc.scalar.activation(b_t[:], k, ACT.Ln, bias=lb[:, u:u + 1], scale=one_lb[:, u:u + 1]).then_inc(lf_ready, 1)
                else:
                    nc.scalar.activation(sq[:], g, ACT.Sigmoid).then_inc(acts, 1)
                for i in range(NG):
                    if u + 1 < NU:
                        evacuate(u + 1, i)
                    if u < H:
                        if i == 1:
                            act.wait_ge(b_ready, u + 1)
                            nc.scalar.activation(e1[:], b_t[:], ACT.Exp).then_inc(e1_ready, 1)
                        if 2 <= i < 2 + LEVELS:
                            lv = i - 2
                            w = level_width(lv)
                            act.wait_ge(d_ready, LEVELS * u + lv + 1)
                            nc.scalar.activation(dd[:, lv % 2, 0:w], dd[:, lv % 2, 0:w], ACT.Exp).then_inc(e_ready, 1)
                        if i == 9:
                            act.wait_ge(wm_ready, u + 1)
                            nc.scalar.activation(dd[:, 1, :], dd[:, 1, :], ACT.Exp).then_inc(w_ready, 1)
                    else:
                        if 1 <= i <= 3:
                            t0, tw = CH[i - 1]
                            act.wait_ge(bc_done, 3 * h + i)
                            nc.scalar.activation(e1[:, t0:t0 + tw], ps_a[:, 1].rearrange("p a b -> p (a b)")[:, 0:tw],
                                                 ACT.Copy).then_inc(bc_a, 1)
                        if i == 4:
                            act.wait_ge(bc_d, 3 * h + 3)
                            for m in range(NT):
                                r = rows_of(m)
                                e = nc.scalar.activation(dd[0:r, 0, m * P:m * P + r], dd[0:r, 0, m * P:m * P + r],
                                                         ACT.Exp, bias=cols[0:r, m, 0, h:h + 1])
                            e.then_inc(wm_ready, 1)
                    if i == 10:
                        for gi, (m0, nn) in enumerate(groups):
                            act.wait_ge(kt_done, KG * u + gi + 1)
                            r = rows_of(m0)
                            if u < H:
                                nc.scalar.activation(kh[0:r, m0:m0 + nn, :], ps_t[0:r, 0:nn, :], ACT.Copy).then_inc(kt_used, 1)
                            else:
                                for j in range(nn):
                                    e = nc.scalar.activation(kh[0:r, m0 + j, :], ps_t[0:r, j, :], ACT.Copy,
                                                             scale=cols[0:r, m0 + j, 1, h:h + 1])
                                e.then_inc(kt_used, 1)
                    if i == NG - 1:
                        e = P if u < H else E
                        for gi, (m0, nn) in enumerate(OG):
                            act.wait_ge(o_done, len(OG) * u + gi + 1)
                            src = ps_o[:, 0:3 * E].rearrange("p (m e) -> p m e", e=E)
                            if m0 + nn == NT:
                                link(nc.scalar.activation(o_sb[:, m0:NT - 1, 0:e], src[:, 0:nn - 1, 0:e], ACT.Copy))
                                nc.scalar.activation(o_sb[0:LAST, NT - 1, 0:e], src[0:LAST, nn - 1, 0:e], ACT.Copy).then_inc(o_used, 1)
                            else:
                                nc.scalar.activation(o_sb[:, m0:m0 + nn, 0:e], src[:, 0:nn, 0:e], ACT.Copy).then_inc(o_used, 1)
                        act.wait_ge(g_ready, u + 1)
                        act.wait_ge(o_used, len(OG) * (u + 1))
                        nc.scalar.activation(sq[:], o_sb[:, :, 0:P], ACT.Square).then_inc(sq_ready, 1)
                        act.wait_ge(std_in, u + 1)
                        nc.scalar.activation(st[:, 2, :], st[:, 1, :], ACT.Sqrt).then_inc(std_out, 1)
                        for gi, (m0, nn) in enumerate(groups):
                            act.wait_ge(yt_done, KG * u + gi + 1)
                            r = rows_of(m0)
                            nc.scalar.activation(mix_t[:, u, m0 * P:m0 * P + (nn - 1) * P + r].rearrange("p (m t) -> p m t", t=r),
                                                 ps_t[:, 0:nn, 0:r], ACT.Copy).then_inc(yt_used, 1)

        @block.vector
        def _(dve):
            n = [0]

            def link(ins):
                n[0] += 1
                ins.then_inc(dchain, 1)
                dve.wait_ge(dchain, n[0])

            link(nc.vector.memset(vg[:], 0.0))
            link(nc.vector.memset(vg[:, :, :, P:P + 1], 1.0))
            link(nc.vector.memset(at[:], 0.0))
            link(nc.vector.memset(o_sb[:], 0.0))
            nc.vector.memset(s_pr[:, 0, :], 0.0).then_inc(init, 1)
            dve.wait_ge(init, 1)
            dve.wait_ge(g_in, 16)

            def halves(x, w, b):
                v = x[:, 0:w].rearrange("p (n two b) -> p n two b", two=2, b=b)
                return v[:, :, 0, :], v[:, :, 1, :]

            def differences(u, lv):
                b, w = 64 >> lv, level_width(lv)
                left, right = halves(b_t, w, b)
                dl, dr = halves(dd[:, lv % 2], w, b)
                mid = left[:, :, b - 1:b].to_broadcast([P, w // (2 * b), b])
                link(nc.vector.tensor_tensor(dl, mid, left, ALU.subtract))
                nc.vector.tensor_tensor(dr, right, mid, ALU.subtract).then_inc(d_ready, 1)
                dve.wait_ge(d_ready, LEVELS * u + lv + 1)

            def decayed(u, lv):
                b, w = 64 >> lv, level_width(lv)
                el, er = halves(dd[:, lv % 2], w, b)
                xl, xr = halves(xx[:, lv % 2], w, b)
                kl, _ = halves(k_t[:, u % 2], w, b)
                _, qr = halves(q_t[:, u % 2], w, b)
                dve.wait_ge(e_ready, LEVELS * u + lv + 1)
                link(nc.vector.tensor_tensor(xl, el, kl, ALU.mult))
                nc.vector.tensor_tensor(xr, er, qr, ALU.mult).then_inc(x_ready, 1)
                dve.wait_ge(x_ready, LEVELS * u + lv + 1)

            def keep(u, lv):
                nn = (LEVELS + 1) * u + lv
                for g in range(2):
                    dve.wait_ge(a_done, 2 * nn + g + 1)
                    nc.vector.copy_predicated(at[:, 4 * g:4 * g + 4, :],
                                              masks[:, lv, :].bitcast(U32).unsqueeze(1).to_broadcast([P, 4, P]),
                                              ps_a[:, g]).then_inc(a_used, 1)
                    dve.wait_ge(a_used, 2 * nn + g + 1)
                if lv in tails:
                    nt = NTAIL * u + tails.index(lv)
                    r = LAST if lv == LEVELS else level_width(lv) - (NT - 1) * P
                    dve.wait_ge(at_done, nt + 1)
                    nc.vector.copy_predicated(at[0:r, NT - 1, 0:r], masks[0:r, lv, 0:r].bitcast(U32),
                                              ps_at[0:r, 0:r]).then_inc(at_used, 1)
                    dve.wait_ge(at_used, nt + 1)

            for u in range(NU):
                h = u - H
                q, k = q_t[:, u % 2], k_t[:, u % 2]
                dve.wait_ge(acts, u + 1)
                g = vg[:, u % 2, :, E:E + P]
                gain = gno[:, 0 if u < H else 1, :].unsqueeze(1).to_broadcast([P, NT, P])
                if u < H:
                    link(nc.vector.tensor_tensor(g, g, sq[:], ALU.mult))
                    nc.vector.tensor_tensor(g, g, gain, ALU.mult).then_inc(g_ready, 1)
                else:
                    nc.vector.tensor_tensor(g, sq[:], gain, ALU.mult).then_inc(g_ready, 1)
                if u < H:
                    dve.wait_ge(lf_ready, u + 1)
                    link(nc.vector.tensor_scalar(k, k, -1.0, 1.0, ALU.mult, ALU.add))
                    link(nc.vector.tensor_scalar(k, k, one_lb[:, u:u + 1], None, ALU.mult))
                    nc.vector.tensor_tensor_scan(b_t[:], reset[:], b_t[:], 0.0, ALU.mult, ALU.add).then_inc(b_ready, 1)
                    dve.wait_ge(b_ready, u + 1)
                    differences(u, 0)
                    for lv in range(LEVELS):
                        if lv + 1 < LEVELS:
                            differences(u, lv + 1)
                        decayed(u, lv)
                        if lv:
                            keep(u, lv - 1)
                    keep(u, LEVELS - 1)
                    keep(u, LEVELS)
                    nb = NT - 1
                    d2 = dd[:, 1]
                    link(nc.vector.tensor_tensor(d2[:, 0:nb * P].rearrange("p (m t) -> p m t", t=P),
                                                 b_t[:, P - 1:nb * P:P].unsqueeze(2).to_broadcast([P, nb, P]),
                                                 b_t[:, 0:nb * P].rearrange("p (m t) -> p m t", t=P), ALU.subtract))
                    link(nc.vector.tensor_tensor(d2[:, nb * P:TP], b_t[:, TP - 1:TP].to_broadcast([P, PTAIL]),
                                                 b_t[:, nb * P:TP], ALU.subtract))
                    nc.vector.tensor_tensor(d2[:, TP:T].rearrange("p (b t) -> p b t", t=DT),
                                            b_t[:, TP + DT - 1:T:DT].unsqueeze(2).to_broadcast([P, DB, DT]),
                                            b_t[:, TP:T].rearrange("p (b t) -> p b t", t=DT), ALU.subtract).then_inc(wm_ready, 1)
                    dve.wait_ge(w_ready, u + 1)
                    nc.vector.tensor_tensor(xx[:, 0, :], k, d2, ALU.mult).then_inc(kx_ready, 1)
                    dve.wait_ge(e1_ready, u + 1)
                else:
                    for c, (t0, tw) in enumerate(CH):
                        dve.wait_ge(bc_done, 3 * h + c + 1)
                        src = ps_a[:, 0].rearrange("p a b -> p (a b)")
                        full = tw // P * P
                        r = nc.vector.tensor_tensor(dd[:, 0, t0:t0 + full].rearrange("p (m t) -> p m t", t=P),
                                                    src[:, 0:full].rearrange("p (m t) -> p m t", t=P),
                                                    negm[:].unsqueeze(1).to_broadcast([P, full // P, P]), ALU.add)
                        if full < tw:
                            link(r)
                            r = nc.vector.tensor_tensor(dd[0:LAST, 0, t0 + full:T], src[0:LAST, full:tw], negtail[:], ALU.add)
                        r.then_inc(bc_d, 1)
                        dve.wait_ge(bc_d, 3 * h + c + 1)
                    dve.wait_ge(wm_ready, H + h + 1)
                    base = 2 * (LEVELS + 1) * H
                    for g in range(2):
                        dve.wait_ge(a_done, base + 2 * h + g + 1)
                        nc.vector.tensor_tensor(at[:, 4 * g:4 * g + 4, :],
                                                dd[:, 0, 4 * g * P:(4 * g + 4) * P].rearrange("p (m t) -> p m t", t=P),
                                                ps_a[:, g], ALU.mult).then_inc(a_used, 1)
                    dve.wait_ge(at_done, NTAIL * H + h + 1)
                    nc.vector.tensor_tensor(at[0:LAST, NT - 1, 0:LAST], dd[0:LAST, 0, (NT - 1) * P:T],
                                            ps_at[0:LAST, 0:LAST], ALU.mult).then_inc(at_used, 1)
                    dve.wait_ge(a_used, base + 2 * h + 2)
                    dve.wait_ge(at_used, NTAIL * H + h + 1)
                    dve.wait_ge(bc_a, 3 * h + 3)
                dec = st[:, 3:5, :].rearrange("p a b -> p (a b)")
                nb = NT - 1
                link(nc.vector.tensor_copy(dec[:, 0:nb], e1[:, P - 1:nb * P:P]))
                link(nc.vector.tensor_copy(dec[:, nb:nb + 1], e1[:, TP - 1:TP]))
                link(nc.vector.tensor_copy(dec[:, nb + 1:nb + 1 + DB], e1[:, TP + DT - 1:T:DT]))
                link(nc.vector.tensor_tensor(e1[:], e1[:], q, ALU.mult))
                link(nc.vector.tensor_tensor(qx[:], e1[:, nb * P:T].unsqueeze(1).to_broadcast([P, DB + 1, LAST]), col_mask[:], ALU.mult))
                dve.wait_ge(kt_used, KG * (u + 1))
                nc.vector.tensor_tensor(khx[:], kh[0:LAST, NT - 1, :].unsqueeze(1).to_broadcast([LAST, DB + 1, P]),
                                        row_mask[:].unsqueeze(2).to_broadcast([LAST, DB + 1, P]), ALU.mult).then_inc(khx_ready, 1)
                e = P if u < H else E
                dve.wait_ge(s_ld, 16 * (u + 1))
                if u:
                    dve.wait_ge(s_out, 32 * u)
                for gi, (i0, nn) in enumerate(UG):
                    dve.wait_ge(u_done, len(UG) * u + gi + 1)
                    for i in range(i0, i0 + nn):
                        src = s_pr[:, i, 0:e] if i < NT else s_in[:, i - NT, 0:e]
                        dst = s_pr[:, i + 1, 0:e] if i < NT else s_new[:, i - NT, 0:e]
                        ins = nc.vector.scalar_tensor_tensor(out=dst, in0=src, scalar=dec[:, i:i + 1],
                                                             in1=ps_u[:, (i - i0) * E:(i - i0) * E + e],
                                                             op0=ALU.mult, op1=ALU.add)
                        if i < i0 + nn - 1:
                            link(ins)
                    ins.then_inc(u_used, 1)
                    dve.wait_ge(u_used, len(UG) * u + gi + 1)
                dve.wait_ge(sq_ready, u + 1)
                link(nc.vector.tensor_reduce(st[:, 0, :], sq[:], AX.X, ALU.add))
                if u >= H:
                    den = o_sb[:, :, P:E].rearrange("p m o -> p (m o)")
                    link(nc.vector.scalar_tensor_tensor(out=st[:, 5, :], in0=den, scalar=-1.0, in1=den, op0=ALU.mult, op1=ALU.max))
                    link(nc.vector.tensor_tensor(st[:, 5, :], st[:, 5, :], cols[:, :, 2, h], ALU.max))
                    link(nc.vector.reciprocal(st[:, 6, :], st[:, 5, :]))
                    link(nc.vector.tensor_tensor(st[:, 0, :], st[:, 0, :], st[:, 6, :], ALU.mult))
                    link(nc.vector.tensor_tensor(st[:, 0, :], st[:, 0, :], st[:, 6, :], ALU.mult))
                nc.vector.tensor_scalar(st[:, 1, :], st[:, 0, :], 1.0 / P, EPS, ALU.mult, ALU.add).then_inc(std_in, 1)
                dve.wait_ge(std_out, u + 1)
                link(nc.vector.reciprocal(st[:, 7, :], st[:, 2, :]))
                if u >= H:
                    link(nc.vector.tensor_tensor(st[:, 7, :], st[:, 7, :], st[:, 6, :], ALU.mult))
                link(nc.vector.tensor_tensor(sq[:], o_sb[:, :, 0:P], st[:, 7, :].unsqueeze(2).to_broadcast([P, NT, P]), ALU.mult))
                nc.vector.tensor_tensor(sq[:], sq[:], vg[:, u % 2, :, E:E + P], ALU.mult).then_inc(y_ready, 1)
                dve.wait_ge(yt_done, KG * (u + 1))
                nc.vector.tensor_copy(st[:, 0, :], st[:, 7, :]).then_inc(dve_unit, 1)
                dve.wait_ge(dve_unit, u + 1)


GW = TP + 2 + DB * (DT + 2)


def ffn_up(nc, tag, h2, a_t, w_up, conv, conv_state, conv_out):
    with ExitStack() as ctx:
        def sb(name, shape, dt=F32):
            return ctx.enter_context(nc.sbuf_tensor(f"{tag}_{name}", shape, dt))

        used = []

        def sem(name):
            used.append(ctx.enter_context(nc.semaphore(f"{tag}_{name}")))
            return used[-1]

        w_sb = sb("w", [P, KD, P])
        w2 = sb("w2", [P, 2, 2, KD, P], F32R)
        gate = sb("gate", [P, GW])
        cv = sb("cv", [P, GW])
        cw = sb("cw", [P, NF * 4])
        cb = sb("cb", [P, 4])
        one = sb("one", [P, P])
        cst = sb("cst", [P, NF * DB * 2])
        ost = sb("ost", [P, NF * (DB + 1) * 2])
        ps = ctx.enter_context(nc.psum_tensor(f"{tag}_ps", [P, 3, 2, 512], F32))
        w_in = sem("w_in")
        high_done = sem("high_done")
        split_done = sem("split_done")
        c_in, zeroed = sem("c_in"), sem("zeroed")
        prod_done = sem("prod_done")
        gate_out = sem("gate_out")
        coef_in = sem("coef_in")
        past_in = sem("past_in")
        conv_done = sem("conv_done")
        silu_done = sem("silu_done")
        a_done = sem("a_done")
        kept = sem("kept")
        taps = sem("taps")
        stored = sem("stored")
        ctx.callback(clear_semaphores, nc, used)
        block = ctx.enter_context(nc.Block())

        @block.sync
        def _(sp):
            sp.dma_start(w_sb[:], w_up[0:P, :]).then_inc(w_in, 16)
            sp.dma_start(cw[:], conv).then_inc(c_in, 16)
            sp.dma_start(cst[:], conv_state).then_inc(c_in, 16)
            with sp.Fori(1, 2 * NF) as u:
                sp.wait_ge(split_done, u)
                sp.dma_start(w_sb[:], w_up[bass.ds(u * P, P), :]).then_inc(w_in, 16)
            sp.wait_ge(kept, 2 * NF)
            sp.dma_start(conv_out, ost[:]).then_inc(stored, 16)
            sp.wait_ge(stored, 16)

        @block.tensor
        def _(pe):
            def one(j, first):
                for two in range(2):
                    for c, (t0, tw) in enumerate(CH):
                        if c == 0:
                            pe.wait_ge(split_done, 2 * j + two + 1)
                        if not first:
                            if two == 0:
                                pe.wait_ge(gate_out, 3 * j + c - 2)
                            else:
                                pe.wait_ge(a_done, 3 * j + c - 2)
                        for k in range(KD):
                            mm = products(pe, ps[:, c, two, 0:tw], [w2[:, two, i, k, :] for i in range(2)],
                                          [h2[:, i, k, t0:t0 + tw] for i in range(2)], k == 0, k == KD - 1)
                        mm.then_inc(prod_done, 1)

            one(0, True)
            with pe.Fori(1, NF) as j:
                one(j, False)

        @block.gpsimd
        def _(pool):
            nc.gpsimd.memset(gate[:], 0.0).then_inc(zeroed, 1)
            nc.gpsimd.memset(one[:], 1.0).then_inc(zeroed, 1)
            pool.wait_ge(zeroed, 2)

            def split(u, two, free):
                pool.wait_ge(w_in, 16 * u + 16)
                if free is not None:
                    pool.wait_ge(prod_done, free)
                nc.gpsimd.tensor_tensor(w2[:, two, 0], w_sb[:], one[:].unsqueeze(1).to_broadcast([P, KD, P]), ALU.mult).then_inc(high_done, 1)
                pool.wait_ge(high_done, u + 1)
                nc.gpsimd.tensor_tensor(w2[:, two, 1], w_sb[:], w2[:, two, 0].bitcast(F32), ALU.subtract).then_inc(split_done, 1)

            split(0, 0, None)
            split(1, 1, None)
            with pool.Fori(1, NF) as j:
                split(2 * j, 0, 6 * j - 3)
                split(2 * j + 1, 1, 6 * j)

        @block.scalar
        def _(act):
            act.wait_ge(zeroed, 2)

            def take(j, c, first):
                t0, tw = CH[c]
                act.wait_ge(prod_done, 6 * j + c + 1)
                if not first and c == 0:
                    act.wait_ge(conv_done, 3 * j)
                if not first and c == 2:
                    act.wait_ge(kept, 2 * j)
                wp = min(tw, TP - t0)
                ins = nc.scalar.activation(gate[:, 2 + t0:2 + t0 + wp], ps[:, c, 0, 0:wp], ACT.Copy)
                if wp < tw:
                    ins = nc.scalar.activation(gate[:, TP + 2:].rearrange("p (b t) -> p b t", t=DT + 2)[:, :, 2:],
                                               ps[:, c, 0, wp:tw].rearrange("p (b t) -> p b t", t=DT), ACT.Copy)
                ins.then_inc(gate_out, 1)

            def silu(j, c):
                t0 = CH[c][0]
                w = CH[c][1] if c < 2 else GW - 2 - t0
                act.wait_ge(conv_done, 3 * j + c + 1)
                nc.scalar.activation(cv[:, t0:t0 + w], cv[:, t0:t0 + w], ACT.Silu, bias=cb[:, 3:4]).then_inc(silu_done, 1)

            def block_of(j, first):
                for c in range(3):
                    take(j, c, first)
                    silu(j, c)

            block_of(0, True)
            with act.Fori(1, NF) as j:
                block_of(j, False)

        @block.vector
        def _(dve):
            dve.wait_ge(c_in, 32)
            dve.wait_ge(zeroed, 2)

            def copy(dst, src):
                return nc.vector.tensor_scalar(dst, src, 1.0, None, ALU.mult)

            def before(j):
                copy(cb[:], cw[:, bass.ds(j * 4, 4)]).then_inc(coef_in, 1)
                copy(gate[:, TP + 2:].rearrange("p (b t) -> p b t", t=DT + 2)[:, :, 0:2],
                     cst[:, bass.ds(j * DB * 2, DB * 2)].rearrange("p (b t) -> p b t", t=2)).then_inc(past_in, 1)
                dve.wait_ge(coef_in, j + 1)

            def convolve(j, c):
                n = 3 * j + c
                t0 = CH[c][0]
                w = CH[c][1] if c < 2 else GW - 2 - t0
                dve.wait_ge(gate_out, n + 1)
                if c == 2:
                    dve.wait_ge(past_in, j + 1)
                    copy(ost[:, bass.ds(j * (DB + 1) * 2, 2)], gate[:, TP:TP + 2]).then_inc(kept, 1)
                    copy(ost[:, bass.ds(j * (DB + 1) * 2 + 2, DB * 2)].rearrange("p (b t) -> p b t", t=2),
                         gate[:, TP + 2:].rearrange("p (b t) -> p b t", t=DT + 2)[:, :, DT:]).then_inc(kept, 1)
                out = cv[:, t0:t0 + w]
                nc.vector.tensor_scalar(out, gate[:, t0 + 2:t0 + 2 + w], cb[:, 2:3], None, ALU.mult).then_inc(taps, 1)
                dve.wait_ge(taps, 2 * n + 1)
                nc.vector.scalar_tensor_tensor(out=out, in0=gate[:, t0 + 1:t0 + 1 + w], scalar=cb[:, 1:2],
                                               in1=out, op0=ALU.mult, op1=ALU.add).then_inc(taps, 1)
                dve.wait_ge(taps, 2 * n + 2)
                nc.vector.scalar_tensor_tensor(out=out, in0=gate[:, t0:t0 + w], scalar=cb[:, 0:1],
                                               in1=out, op0=ALU.mult, op1=ALU.add).then_inc(conv_done, 1)

            def times_value(j, c):
                t0 = CH[c][0]
                wp = min(CH[c][1], TP - t0)
                dve.wait_ge(silu_done, 3 * j + c + 1)
                dve.wait_ge(prod_done, 6 * j + c + 4)
                ins = nc.vector.tensor_tensor(a_t[:, bass.ds(j * T + t0, wp)], cv[:, t0:t0 + wp], ps[:, c, 1, 0:wp], ALU.mult)
                if c == 2:
                    ins = nc.vector.tensor_tensor(a_t[:, bass.ds(j * T + TP, TS)].rearrange("p (b t) -> p b t", t=DT),
                                                  cv[:, TP + 2:].rearrange("p (b t) -> p b t", t=DT + 2)[:, :, 0:DT],
                                                  ps[:, c, 1, wp:wp + TS].rearrange("p (b t) -> p b t", t=DT), ALU.mult)
                ins.then_inc(a_done, 1)

            with dve.Fori(0, NF) as j:
                before(j)
                for c in range(3):
                    convolve(j, c)
                for c in range(3):
                    times_value(j, c)


LAM_INIT = 0.8 - 0.6 * math.exp(-0.3)
KL = LAST


def att_project(nc, const, h_t, w_att, w_att_i, qc_t, kc_t, v_c, qd_t, kd_t, v_d, qi_t, ki_t, w_i, outs):
    ident = const["ident"]
    rope = const["rope"]
    with ExitStack() as ctx:
        def sb(name, shape, dt=F32):
            return ctx.enter_context(nc.sbuf_tensor(f"p_{name}", shape, dt))

        used = []

        def sem(name):
            used.append(ctx.enter_context(nc.semaphore(f"p_{name}")))
            return used[-1]

        NR, NP_ = 4, 4
        NS = 5
        w_sb = sb("w", [P, NS, 512])
        w2 = sb("w2", [P, KD, 2, 512], F32R)
        h2 = sb("h2", [P, 2, 2, KD, P], F32R)
        row = sb("row", [P, NR, 512])
        t1 = sb("t1", [P, 256])
        t2 = sb("t2", [P, 256])
        ps = ctx.enter_context(nc.psum_tensor("p_ps", [P, NP_, 512], F32))
        ps_t = ctx.enter_context(nc.psum_tensor("p_pst", [P, 4, 4, P], F32))
        w_in = [sem(f"w_in{i}") for i in range(NS)]
        w_high, w_split, w_used, h_high, h_split = (sem(x) for x in ("w_high", "w_split", "w_used", "h_high", "h_split"))
        prod, taken, chain, rotated, turned, placed, done_v = (
            sem(x) for x in ("prod", "taken", "chain", "rotated", "turned", "placed", "done_v"))
        stored = [sem(f"stored{i}") for i in range(NR)]
        ctx.callback(clear_semaphores, nc, used)
        block = ctx.enter_context(nc.Block())
        NGR = 6
        items = [(g, m) for g in range(NGR) for m in range(NT)]
        rot = {0: [(0, 8, 64, 8, 0)], 1: [(0, 8, 64, 8, 0)], 2: [], 3: [(0, 4, 128, 16, 8)],
               4: [(0, 1, 128, 16, 8), (256, 4, 64, 8, 0)], 5: [(0, 1, 64, 8, 0)]}
        kc_o, vc_o, kd_o, vd_o, ki_o = outs

        def stores(g, m):
            r = rows_of(m)
            rr = slice(m * P, m * P + r)
            return {1: [(kc_o[rr, :], 0, 512)], 2: [(vc_o[rr, :], 0, 512)],
                    4: [(kd_o[rr, :], 0, P), (vd_o[rr, :], P, 2 * P)], 5: [(ki_o[rr, :], 0, 64)]}.get(g, [])

        def stored_upto(n):
            return 16 * sum(len(stores(*items[i])) for i in range(n % NR, n + 1, NR))

        turns = {0: 4, 1: 4, 2: 0, 3: 4, 4: 3, 5: 1}
        with_turn = [n for n, (g, m) in enumerate(items) if turns[g]]
        turn_no = {n: i for i, n in enumerate(with_turn)}

        def put(sp, n):
            g, m = items[n]
            if stores(g, m):
                sp.wait_ge(rotated, n + 1)
            for dst, c0, c1 in stores(g, m):
                sp.dma_start(dst, row[0:rows_of(m), n % NR, c0:c1]).then_inc(stored[n % NR], 16)

        @block.sync
        def _(sp):
            for n in range(len(items)):
                put(sp, n)
            for i in range(NR):
                sp.wait_ge(stored[i], stored_upto(len(items) - 1 - (len(items) - 1 - i) % NR))

        def cols(g):
            return 512 if g < 5 else 68

        @block.gpsimd
        def _(pool):
            for n, (g, m) in enumerate(items):
                r = rows_of(m)
                if n >= 2:
                    pool.wait_ge(prod, n - 1)
                nc.gpsimd.tensor_copy(h2[:, n % 2, 0, :, 0:r], h_t[:, :, m * P:m * P + r]).then_inc(h_high, 1)

        @block.tensor
        def _(pe):
            def turn(n):
                g, m = items[n]
                if not turns[g]:
                    return
                r = rows_of(m)
                t = turn_no[n]
                pe.wait_ge(rotated, n + 1)
                if t >= 4:
                    pe.wait_ge(placed, t - 3)
                c0s = {4: [0, 256, 384], 5: [0]}.get(g, [0, 128, 256, 384])
                for i, c0 in enumerate(c0s):
                    x = pe.transpose(ps_t[:, t % 4, i, 0:r], row[0:r, n % NR, c0:c0 + P], ident[0:r, 0:r])
                x.then_inc(turned, 1)

            for n, (g, m) in enumerate(items):
                pe.wait_ge(h_split, n + 1)
                if n >= NP_:
                    pe.wait_ge(taken, n - NP_ + 1)
                for k in range(KD):
                    if m == 0:
                        pe.wait_ge(w_split, g * KD + k + 1)
                    mm = products(pe, ps[:, n % NP_, 0:cols(g)], [h2[:, n % 2, i, k, :] for i in range(2)],
                                  [w2[:, k, i, 0:cols(g)] for i in range(2)], k == 0, k == KD - 1)
                    if m == NT - 1 and k < KD - 1:
                        mm.then_inc(w_used, 1)
                mm.then_inc(prod, 1)
                if n >= 2:
                    turn(n - 2)
            turn(len(items) - 2)
            turn(len(items) - 1)

        @block.scalar
        def _(act):
            def place(n):
                g, m = items[n]
                if not turns[g]:
                    return
                r = rows_of(m)
                t = turn_no[n]
                act.wait_ge(turned, t + 1)
                c = slice(m * P, m * P + r)
                if g in (0, 1, 3):
                    dst = {0: qc_t, 1: kc_t, 3: qd_t}[g]
                    ins = nc.scalar.activation(dst[:, :, c], ps_t[:, t % 4, :, 0:r], ACT.Copy)
                elif g == 4:
                    nc.scalar.activation(kd_t[:, c], ps_t[:, t % 4, 0, 0:r], ACT.Copy)
                    ins = nc.scalar.activation(qi_t[:, :, c], ps_t[:, t % 4, 1:3, 0:r], ACT.Copy)
                else:
                    ins = nc.scalar.activation(ki_t[:, c], ps_t[:, t % 4, 0, 0:r], ACT.Copy)
                ins.then_inc(placed, 1)

            def load(q):
                g, k = divmod(q, KD)
                if g < NGR:
                    act.dma_start(w_sb[:, q % NS, 0:cols(g)], w_att[g, :, k, :] if g < 5 else w_att_i[:, k, :]).then_inc(w_in[q % NS], 16)

            def high_parts(g):
                for q in range(g * KD, (g + 1) * KD):
                    k = q % KD
                    act.wait_ge(w_in[q % NS], 16 * (q // NS + 1))
                    if g:
                        act.wait_ge(*((w_used, (KD - 1) * (g - 1) + k + 1) if k < KD - 1 else (prod, NT * g)))
                    nc.scalar.activation(w2[:, k, 0, 0:cols(g)], w_sb[:, q % NS, 0:cols(g)], ACT.Copy).then_inc(w_high, 1)
                    if q:
                        act.wait_ge(w_split, q)
                        load(q + NS - 1)

            for q in range(NS):
                load(q)
            high_parts(0)
            for n, (g, m) in enumerate(items):
                r = rows_of(m)
                w = cols(g)
                if m == NT - 1 and g + 1 < NGR:
                    high_parts(g + 1)
                act.wait_ge(prod, n + 1)
                if n >= NR:
                    if stored_upto(n - NR):
                        act.wait_ge(stored[n % NR], stored_upto(n - NR))
                    act.wait_ge(done_v, n - NR + 1)
                    if n - NR in turn_no:
                        act.wait_ge(turned, turn_no[n - NR] + 1)
                nc.scalar.activation(row[0:r, n % NR, 0:w], ps[0:r, n % NP_, 0:w], ACT.Copy).then_inc(taken, 1)
                if n >= 3:
                    place(n - 3)
            for n in range(len(items) - 3, len(items)):
                place(n)

        @block.vector
        def _(dve):
            cnt = [0]

            def link(ins):
                cnt[0] += 1
                ins.then_inc(chain, 1)
                dve.wait_ge(chain, cnt[0])

            def rests(g):
                for q in range(g * KD, (g + 1) * KD):
                    dve.wait_ge(w_high, q + 1)
                    nc.vector.tensor_tensor(w2[:, q % KD, 1, 0:cols(g)], w_sb[:, q % NS, 0:cols(g)],
                                            w2[:, q % KD, 0, 0:cols(g)].bitcast(F32), ALU.subtract).then_inc(w_split, 1)

            def h_rest(n):
                m = items[n][1]
                r = rows_of(m)
                dve.wait_ge(h_high, n + 1)
                nc.vector.tensor_tensor(h2[:, n % 2, 1, :, 0:r], h_t[:, :, m * P:m * P + r],
                                        h2[:, n % 2, 0, :, 0:r].bitcast(F32), ALU.subtract).then_inc(h_split, 1)

            h_rest(0)
            rests(0)
            for n, (g, m) in enumerate(items):
                r = rows_of(m)
                if n + 1 < len(items):
                    h_rest(n + 1)
                if m == NT - 1 and g + 1 < NGR:
                    rests(g + 1)
                x = row[0:r, n % NR, :]
                dve.wait_ge(taken, n + 1)
                for c0, nh, d, half, tc in rot[g]:
                    v = x[:, c0:c0 + nh * d].rearrange("p (h d) -> p h d", d=d)[:, :, 0:2 * half] \
                        .rearrange("p h (two e) -> p h two e", two=2)
                    a = t1[0:r, 0:nh * 2 * half].rearrange("p (h two e) -> p h two e", two=2, e=half)
                    b = t2[0:r, 0:nh * 2 * half].rearrange("p (h two e) -> p h two e", two=2, e=half)
                    cos = rope[0:r, m, 0, tc:tc + half].unsqueeze(1).unsqueeze(1).to_broadcast([r, nh, 2, half])
                    sin = rope[0:r, m, 1, tc:tc + half].unsqueeze(1).unsqueeze(1).to_broadcast([r, nh, 2, half])
                    link(nc.vector.tensor_tensor(a, v, cos, ALU.mult))
                    link(nc.vector.tensor_tensor(b, v, sin, ALU.mult))
                    link(nc.vector.tensor_tensor(v[:, :, 0], a[:, :, 0], b[:, :, 1], ALU.subtract))
                    link(nc.vector.tensor_tensor(v[:, :, 1], b[:, :, 0], a[:, :, 1], ALU.add))
                if g == 5:
                    link(nc.vector.tensor_scalar(w_i[0:r, m, :], x[:, 64:68], H ** -0.5, None, ALU.mult))
                    link(nc.vector.tensor_copy(x[:, 64:P], x[:, 0:64]))
                nc.vector.tensor_copy(t1[0:1, 0:1], x[0:1, 0:1]).then_inc(rotated, 1)
                if g == 2:
                    nc.vector.tensor_copy(v_c[0:r, m, :], x).then_inc(done_v, 1)
                elif g == 4:
                    nc.vector.tensor_copy(v_d[0:r, m, :], x[:, P:2 * P]).then_inc(done_v, 1)
                else:
                    nc.vector.tensor_copy(t2[0:1, 0:1], x[0:1, 0:1]).then_inc(done_v, 1)
                dve.wait_ge(done_v, n + 1)
                dve.wait_ge(rotated, n + 1)


def prompt_attention(nc, const, qc_t, kc_t, v_c, qd_t, kd_t, v_d, qi_t, ki_t, w_i, o_t, neg_lam, diff_lambda, g_diff):
    ident, neg = const["ident"], const["neg_future"]
    with ExitStack() as ctx:
        def sb(name, shape):
            return ctx.enter_context(nc.sbuf_tensor(f"a_{name}", shape, F32))

        used = []

        def sem(name):
            used.append(ctx.enter_context(nc.semaphore(f"a_{name}")))
            return used[-1]

        lamp = sb("lamp", [P, 4, DC])
        lt = sb("lt", [P, 2, DC])
        le = sb("le", [P, 4])
        gd = sb("gd", [P, P])
        p_sb = sb("p", [P, 4, TP])
        score = sb("score", [P, 2, TP])
        relu = sb("relu", [P, 2, TP])
        top = sb("top", [P, 8])
        stat = sb("stat", [P, 4, 8])
        a_t = sb("a_t", [P, 2, NT, P])
        o_sb = sb("o", [P, 2, 8, P])
        osq = sb("osq", [P, 4, P])
        ost = sb("ost", [P, 4, 4])
        ps_s = ctx.enter_context(nc.psum_tensor("a_pss", [P, 4 * 512], F32))
        ps_t = ctx.enter_context(nc.psum_tensor("a_pst", [P, 2, 4, P], F32))
        ps_o = ctx.enter_context(nc.psum_tensor("a_pso", [P, 2, 512], F32))
        loaded, lam_sum, lam_exp, chain = (sem(x) for x in ("loaded", "lam_sum", "lam_exp", "chain"))
        s_done, max_done, exp_done, relu_done, relu_used, picked = (
            sem(x) for x in ("s_done", "max_done", "exp_done", "relu_done", "relu_used", "picked"))
        mixed, turned, placed, o_done, o_read, osq_done, ovar, ostd, normed = (
            sem(x) for x in ("mixed", "turned", "placed", "o_done", "o_read", "osq_done", "ovar", "ostd", "normed"))
        ctx.callback(clear_semaphores, nc, used)
        block = ctx.enter_context(nc.Block())

        tiles = [0, 1] + list(range(NT - 1, 1, -1))

        def first(m):
            return tiles[m] * P

        def qrows(m):
            return P if tiles[m] < NT - 1 else PTAIL

        def width(m):
            return min((tiles[m] + 1) * P, TP)

        def indexed(m):
            return width(m) > TOPK

        units, softmaxes, relus, heads = [], [], [], []
        for m in range(NT):
            if m + 1 < NT and indexed(m + 1):
                for h in range(H):
                    units.append(("index", m + 1, h, 0))
                    relus.append(len(units) - 1)
            for h in range(H):
                for c in range(2):
                    units.append(("diff", m, h, c))
                    softmaxes.append(len(units) - 1)
            for h in range(H):
                units.append(("dsa", m, h, 0))
                softmaxes.append(len(units) - 1)
        u_no = {u: n for n, u in enumerate(units)}
        k_no = {u: n for n, u in enumerate(softmaxes)}
        r_no = {u: n for n, u in enumerate(relus)}
        turn_list = []
        for m in range(NT):
            for hd in range(8):
                nk = -(-width(m) // P)
                for b0 in range(0, nk, 4):
                    turn_list.append((m, hd, b0, min(4, nk - b0)))
                if hd == 0 and m:
                    turn_list += [(m - 1, "out", 0, 4), (m - 1, "out", 4, 4)]
        turn_list += [(NT - 1, "out", 0, 4), (NT - 1, "out", 4, 4)]
        t_no = {t[:3]: n for n, t in enumerate(turn_list)}

        def region(n):
            m = units[n][1]
            o = (n % 2) * 1024 if tiles[m] < NT - 1 else 0
            return o, width(m)

        def head_scores(m, hd):
            return [u_no[("diff", m, hd, c)] for c in range(2)] if hd < 4 else [u_no[("dsa", m, hd - 4, 0)]]

        def before(m, hd):
            return (m, hd - 1) if hd else (m - 1, 7)

        @block.sync
        def _(sp):
            sp.dma_start(lamp[:], diff_lambda.partition_broadcast(P)).then_inc(loaded, 16)
            sp.dma_start(gd[:], g_diff.partition_broadcast(P)).then_inc(loaded, 16)
            sp.wait_ge(loaded, 32)

        @block.tensor
        def _(pe):
            def scores(n):
                kind, m, h, c = units[n]
                r, (o, w) = qrows(m), region(n)
                q = slice(first(m), first(m) + r)
                wide = NT - 1 in (tiles[m], tiles[units[n - 1][1]])
                old = n - 1 if wide else n - 2
                if old in k_no:
                    pe.wait_ge(exp_done, k_no[old] + 1)
                elif old in r_no:
                    pe.wait_ge(relu_done, r_no[old] + 1)
                mask = kind == "dsa" and indexed(m)
                d0 = w if mask or kind == "index" else first(m)
                cuts = [(k0, min(512, d0 - k0)) for k0 in range(0, d0, 512)] + ([(d0, w - d0)] if d0 < w else [])
                for k0, kw in cuts:
                    out, k = ps_s[0:r, o + k0:o + k0 + kw], slice(k0, k0 + kw)
                    if kind == "dsa":
                        lhs, rhs = qd_t[:, h, q], kd_t[:, k]
                    elif kind == "diff":
                        lhs, rhs = qc_t[c * DC:(c + 1) * DC, h, q], kc_t[c * DC:(c + 1) * DC, h, k]
                    else:
                        p = slice((h % 2) * 64, (h % 2) * 64 + 64)
                        lhs, rhs = qi_t[p, h // 2, q], ki_t[p, k]
                    diag = k0 == d0
                    mm = pe.matmul(out, lhs, rhs, start=True, stop=not (mask or diag))
                    if mask or diag:
                        mm = pe.matmul(out, ident[0:r, 0:r], score[0:r, m % 2, k] if mask else neg[0:r, 0:kw], start=False, stop=True)
                mm.then_inc(s_done, 1)

            def head_out(m, hd):
                r, j = qrows(m), 8 * m + hd
                k = k_no[u_no[("diff", m, hd, 1) if hd < 4 else ("dsa", m, hd - 4, 0)]]
                pe.wait_ge(mixed, j + 1)
                nk = -(-width(m) // P)
                for b0 in range(0, nk, 4):
                    t = t_no[(m, hd, b0)]
                    if t >= 2:
                        pe.wait_ge(placed, t - 1)
                    for b in range(b0, min(b0 + 4, nk)):
                        kw = min(P, width(m) - b * P)
                        x = pe.transpose(ps_t[0:kw, t % 2, b - b0, 0:r], p_sb[0:r, (k - (hd < 4)) % 4, b * P:b * P + kw],
                                         ident[0:r, 0:r])
                    x.then_inc(turned, 1)
                return j

            def values(m, hd):
                r, j = qrows(m), 8 * m + hd
                nk = -(-width(m) // P)
                pe.wait_ge(placed, t_no[(m, hd, (nk - 1) // 4 * 4)] + 1)
                if j >= 2:
                    pe.wait_ge(o_read, j - 1)
                for b in range(nk):
                    kw = min(P, width(m) - b * P)
                    v = v_c[0:kw, b, hd * P:(hd + 1) * P] if hd < 4 else v_d[0:kw, b, :]
                    mm = pe.matmul(ps_o[0:r, j % 2, 0:P], a_t[0:kw, j % 2, b, 0:r], v, start=(b == 0), stop=(b == nk - 1))
                mm.then_inc(o_done, 1)

            def outputs(m):
                r = qrows(m)
                pe.wait_ge(normed, m + 1)
                pe.wait_ge(o_read, 8 * m + 8)
                for i0 in (0, 4):
                    t = t_no[(m, "out", i0)]
                    pe.wait_ge(placed, t - 1)
                    for i in range(4):
                        x = pe.transpose(ps_t[:, t % 2, i, 0:r], o_sb[0:r, m % 2, i0 + i, :], ident[0:r, 0:r])
                    x.then_inc(turned, 1)

            for m in range(NT):
                if m + 1 < NT and indexed(m + 1):
                    for h in range(H):
                        scores(u_no[("index", m + 1, h, 0)])
                for hd in range(8):
                    if hd == 4 and indexed(m):
                        pe.wait_ge(picked, sum(indexed(i) for i in range(m + 1)))
                    for n in head_scores(m, hd):
                        scores(n)
                    if m or hd:
                        head_out(*before(m, hd))
                        values(*before(m, hd))
                    if m and hd == 1:
                        outputs(m - 1)
            head_out(NT - 1, 7)
            values(NT - 1, 7)
            outputs(NT - 1)

        @block.scalar
        def _(act):
            act.wait_ge(lam_sum, 1)
            nc.scalar.activation(le[:, 2:4], le[:, 0:2], ACT.Exp).then_inc(lam_exp, 1)

            def softmax(n):
                kind, m, h, c = units[n]
                k = k_no[n]
                r, (o, w) = qrows(m), region(n)
                act.wait_ge(max_done, k + 1)
                if k >= 4:
                    old = units[softmaxes[k - 4]]
                    hd = old[2] + (4 if old[0] == "dsa" else 0)
                    nk = -(-width(old[1]) // P)
                    act.wait_ge(turned, t_no[(old[1], hd, (nk - 1) // 4 * 4)] + 1)
                scale = DC ** -0.5 if kind == "diff" else float(P) ** -0.5
                nc.scalar.activation(p_sb[0:r, k % 4, 0:w], ps_s[0:r, o:o + w], ACT.Exp, bias=stat[0:r, k % 4, 1:2],
                                     scale=scale, accum_out=stat[0:r, k % 4, 2:3]).then_inc(exp_done, 1)

            def index(n):
                kind, m, h, c = units[n]
                r, (o, w) = qrows(m), region(n)
                i = r_no[n]
                act.wait_ge(s_done, n + 1)
                if i >= 2:
                    act.wait_ge(relu_used, i - 1)
                nc.scalar.activation(relu[0:r, i % 2, 0:w], ps_s[0:r, o:o + w], ACT.Relu, scale=64 ** -0.5).then_inc(relu_done, 1)

            def head_out(m, hd):
                r, j = qrows(m), 8 * m + hd
                nk = -(-width(m) // P)
                if j >= 2:
                    act.wait_ge(o_done, j - 1)
                for b0 in range(0, nk, 4):
                    n = min(4, nk - b0)
                    act.wait_ge(turned, t_no[(m, hd, b0)] + 1)
                    t = t_no[(m, hd, b0)]
                    kw = min(P, width(m) - b0 * P)
                    nc.scalar.activation(a_t[0:kw, j % 2, b0:b0 + n, 0:r], ps_t[0:kw, t % 2, 0:n, 0:r], ACT.Copy).then_inc(placed, 1)

            def values(m, hd):
                r, j = qrows(m), 8 * m + hd
                k = k_no[u_no[("diff", m, hd, 0) if hd < 4 else ("dsa", m, hd - 4, 0)]]
                act.wait_ge(o_done, j + 1)
                nc.scalar.activation(o_sb[0:r, m % 2, hd, :], ps_o[0:r, j % 2, 0:P], ACT.Copy,
                                     scale=stat[0:r, k % 4, 3:4]).then_inc(o_read, 1)

            def squares(m):
                r = qrows(m)
                act.wait_ge(o_read, 8 * m + 4)
                if m:
                    act.wait_ge(normed, m)
                nc.scalar.activation(osq[0:r], o_sb[0:r, m % 2, 0:4, :], ACT.Square).then_inc(osq_done, 1)

            def outputs(m):
                r = qrows(m)
                for i0 in (0, 4):
                    t = t_no[(m, "out", i0)]
                    act.wait_ge(turned, t + 1)
                    nc.scalar.activation(o_t[:, i0:i0 + 4, first(m):first(m) + r], ps_t[:, t % 2, :, 0:r], ACT.Copy).then_inc(placed, 1)

            def finish(m, hd):
                r = qrows(m)
                head_out(m, hd)
                values(m, hd)
                if hd == 3:
                    squares(m)
                if hd == 5:
                    act.wait_ge(ovar, m + 1)
                    nc.scalar.activation(ost[0:r, 2, :], ost[0:r, 1, :], ACT.Sqrt).then_inc(ostd, 1)

            for m in range(NT):
                if m + 1 < NT and indexed(m + 1):
                    for h in range(H):
                        index(u_no[("index", m + 1, h, 0)])
                for hd in range(8):
                    for n in head_scores(m, hd):
                        softmax(n)
                    if m or hd:
                        finish(*before(m, hd))
                    if m and hd == 1:
                        outputs(m - 1)
            finish(NT - 1, 7)
            outputs(NT - 1)

        @block.vector
        def _(dve):
            cnt = [0]

            def link(ins):
                cnt[0] += 1
                ins.then_inc(chain, 1)
                dve.wait_ge(chain, cnt[0])

            dve.wait_ge(loaded, 32)
            lv = lamp[:].rearrange("p (two qk) d -> p two qk d", two=2)
            link(nc.vector.tensor_tensor(lt[:], lv[:, :, 0, :], lv[:, :, 1, :], ALU.mult))
            nc.vector.tensor_reduce(le[:, 0:2], lt[:], AX.X, ALU.add).then_inc(lam_sum, 1)
            dve.wait_ge(lam_exp, 1)
            link(nc.vector.tensor_tensor(neg_lam[:], le[:, 3:4], le[:, 2:3], ALU.subtract))
            link(nc.vector.tensor_scalar(neg_lam[:], neg_lam[:], LAM_INIT, None, ALU.subtract))
            link(nc.vector.tensor_scalar(gd[:], gd[:], 1.0 - LAM_INIT, None, ALU.mult))

            def maximum(n):
                kind, m, h, c = units[n]
                k = k_no[n]
                r, (o, w) = qrows(m), region(n)
                scale = DC ** -0.5 if kind == "diff" else float(P) ** -0.5
                dve.wait_ge(s_done, n + 1)
                if k >= 4:
                    old = units[softmaxes[k - 4]]
                    dve.wait_ge(o_read, 8 * old[1] + old[2] + (4 if old[0] == "dsa" else 0) + 1)
                link(nc.vector.tensor_reduce(stat[0:r, k % 4, 0:1], ps_s[0:r, o:o + w], AX.X, ALU.max))
                nc.vector.tensor_scalar(stat[0:r, k % 4, 1:2], stat[0:r, k % 4, 0:1], -scale, None, ALU.mult).then_inc(max_done, 1)

            def mix(m, hd):
                r, w, j = qrows(m), width(m), 8 * m + hd
                k = k_no[u_no[("diff", m, hd, 0) if hd < 4 else ("dsa", m, hd - 4, 0)]]
                s0 = stat[0:r, k % 4]
                dve.wait_ge(exp_done, k + 1)
                if hd >= 4:
                    nc.vector.reciprocal(s0[:, 3:4], s0[:, 2:3]).then_inc(mixed, 1)
                    dve.wait_ge(mixed, j + 1)
                    return
                s1 = stat[0:r, (k + 1) % 4]
                link(nc.vector.reciprocal(s0[:, 3:4], s0[:, 2:3]))
                dve.wait_ge(exp_done, k + 2)
                link(nc.vector.reciprocal(s1[:, 3:4], s1[:, 2:3]))
                link(nc.vector.tensor_tensor(s1[:, 4:5], s1[:, 3:4], s0[:, 2:3], ALU.mult))
                link(nc.vector.tensor_tensor(s1[:, 5:6], s1[:, 4:5], neg_lam[0:r, :], ALU.mult))
                nc.vector.scalar_tensor_tensor(out=p_sb[0:r, k % 4, 0:w], in0=p_sb[0:r, (k + 1) % 4, 0:w],
                                               scalar=s1[:, 5:6], in1=p_sb[0:r, k % 4, 0:w],
                                               op0=ALU.mult, op1=ALU.add).then_inc(mixed, 1)
                dve.wait_ge(mixed, j + 1)

            def index_sum(m):
                r, w = qrows(m), width(m)
                if indexed(m - 2):
                    dve.wait_ge(s_done, u_no[("dsa", m - 2, H - 1, 0)] + 1)
                out = score[0:r, m % 2, 0:w]
                for h in range(H):
                    i = r_no[u_no[("index", m, h, 0)]]
                    dve.wait_ge(relu_done, i + 1)
                    wh = w_i[0:r, tiles[m], h:h + 1]
                    if h == 0:
                        x = nc.vector.tensor_scalar(out, relu[0:r, i % 2, 0:w], wh, None, ALU.mult)
                    else:
                        x = nc.vector.scalar_tensor_tensor(out=out, in0=relu[0:r, i % 2, 0:w], scalar=wh,
                                                           in1=out, op0=ALU.mult, op1=ALU.add)
                    x.then_inc(relu_used, 1)
                    dve.wait_ge(relu_used, i + 1)
                diag = out[:, first(m):w]
                link(nc.vector.tensor_tensor(diag, diag, neg[0:r, 0:w - first(m)], ALU.add))

            def rounds(m, n):
                x = score[0:qrows(m), m % 2, 0:width(m)]
                for _ in range(n):
                    link(nc.vector.max(top[0:qrows(m), :], x))
                    link(nc.vector.match_replace(x, top[0:qrows(m), :], x, PICKED))

            def mask(m):
                r, w = qrows(m), width(m)
                x = score[0:r, m % 2, 0:w]
                link(nc.vector.tensor_scalar(x, x, PICKED, NEG, ALU.not_equal, ALU.mult))
                nc.vector.tensor_tensor(x[:, first(m):w], x[:, first(m):w], neg[0:r, 0:w - first(m)], ALU.add).then_inc(picked, 1)

            for m in range(NT):
                r = qrows(m)
                ahead = m + 1 < NT and indexed(m + 1)
                if ahead:
                    index_sum(m + 1)
                for hd in range(8):
                    for n in head_scores(m, hd):
                        maximum(n)
                    if ahead:
                        rounds(m + 1, TOPK // 64)
                    mix(m, hd)
                    if hd == 5:
                        dve.wait_ge(osq_done, m + 1)
                        link(nc.vector.tensor_reduce(ost[0:r, 0, :], osq[0:r], AX.X, ALU.add))
                        nc.vector.tensor_scalar(ost[0:r, 1, :], ost[0:r, 0, :], 1.0 / P, EPS, ALU.mult, ALU.add).then_inc(ovar, 1)
                if ahead:
                    mask(m + 1)
                dve.wait_ge(ostd, m + 1)
                link(nc.vector.reciprocal(ost[0:r, 3, :], ost[0:r, 2, :]))
                o = o_sb[0:r, m % 2, 0:4, :]
                link(nc.vector.tensor_tensor(o, o, ost[0:r, 3, :].unsqueeze(2).to_broadcast([r, 4, P]), ALU.mult))
                nc.vector.tensor_tensor(o, o, gd[0:r, :].unsqueeze(1).to_broadcast([r, 4, P]), ALU.mult).then_inc(normed, 1)
                dve.wait_ge(normed, m + 1)


def sample_queries(nc, new, qc_t, kc_t, v_c, qd_t, kd_t, v_d, qi_t, ki_t, w_i):
    with ExitStack() as ctx:
        qi_odd = ctx.enter_context(nc.sbuf_tensor("q_qi_odd", [64, 2, TS], F32))
        used = [ctx.enter_context(nc.semaphore(f"q_{n}")) for n in ("odd_in", "steps", "copied")]
        odd_in, steps, copied = used
        ctx.callback(clear_semaphores, nc, used)
        block = ctx.enter_context(nc.Block())

        @block.sync
        def _(sp):
            sp.dma_start(qi_odd[:], qi_t[64:P, :, TP:T]).then_inc(odd_in, 16)

        @block.scalar
        def _(act):
            last = slice((NT - 1) * P, T)
            for dst, src in (("kc", kc_t[:, :, last]), ("kd", kd_t[:, last]), ("ki", ki_t[0:64, last]),
                             ("vc", v_c[0:KL, NT - 1, :]), ("vd", v_d[0:KL, NT - 1, :]), ("w", w_i[0:KL, NT - 1, :])):
                nc.scalar.activation(new[dst][:], src, ACT.Copy).then_inc(copied, 1)
            act.wait_ge(copied, 6)

        @block.vector
        def _(dve):
            n = 3
            for x in ("qx", "qdx", "qix"):
                nc.vector.memset(new[x][:], 0.0).then_inc(steps, 1)
            dve.wait_ge(steps, 3)
            q_new = slice(TP, T)

            def place(dst, src):
                nc.vector.tensor_copy(dst, src.rearrange("p (b q) -> p b q", q=DT)).then_inc(steps, 1)

            for h in range(H):
                for c in range(2):
                    p = slice(64 * c, 64 * c + 64)
                    place(new["qx"][p, :, h, h * 8 + c * 4:h * 8 + c * 4 + 4], qc_t[p, h, q_new])
                place(new["qdx"][:, :, 4 * h:4 * h + 4], qd_t[:, h, q_new])
                if h % 2 == 0:
                    place(new["qix"][:, :, 4 * h:4 * h + 4], qi_t[0:64, h // 2, q_new])
                n += 3 + (h % 2 == 0)
            dve.wait_ge(odd_in, 16)
            for h in (1, 3):
                place(new["qix"][:, :, 4 * h:4 * h + 4], qi_odd[:, h // 2, :])
            dve.wait_ge(steps, n + 2)


def sample_attention(nc, const, a, new, o_t, neg_lam):
    ident = const["ident"]
    NKC = PAST + KL
    NB = NPG + 1
    QP = 4
    NQ = NPG // QP
    with ExitStack() as ctx:
        def sb(name, shape, dt=F32):
            return ctx.enter_context(nc.sbuf_tensor(f"s_{name}", shape, dt))

        used = []

        def sem(name):
            used.append(ctx.enter_context(nc.semaphore(f"s_{name}")))
            return used[-1]

        RI, RC = 8, 10
        tbl = sb("tbl", [1, DB * NPG], I32)
        ik_ring = sb("ik_ring", [64, RI, QP, P])
        ring = sb("ring", [P, RC, QP * H * P])
        qx, qdx, qix = new["qx"], new["qdx"], new["qix"]
        sc = sb("sc", [2 * 16, NKC])
        p_sb = sb("p", [P, NKC])
        rl = sb("rl", [P, NKC])
        a_t = sb("a_t", [P, NB, 4, 32])
        os_c = rl[:, 0:2 * H * P].rearrange("p (g e) -> p g e", g=2)
        o_s = rl[0:TS, 2 * H * P:4 * H * P].rearrange("p (k e) -> p k e", k=2)
        os_d = sb("os_d", [P, 2, P])
        osq = sb("osq", [TS, H, P])
        ost = sb("ost", [TS, 4, H])
        gd = sb("gd", [TS, P])
        wsel = sb("wsel", [P, 2, TS])
        wrow = sb("wrow", [P, 2, H])
        wr1 = sb("wr1", [P, 2])
        top = sb("top", [TS, 8])
        st = sb("st", [P, 8])
        half_c = sb("half_c", [P, 2])
        ps_s = ctx.enter_context(nc.psum_tensor("s_pss", [P, 5 * 512], F32))
        ps_t = ctx.enter_context(nc.psum_tensor("s_pst", [P, 2, 4, P], F32))
        ps_o = ctx.enter_context(nc.psum_tensor("s_pso", [P, 512], F32))
        names = ("t_in", "zeroed", "q_ready", "w_ps", "wsel_ready", "chain", "achain", "s_done", "relu_done", "sc_ps", "sc_out",
                 "picked", "max_done", "exp_done", "scaled", "turned", "placed", "o_done", "o_read", "sel_done", "sel_read",
                 "osq_done", "ovar", "ostd", "normed", "o_turned", "o_placed", "ik_used", "used", "c_in")
        S = {n: sem(n) for n in names}
        ik_in = [sem(f"ik_in{i}") for i in range(RI)]
        c_in = [sem(f"c_in{i}") for i in range(RC)]
        ctx.callback(clear_semaphores, nc, used)
        block = ctx.enter_context(nc.Block())
        ik_loads = [(b, c) for b in range(DB) for c in range(NQ)]
        loads = []
        for g in range(2):
            for kind in ("ck", "cv"):
                loads += [(kind, 4 * g + j, c) for j in range(4) for c in range(NQ)]
        loads += [("d", b, c) for b in range(DB) for c in range(NQ // 2)]
        at = {x: n for n, x in enumerate(loads)}
        stages = [("c", 0), ("c", 1), ("d", 0), ("d", 1)]

        def arrived(n):
            return 16 * sum(QP * (2 if loads[i][0] == "d" else 1) for i in range(n % RC, n + 1, RC))

        def fetch(eng, parity):
            eng.wait_ge(S["t_in"], 16)

            def page_of(b, i):
                e = b * NPG + i
                return eng.value_load(tbl[0:1, e:e + 1], min_val=0, max_val=a["pool_ck"].shape[0] // P - 1)

            for n in range(parity, len(ik_loads), 2):
                b, c = ik_loads[n]
                if n >= RI:
                    eng.wait_ge(S["ik_used"], n - RI + 1)
                for i in range(QP):
                    page = page_of(b, c * QP + i)
                    eng.dma_start(ik_ring[:, n % RI, i, :], a["pool_ik"][bass.ds(page * 64, 64), :]).then_inc(ik_in[n % RI], 16)
            for n in range(parity, len(loads), 2):
                kind, b, c = loads[n]
                if n >= RC:
                    eng.wait_ge(S["used"], n - RC + 1)
                pages, w, pool = (2 * QP, 2 * P, a["pool_d"]) if kind == "d" else (QP, H * P, a["pool_" + kind])
                for i in range(pages):
                    page = page_of(b, c * pages + i)
                    eng.dma_start(ring[:, n % RC, i * w:(i + 1) * w], pool[bass.ds(page * P, P), :]).then_inc(c_in[n % RC], 16)

        @block.sync
        def _(sp):
            sp.dma_start(tbl[:], a["pages"]).then_inc(S["t_in"], 16)
            sp.dma_start(gd[:], a["g_diff"].partition_broadcast(TS)).then_inc(S["c_in"], 16)
            fetch(sp, 0)

        @block.gpsimd
        def _(pool):
            nc.gpsimd.memset(a_t[:], 0.0).then_inc(S["zeroed"], 1)
            fetch(pool, 1)

        @block.tensor
        def _(pe):
            for g in range(2):
                mm = pe.matmul(ps_o[:, g * H:(g + 1) * H], const["sel_tok"][:, g, :], new["w"][:], start=True, stop=True)
            mm.then_inc(S["w_ps"], 1)

            def ik_scores(g, j, c):
                n = (4 * g + j) * NQ + c
                pe.wait_ge(ik_in[n % RI], 16 * QP * (n // RI + 1))
                out = ps_s[32 * j:32 * j + 32, c * 512:(c + 1) * 512]
                pe.matmul(out, qix[:, 4 * g + j, :], ik_ring[:, n % RI].rearrange("p i k -> p (i k)"),
                          start=True, stop=True).then_inc(S["ik_used"], 1)

            def k_scores(kind, g, j, c):
                b = 4 * g + j
                out = ps_s[32 * j:32 * j + 32, c * 512:(c + 1) * 512].rearrange("r (i k) -> r i k", k=P)
                if kind == "c":
                    n = at[("ck", b, c)]
                    pe.wait_ge(c_in[n % RC], arrived(n))
                    pages = ring[:, n % RC].rearrange("p (i h k) -> p i h k", i=QP, h=H)
                    for h in range(H):
                        mm = pe.matmul(out, qx[:, b, h, :], pages[:, :, h, :], start=(h == 0), stop=(h == H - 1))
                    mm.then_inc(S["used"], 1)
                else:
                    n = at[("d", b, c // 2)]
                    pe.wait_ge(c_in[n % RC], arrived(n))
                    pages = ring[:, n % RC].rearrange("p (i two k) -> p i two k", i=2 * QP, two=2)
                    pe.matmul(out, qdx[:, b, :], pages[:, (c % 2) * QP:(c % 2 + 1) * QP, 0, :], start=False, stop=True,
                              skip_group_check=True)

            tail = slice(PAST, NKC)
            for g in range(2):
                if g:
                    pe.wait_ge(S["relu_done"], g)
                for j in range(4):
                    for c in range(NQ):
                        ik_scores(g, j, c)
                    mm = pe.matmul(ps_s[32 * j:32 * j + 32, tail], qix[:, 4 * g + j, :], new["ki"][:], start=True, stop=True)
                mm.then_inc(S["s_done"], 1)
                pe.wait_ge(S["relu_done"], g + 1)
                pe.wait_ge(S["wsel_ready"], 1)
                if g == 0:
                    continue
                for k0 in range(0, NKC, 512):
                    kw = min(512, NKC - k0)
                    for gg, r in ((0, p_sb), (1, rl)):
                        mm = pe.matmul(ps_s[0:TS, k0:k0 + kw], wsel[:, gg, :], r[:, k0:k0 + kw], start=(gg == 0), stop=(gg == 1))
                mm.then_inc(S["sc_ps"], 1)

            for si, (kind, g) in enumerate(stages):
                if si == 0:
                    pe.wait_ge(S["sc_out"], 1)
                else:
                    pe.wait_ge(S["exp_done"], si)
                if kind == "d":
                    pe.wait_ge(S["picked"], 1)
                    for k0 in range(0, NKC, 512):
                        kw = min(512, NKC - k0)
                        pe.matmul(ps_s[:, k0:k0 + kw], const["sel_back"][:, g, :], sc[:, k0:k0 + kw],
                                  start=True, stop=False, skip_group_check=True)
                for j in range(4):
                    b = 4 * g + j
                    for c in range(NQ):
                        k_scores(kind, g, j, c)
                    out = ps_s[32 * j:32 * j + 32, tail]
                    if kind == "c":
                        for h in range(H):
                            pe.matmul(out, qx[:, b, h, :], new["kc"][:, h, :], start=(h == 0), stop=False)
                        mm = pe.matmul(out, ident[0:32, 0:32], const["negs"][:, b, :], start=False, stop=True)
                    else:
                        mm = pe.matmul(out, qdx[:, b, :], new["kd"][:], start=False, stop=True, skip_group_check=True)
                mm.then_inc(S["s_done"], 1)
                pe.wait_ge(S["scaled"], si + 1)
                for b0 in range(0, NB, 4):
                    t = 5 * si + b0 // 4
                    if t >= 2:
                        pe.wait_ge(S["placed"], t - 1)
                    for kb in range(b0, min(NB, b0 + 4)):
                        kw = min(P, NKC - kb * P)
                        x = pe.transpose(ps_t[0:kw, t % 2, kb - b0, :], p_sb[:, kb * P:kb * P + kw], ident[:])
                    x.then_inc(S["turned"], 1)
                pe.wait_ge(S["placed"], 5 * (si + 1))
                if si:
                    pe.wait_ge(S["o_read"], si)
                else:
                    pe.wait_ge(S["wsel_ready"], 1)
                e = H * P if kind == "c" else P
                for j in range(4):
                    b = 4 * g + j
                    per = QP if kind == "c" else 2 * QP
                    for kb in range(NPG):
                        n = at[("cv" if kind == "c" else "d", b, kb // per)]
                        if kind == "c":
                            if kb % per == 0:
                                pe.wait_ge(c_in[n % RC], arrived(n))
                            v = ring[:, n % RC, (kb % per) * H * P:(kb % per + 1) * H * P]
                        else:
                            v = ring[:, n % RC, (kb % per) * 2 * P + P:(kb % per + 1) * 2 * P]
                        mm = pe.matmul(ps_o[32 * j:32 * j + 32, 0:e], a_t[:, kb, j, :], v, start=(kb == 0), stop=False)
                        if kb % per == per - 1:
                            mm.then_inc(S["used"], 1)
                    mm = pe.matmul(ps_o[32 * j:32 * j + 32, 0:e], a_t[0:KL, NPG, j, :], new["vc" if kind == "c" else "vd"][:],
                                   start=False, stop=True)
                mm.then_inc(S["o_done"], 1)

            pe.wait_ge(S["o_read"], 4)
            for i, o in enumerate((os_c, os_d)):
                for h in range(H):
                    for g in range(2):
                        src = o[:, g, h * P:(h + 1) * P] if i == 0 else o[:, g, :]
                        mm = pe.matmul(ps_s[0:TS, i * 512 + h * P:i * 512 + (h + 1) * P], const["sel"][:, g, h, :], src,
                                       start=(g == 0), stop=(g == 1))
            mm.then_inc(S["sel_done"], 1)
            pe.wait_ge(S["normed"], 1)
            for i in range(8):
                x = pe.transpose(ps_t[:, i // 4, i % 4, 0:TS], o_s[:, i // 4, (i % 4) * P:(i % 4 + 1) * P], ident[0:TS, 0:TS])
            x.then_inc(S["o_turned"], 1)

        @block.scalar
        def _(act):
            for g, dst in ((0, p_sb), (1, rl)):
                act.wait_ge(S["s_done"], g + 1)
                nc.scalar.activation(dst[:], ps_s[:, 0:NKC], ACT.Relu, scale=64 ** -0.5).then_inc(S["relu_done"], 1)
            act.wait_ge(S["sc_ps"], 1)
            for si, (kind, g) in enumerate(stages):
                act.wait_ge(S["max_done"], si + 1)
                if si:
                    act.wait_ge(S["turned"], 5 * si)
                scale = DC ** -0.5 if kind == "c" else float(P) ** -0.5
                nc.scalar.activation(p_sb[:], ps_s[:, 0:NKC], ACT.Exp, bias=st[:, 1:2], scale=scale,
                                     accum_out=st[:, 2:3]).then_inc(S["exp_done"], 1)
                act.wait_ge(S["o_done"], si + 1)
                if kind == "c":
                    nc.scalar.activation(os_c[:, g, :], ps_o[:], ACT.Copy).then_inc(S["o_read"], 1)
                else:
                    nc.scalar.activation(os_d[:, g, :], ps_o[:, 0:P], ACT.Copy).then_inc(S["o_read"], 1)
            act.wait_ge(S["sel_done"], 1)
            nc.scalar.activation(o_s, ps_s[0:TS, 0:1024].rearrange("p (k e) -> p k e", k=2), ACT.Copy).then_inc(S["sel_read"], 1)
            act.wait_ge(S["sel_read"], 1)
            nc.scalar.activation(osq[:], o_s[:, 0, :], ACT.Square).then_inc(S["osq_done"], 1)
            act.wait_ge(S["ovar"], 1)
            nc.scalar.activation(ost[:, 2, :], ost[:, 1, :], ACT.Sqrt).then_inc(S["ostd"], 1)
            act.wait_ge(S["o_turned"], 1)
            nc.scalar.activation(o_t[:, :, TP:T], ps_t[:, :, :, 0:TS].rearrange("p a b t -> p (a b) t"), ACT.Copy).then_inc(S["o_placed"], 1)
            act.wait_ge(S["o_placed"], 1)

        @block.vector
        def _(dve):
            cnt = [0]

            def link(ins):
                cnt[0] += 1
                ins.then_inc(S["chain"], 1)
                dve.wait_ge(S["chain"], cnt[0])

            link(nc.vector.tensor_scalar(half_c[:, 1:2], const["second_half"][:], neg_lam[:], None, ALU.mult))
            nc.vector.tensor_tensor(half_c[:, 0:1], half_c[:, 1:2], const["first_half"][:], ALU.add).then_inc(S["q_ready"], 1)
            dve.wait_ge(S["q_ready"], 1)
            dve.wait_ge(S["w_ps"], 1)
            link(nc.vector.tensor_tensor(wrow[:], ps_o[:, 0:2 * H].rearrange("p (g h) -> p g h", g=2),
                                         const["hot"][:].unsqueeze(1).to_broadcast([P, 2, H]), ALU.mult))
            link(nc.vector.tensor_reduce(wr1[:], wrow[:], AX.X, ALU.add))
            nc.vector.tensor_tensor(wsel[:], const["sel_sum"][:], wr1[:].unsqueeze(2).to_broadcast([P, 2, TS]), ALU.mult).then_inc(S["wsel_ready"], 1)
            dve.wait_ge(S["sc_ps"], 1)
            link(nc.vector.tensor_copy(sc[:, 0:PAST], ps_s[0:TS, 0:PAST]))
            nc.vector.tensor_tensor(sc[:, PAST:NKC], ps_s[0:TS, PAST:NKC], const["neg_rows"][:], ALU.add).then_inc(S["sc_out"], 1)
            dve.wait_ge(S["sc_out"], 1)
            dve.wait_ge(S["zeroed"], 1)

            def rounds(n):
                for _ in range(n):
                    link(nc.vector.max(top[:], sc[:]))
                    link(nc.vector.match_replace(sc[:], top[:], sc[:], PICKED))

            for si, (kind, g) in enumerate(stages):
                if kind == "c":
                    rounds(TOPK // 16)
                    if g == 1:
                        link(nc.vector.tensor_scalar(sc[:], sc[:], PICKED, NEG, ALU.not_equal, ALU.mult))
                        nc.vector.tensor_tensor(sc[:, PAST:NKC], sc[:, PAST:NKC], const["neg_rows"][:], ALU.add).then_inc(S["picked"], 1)
                scale = DC ** -0.5 if kind == "c" else float(P) ** -0.5
                dve.wait_ge(S["s_done"], 2 + si + 1)
                link(nc.vector.tensor_reduce(st[:, 0:1], ps_s[:, 0:NKC], AX.X, ALU.max))
                nc.vector.tensor_scalar(st[:, 1:2], st[:, 0:1], -scale, None, ALU.mult).then_inc(S["max_done"], 1)
                dve.wait_ge(S["exp_done"], si + 1)
                link(nc.vector.reciprocal(st[:, 3:4], st[:, 2:3]))
                if kind == "c":
                    link(nc.vector.tensor_tensor(st[:, 3:4], st[:, 3:4], half_c[:, 0:1], ALU.mult))
                nc.vector.tensor_scalar(p_sb[:], p_sb[:], st[:, 3:4], None, ALU.mult).then_inc(S["scaled"], 1)
                if si:
                    dve.wait_ge(S["o_done"], si)
                for b0 in range(0, NB, 4):
                    t = 5 * si + b0 // 4
                    n = min(4, NB - b0)
                    kw = min(P, NKC - b0 * P)
                    dve.wait_ge(S["turned"], t + 1)
                    src = ps_t[0:kw, t % 2, 0:n, :]
                    if kind == "c":
                        x = [nc.vector.tensor_reduce(a_t[0:kw, b0 + i, :, 0:16].rearrange("k j (h q) -> k j h q", q=DT),
                                                     ps_t[0:kw, t % 2, i, :].rearrange("k (j h c q) -> k j h q c", j=4, h=H, c=2),
                                                     AX.X, ALU.add) for i in range(n)][-1]
                    else:
                        x = nc.vector.tensor_copy(a_t[0:kw, b0:b0 + n].rearrange("k b j r -> k b (j r)"), src)
                    x.then_inc(S["placed"], 1)
                dve.wait_ge(S["placed"], 5 * (si + 1))
            dve.wait_ge(S["c_in"], 16)
            link(nc.vector.tensor_scalar(gd[:], gd[:], 1.0 - LAM_INIT, None, ALU.mult))
            dve.wait_ge(S["osq_done"], 1)
            link(nc.vector.tensor_reduce(ost[:, 0, :], osq[:], AX.X, ALU.add))
            nc.vector.tensor_scalar(ost[:, 1, :], ost[:, 0, :], 1.0 / P, EPS, ALU.mult, ALU.add).then_inc(S["ovar"], 1)
            dve.wait_ge(S["ostd"], 1)
            link(nc.vector.reciprocal(ost[:, 3, :], ost[:, 2, :]))
            o = o_s[:, 0, :].rearrange("t (h e) -> t h e", e=P)
            link(nc.vector.tensor_tensor(o, o, ost[:, 3, :].unsqueeze(2).to_broadcast([TS, H, P]), ALU.mult))
            nc.vector.tensor_tensor(o, o, gd[:].unsqueeze(1).to_broadcast([TS, H, P]), ALU.mult).then_inc(S["normed"], 1)


def attention_mixer(nc, sb, load_consts, const, a, h_t):
    with ExitStack() as st:
        new_shapes = {"qx": [P, DB, H, 32], "qdx": [P, DB, 32], "qix": [64, DB, 32], "kc": [P, H, KL], "kd": [P, KL],
                      "ki": [64, KL], "vc": [KL, H * P], "vd": [KL, P], "w": [KL, H]}
        new = {n: sb(st, f"new_{n}", shape) for n, shape in new_shapes.items()}
        neg_lam = sb(st, "neg_lam", [P, 1])
        with ExitStack() as qs:
            def t(name, shape):
                return sb(qs, name, shape)

            kc_t, qd_t, qc_t = t("kc_t", [P, H, T]), t("qd_t", [P, H, T]), t("qc_t", [P, H, T])
            kd_t, ki_t, qi_t = t("kd_t", [P, T]), t("ki_t", [P, T]), t("qi_t", [P, 2, T])
            v_c, v_d, w_i = t("v_c", [P, NT, 512]), t("v_d", [P, NT, P]), t("w_i", [P, NT, H])
            with ExitStack() as rt:
                rc = dict(const, **load_consts(rt, "rope", ["rope"]))
                att_project(nc, rc, h_t, a["w_att"], a["w_att_i"], qc_t, kc_t, v_c, qd_t, kd_t, v_d, qi_t, ki_t, w_i,
                            (a["kc"], a["vc"], a["kd"], a["vd"], a["ki"]))
            o_t = h_t
            with ExitStack() as rt:
                rc = dict(const, **load_consts(rt, "prompt", ["neg_future"]))
                prompt_attention(nc, rc, qc_t, kc_t, v_c, qd_t, kd_t, v_d, qi_t, ki_t, w_i, o_t, neg_lam, a["diff_lambda"],
                                 a["g_diff"])
            sample_queries(nc, new, qc_t, kc_t, v_c, qd_t, kd_t, v_d, qi_t, ki_t, w_i)
        with ExitStack() as rt:
            rc = dict(const, **load_consts(rt, "sample", ["sel", "sel_sum", "sel_tok", "sel_back", "hot", "negs", "neg_rows",
                                                          "first_half", "second_half"]))
            sample_attention(nc, rc, a, new, o_t, neg_lam)


def build(nc, a):
    x_mid = nc.dram_tensor("x_mid", (T, D), F32, kind="Internal").ap()
    with ExitStack() as ctx:
        def sb(stack, name, shape, dtype=F32, side=None):
            return stack.enter_context(nc.sbuf_tensor(name, shape, dtype, side=side))

        def load_consts(stack, tag, names):
            tiles = {n: sb(stack, f"c_{n}", list(a[n].shape)) for n in names}
            done = stack.enter_context(nc.semaphore(f"{tag}_consts"))
            with nc.Block() as block:
                @block.sync
                def _(sp):
                    for n in names:
                        sp.dma_start(tiles[n][:], a[n]).then_inc(done, 16)
                    sp.wait_ge(done, 16 * len(names))
            clear_semaphores(nc, [done])
            return tiles

        const = load_consts(ctx, "all", ["ident"])
        gain = a["gains_row"]
        gain_c = a["gains_col"]
        h_mem, mid_mem = ExitStack(), ExitStack()

        h_t = sb(h_mem, "h_t0", [P, KD, T])
        norm_rows(nc, "n0", const, a["x"], gain_c[0, 0], h_t)
        mix_t = sb(mid_mem, "mix_t", [P, KD, T], side="right")
        with ExitStack() as rt:
            names = ["level_masks", "neg_upper", "neg_tail", "row_mask", "col_mask", "reset", "sel4"]
            rc = dict(const, **load_consts(rt, "rec", names))
            rows = sb(rt, "rows", [H, 2, T])
            cols = sb(rt, "cols", [P, NT, 3, H])
            lb, one_lb = sb(rt, "lb", [P, H]), sb(rt, "one_lb", [P, H])
            gate_rows(nc, rc, h_t, a["w_gates"], a["b_gates"], a["m0"], a["lb_logits"], rows, cols, lb, one_lb,
                      a["m_new"])
            recurrent_mixers(nc, rc, h_t, mix_t, a["w_rec"], a["state_a"], a["state_b"], rows, cols, lb, one_lb,
                             a["g_rec"], a["new_a"], a["new_b"])
        h_mem.close()
        h2 = sb(h_mem, "h2_0", [P, 2, KD, T], F32R)
        project_add_norm(nc, "r0", const, a["x"], lambda k, t0, n: mix_t[:, k, t0:t0 + n], KD, a["w_out_rec"],
                         gain[0, 1], x_mid, gain_c[0, 2], h2, parts=True)
        mid_mem.close()
        a_t = sb(mid_mem, "a_t0", [P, NF * T], side="right")
        ffn_up(nc, "f0", h2, a_t, a["w_up"][0], a["conv"][0], a["conv_state"][0], a["conv_new"][0])
        h_mem.close()
        h_t = sb(h_mem, "h_t1", [P, KD, T])
        project_add_norm(nc, "d0", const, x_mid, lambda k, t0, n: a_t[:, k * T + t0:k * T + t0 + n], NF, a["w_down"][0],
                         gain[0, 3], x_mid, gain_c[1, 0], h_t, depth=2)
        mid_mem.close()

        attention_mixer(nc, sb, load_consts, const, a, h_t)
        h2 = sb(mid_mem, "h2_1", [P, 2, KD, T], F32R, side="right")
        project_add_norm(nc, "r1", const, x_mid, lambda k, t0, n: h_t[:, k, t0:t0 + n], KD, a["w_out_att"],
                         gain[1, 1], x_mid, gain_c[1, 2], h2, parts=True)
        h_mem.close()
        a_t = sb(h_mem, "a_t1", [P, NF * T])
        ffn_up(nc, "f1", h2, a_t, a["w_up"][1], a["conv"][1], a["conv_state"][1], a["conv_new"][1])
        mid_mem.close()
        project_add_norm(nc, "d1", const, x_mid, lambda k, t0, n: a_t[:, k * T + t0:k * T + t0 + n], NF, a["w_down"][1],
                         gain[1, 3], a["y"], None, None)
        h_mem.close()




def shape_tables():
    i = np.arange(P)
    s, t = i[:, None], i[None, :]
    masks = np.zeros((P, LEVELS + 1, P), np.float32)
    for lv in range(LEVELS):
        b = 64 >> lv
        masks[:, lv, :] = (s // (2 * b) == t // (2 * b)) & (s % (2 * b) < b) & (t % (2 * b) >= b)
    masks[:, LEVELS, :] = s == t
    tail = np.concatenate([np.zeros(PTAIL, int), 1 + np.arange(TS) // DT])
    r = np.arange(LAST)
    ok = (tail[:, None] == tail[None, :]) & (r[:, None] <= r[None, :])
    starts = np.ones(T, np.float32)
    starts[0:TP:P] = 0
    starts[TP::DT] = 0
    n = np.arange(DB + 1)
    sel4 = np.zeros((H, H, P), np.float32)
    sel4[np.arange(H), np.arange(H)] = 1
    pos = np.concatenate([np.arange(TP), np.tile(PAST + np.arange(DT), DB)]).astype(np.float32)
    rope = np.zeros((NT * P, 2, 24), np.float32)
    for off, d in ((0, 64), (8, 128)):
        rr = d // 4
        inv = np.float32(500000.0) ** (-np.arange(rr // 2, dtype=np.float32) * np.float32(2.0) / np.float32(rr))
        ang = (pos[:, None] * inv.astype(np.float32)[None, :]).astype(np.float32).astype(np.float64)
        rope[:T, 0, off:off + rr // 2] = np.cos(ang)
        rope[:T, 1, off:off + rr // 2] = np.sin(ang)
    row = np.arange(P)
    j, hq = row // 32, row % 32
    used = hq < 16
    sel = np.zeros((P, 2, H, TS), np.float32)
    for g in range(2):
        for rr in row[used]:
            sel[rr, g, hq[rr] // 4, (4 * g + j[rr]) * DT + hq[rr] % 4] = 1
    sel_sum = sel.sum(2)
    tok = np.zeros((LAST, 2, P), np.float32)
    tok[PTAIL:] = sel_sum.transpose(2, 1, 0)
    hot = np.zeros((P, H), np.float32)
    hot[row[used], hq[used] // 4] = 1
    q = np.arange(32) % DT
    negs = np.full((32, DB, LAST), NEG, np.float32)
    for b in range(DB):
        for c in range(DT):
            negs[q >= c, b, PTAIL + DT * b + c] = 0
    return {
        "ident": np.eye(P, dtype=np.float32),
        "level_masks": masks,
        "neg_upper": np.where(s <= t, 0, NEG).astype(np.float32),
        "neg_tail": np.where(ok, 0, NEG).astype(np.float32),
        "row_mask": (tail[:, None] == n[None, :]).astype(np.float32),
        "col_mask": np.broadcast_to((n[:, None] == tail[None, :]).astype(np.float32), (P, DB + 1, LAST)),
        "reset": np.broadcast_to(starts, (P, T)),
        "sel4": sel4,
        "rope": rope.reshape(NT, P, 2, 24).transpose(1, 0, 2, 3),
        "neg_future": np.where(t <= s, 0, NEG).astype(np.float32),
        "sel": sel,
        "sel_sum": sel_sum,
        "sel_tok": tok,
        "sel_back": sel_sum.transpose(2, 1, 0),
        "hot": hot,
        "negs": negs,
        "first_half": (hq % 8 < 4).astype(np.float32)[:, None],
        "second_half": (hq % 8 >= 4).astype(np.float32)[:, None],
        "neg_rows": negs[np.tile(np.arange(DT), DB), np.repeat(np.arange(DB), DT)],
    }


def kernel(**inputs):
    import concourse.bacc as _bacc
    from concourse.bass_utils import run_bass_kernel_spmd as _run

    x = {n: np.asarray(v) for n, v in inputs.items()}

    def blocks(w, n):
        return w.reshape(w.shape[0] // P, P, n, -1).transpose(2, 1, 0, 3)

    arrays = dict(shape_tables())
    arrays["x"] = np.concatenate([x["meta_tokens"], x["x_prompt"][0], x["x_sample"].reshape(TS, D)])
    arrays["gains_row"] = x["norm_gains"]
    arrays["gains_col"] = x["norm_gains"].reshape(2, 4, KD, P).transpose(0, 1, 3, 2)
    wr = x["w_in_rec"][0]
    heads = wr[:, :8 * 512].reshape(D, 8, H, P)
    arrays["w_rec"] = np.concatenate([heads[:, 0:4].transpose(2, 0, 1, 3), heads[:, 4:8].transpose(2, 0, 1, 3)]) \
        .reshape(NU, KD, P, 512).transpose(0, 2, 1, 3)
    arrays["w_gates"] = wr[:, 8 * 512:].reshape(KD, P, 2 * H).transpose(1, 0, 2)
    arrays["b_gates"] = x["b_gates_rec"][0].reshape(2 * H)
    arrays["m0"] = x["state_mlstm_m"][0].T
    arrays["lb_logits"] = x["lb_logits"].reshape(2, H, P).transpose(2, 0, 1)
    arrays["state_a"] = x["state_hgrn"][0].transpose(1, 2, 0, 3)
    arrays["state_b"] = np.concatenate([x["state_mlstm_C"][0], x["state_mlstm_n"][0][..., None]], -1).transpose(1, 2, 0, 3)
    arrays["g_rec"] = np.concatenate([x["g_norm_hgrn"], x["g_norm_mlstm"]])
    arrays["w_out_rec"] = x["w_out_rec"][0].reshape(KD, P, D).transpose(1, 0, 2)
    arrays["w_up"] = x["w_ffn_up"].reshape(2, KD, P, 2, NF, P).transpose(0, 4, 3, 2, 1, 5).reshape(2, NF * 2 * P, KD * P)
    arrays["w_down"] = x["w_ffn_down"].reshape(2, NF, P, D).transpose(0, 2, 1, 3)
    arrays["conv"] = np.concatenate([x["ffn_conv_w"], x["ffn_conv_b"][:, None]], 1).reshape(2, 4, NF, P) \
        .transpose(0, 3, 2, 1).reshape(2, P, NF * 4)
    arrays["conv_state"] = x["state_ffn_conv"].reshape(2, DB, 2, NF, P).transpose(0, 4, 3, 1, 2).reshape(2, P, NF * DB * 2)
    wa = x["w_in_att"][0]
    arrays["w_att"] = wa[:, :2560].reshape(KD, P, 5, 512).transpose(2, 1, 0, 3)
    arrays["w_att_i"] = wa[:, 2560:].reshape(KD, P, 68).transpose(1, 0, 2)
    arrays["w_out_att"] = x["w_out_att"][0].reshape(KD, P, D).transpose(1, 0, 2)
    arrays["diff_lambda"] = x["diff_lambda"][0].reshape(4 * DC)
    arrays["g_diff"] = x["g_norm_diff"][0]
    arrays["pages"] = x["page_table"].reshape(1, DB * NPG)
    npool = x["cache_diff_k"].shape[1]
    arrays["pool_ck"] = x["cache_diff_k"][0].transpose(0, 3, 2, 1).reshape(npool * P, H * P)
    arrays["pool_cv"] = x["cache_diff_v"][0].reshape(npool * P, H * P)
    arrays["pool_d"] = np.concatenate([x["cache_dsa_k"][0].transpose(0, 2, 1), x["cache_dsa_v"][0]], -1).reshape(npool * P, 2 * P)
    arrays["pool_ik"] = x["cache_idx_k"][0].transpose(0, 2, 1).reshape(npool * 64, P)
    arrays = {n: np.ascontiguousarray(v) for n, v in arrays.items()}

    nc = _bacc.Bacc("TRN2", target_bir_lowering=False, num_devices=1)
    aps = {n: nc.dram_tensor(f"in_{n}", v.shape, mybir.dt.from_np(v.dtype), kind="ExternalInput").ap()
           for n, v in arrays.items()}
    outs = {"y": (T, D), "new_a": (H, P, DB + 1, P), "new_b": (H, P, DB + 1, P + 1), "m_new": (H, DB + 1),
            "conv_new": (2, P, NF * (DB + 1) * 2), "kc": (T, 512), "vc": (T, 512), "kd": (T, P), "vd": (T, P), "ki": (T, 64)}
    for n, s in outs.items():
        aps[n] = nc.dram_tensor(f"out_{n}", s, F32, kind="ExternalOutput").ap()
    build(nc, aps)
    r = _run(nc, [{f"in_{n}": v for n, v in arrays.items()}], core_ids=[0]).results[0]
    o = {n: r[f"out_{n}"] for n in outs}
    y = o["y"]
    sa = o["new_a"].transpose(2, 0, 1, 3)
    sbn = o["new_b"].transpose(2, 0, 1, 3)
    cv = o["conv_new"].reshape(2, P, NF, DB + 1, 2).transpose(0, 3, 4, 2, 1).reshape(2, DB + 1, 2, DFF)
    m = o["m_new"].T

    def both(v, tail):
        return v[:TP].reshape((1, 1, TP) + tail), v[TP:].reshape((1, DB, DT) + tail)

    c_k, c_v = both(o["kc"], (H, P)), both(o["vc"], (H, P))
    d_k, d_v, i_k = both(o["kd"], (P,)), both(o["vd"], (P,)), both(o["ki"], (64,))
    return (y[N_META:TP].reshape(1, SEQ, D), y[TP:].reshape(DB, DT, D),
            sa[None, 0:1], sa[None, 1:], sbn[None, 0:1, ..., :P], sbn[None, 1:, ..., :P],
            sbn[None, 0:1, ..., P], sbn[None, 1:, ..., P], m[None, 0:1], m[None, 1:],
            cv[:, 0:1], cv[:, 1:], *c_k, *c_v, *d_k, *d_v, *i_k)
```
